# Optimizing a Trainium2 kernel written in Bass

```python
import math
import jax, jax.numpy as jnp
from jax import lax
import numpy as np

D_MODEL = 1024
BATCH = 1
SEQ = 256
DEPTH = 2

CTX_LEN = 256
GRID_W = 64
HEAD_DIM = 64
ATTN_WIDTH = D_MODEL // 2
SGU_WIDTH = D_MODEL // 4
FOURIER_WIDTH = D_MODEL // 4
MIX_WIDTH = ATTN_WIDTH + SGU_WIDTH + FOURIER_WIDTH
N_Q_HEADS = ATTN_WIDTH // HEAD_DIM
N_KV_HEADS = N_Q_HEADS // 4
KV_WIDTH = N_KV_HEADS * HEAD_DIM
SGU_HEAD_DIM = 64
N_SGU_HEADS = SGU_WIDTH // SGU_HEAD_DIM
FOURIER_GROUP_DIM = 64
N_FOURIER_GROUPS = FOURIER_WIDTH // FOURIER_GROUP_DIM
IN_WIDTH = ATTN_WIDTH + 2 * KV_WIDTH + 2 * SGU_WIDTH + FOURIER_WIDTH
Q_END = ATTN_WIDTH
K_END = Q_END + KV_WIDTH
V_END = K_END + KV_WIDTH
U_END = V_END + SGU_WIDTH
G_END = U_END + SGU_WIDTH
WINDOW = 128
BLOCK = 128
CHUNK = 128
D_FF = 4 * D_MODEL
ROPE_THETA = 10000.0
EPS = 1e-6
NEG_INF = -1e30


def rmsnorm(x, g):
    xf = x.astype(jnp.float32)
    y = xf * lax.rsqrt(jnp.mean(xf * xf, axis=-1, keepdims=True) + EPS)
    return (y * g.astype(jnp.float32)).astype(x.dtype)

def axial_rope_tables(rows):
    row = jnp.repeat(jnp.arange(rows), GRID_W).astype(jnp.float32)
    col = jnp.tile(jnp.arange(GRID_W), rows).astype(jnp.float32)
    n_freq = HEAD_DIM // 4
    inv_freq = ROPE_THETA ** (-jnp.arange(n_freq, dtype=jnp.float32) / n_freq)
    ang_r = row[:, None] * inv_freq[None, :]
    ang_c = col[:, None] * inv_freq[None, :]
    ang = jnp.concatenate([ang_r, ang_r, ang_c, ang_c], axis=-1)
    return jnp.cos(ang), jnp.sin(ang)

def apply_rope(x, cos, sin):
    x1, x2, x3, x4 = jnp.split(x, 4, axis=-1)
    rot = jnp.concatenate([-x2, x1, -x4, x3], axis=-1)
    out = x * cos[None, :, None, :] + rot * sin[None, :, None, :]
    return out.astype(x.dtype)

def neighbour_blocks(t):
    z = jnp.zeros_like(t[:, :1])
    prev = jnp.concatenate([z, t[:, :-1]], axis=1)
    nxt = jnp.concatenate([t[:, 1:], z], axis=1)
    return jnp.concatenate([prev, t, nxt], axis=2)

def latent_window_attention(q, k, v, ck, cv, sink):
    B, S, H, hd = q.shape
    G = H // N_KV_HEADS
    nb = S // BLOCK
    scale = hd ** -0.5
    qb = q.reshape(B, nb, BLOCK, N_KV_HEADS, G, hd)
    kw = neighbour_blocks(k.reshape(B, nb, BLOCK, N_KV_HEADS, hd))
    vw = neighbour_blocks(v.reshape(B, nb, BLOCK, N_KV_HEADS, hd))
    s_loc = jnp.einsum('bnqhgd,bnkhd->bnhgqk', qb, kw, preferred_element_type=jnp.float32) * scale
    qpos = jnp.arange(BLOCK)[:, None]
    kpos = jnp.arange(3 * BLOCK)[None, :] - BLOCK
    band = jnp.abs(kpos - qpos) <= WINDOW
    kabs = jnp.arange(nb)[:, None, None] * BLOCK + kpos[None]
    valid = band[None] & (kabs >= 0) & (kabs < S)
    s_loc = jnp.where(valid[None, :, None, None], s_loc, NEG_INF)
    s_ctx = jnp.einsum('bnqhgd,bchd->bnhgqc', qb, ck, preferred_element_type=jnp.float32) * scale
    s_sink = jnp.broadcast_to(sink.astype(jnp.float32).reshape(1, 1, N_KV_HEADS, G, 1, 1),
                              s_loc.shape[:-1] + (1,))
    p = jax.nn.softmax(jnp.concatenate([s_loc, s_ctx, s_sink], axis=-1), axis=-1)
    n_loc = 3 * BLOCK
    n_ctx = ck.shape[1]
    p_loc = p[..., :n_loc].astype(v.dtype)
    p_ctx = p[..., n_loc:n_loc + n_ctx].astype(v.dtype)
    out = (jnp.einsum('bnhgqk,bnkhd->bnqhgd', p_loc, vw)
           + jnp.einsum('bnhgqc,bchd->bnqhgd', p_ctx, cv))
    return out.reshape(B, S, H * hd)

def context_attention(cq, ck, cv, sink):
    B, L, H, hd = cq.shape
    G = H // N_KV_HEADS
    qg = cq.reshape(B, L, N_KV_HEADS, G, hd)
    s = jnp.einsum('bqhgd,bkhd->bhgqk', qg, ck, preferred_element_type=jnp.float32) * (hd ** -0.5)
    s_sink = jnp.broadcast_to(sink.astype(jnp.float32).reshape(1, N_KV_HEADS, G, 1, 1),
                              s.shape[:-1] + (1,))
    p = jax.nn.softmax(jnp.concatenate([s, s_sink], axis=-1), axis=-1)[..., :L]
    out = jnp.einsum('bhgqk,bkhd->bqhgd', p.astype(cv.dtype), cv)
    return out.reshape(B, L, H * hd)

def spatial_gating(u, v, w_s, b_s, g_s):
    B, S, _ = u.shape
    vh = rmsnorm(v.reshape(B, S, N_SGU_HEADS, SGU_HEAD_DIM), g_s)
    vc = vh.reshape(B, S // CHUNK, CHUNK, N_SGU_HEADS, SGU_HEAD_DIM)
    mixed = jnp.einsum('hpq,bnqhd->bnphd', w_s, vc) + b_s.T[None, None, :, :, None]
    return u * mixed.reshape(B, S, SGU_WIDTH)

def fourier_mix(f):
    B, S, _ = f.shape
    fg = f.reshape(B, S, N_FOURIER_GROUPS, FOURIER_GROUP_DIM).astype(jnp.float32)
    y = jnp.real(jnp.fft.fft2(fg, axes=(1, 3), norm='ortho'))
    return y.reshape(B, S, FOURIER_WIDTH).astype(f.dtype)

def merge_heads(attn, sgu, four, g_mix, w_out):
    a = rmsnorm(attn, g_mix[:ATTN_WIDTH])
    s = rmsnorm(sgu, g_mix[ATTN_WIDTH:ATTN_WIDTH + SGU_WIDTH])
    f = rmsnorm(four, g_mix[ATTN_WIDTH + SGU_WIDTH:])
    return jnp.concatenate([a, s, f], axis=-1) @ w_out

def squared_relu_mlp(h, w1, w2):
    return jnp.square(jax.nn.relu(h @ w1)) @ w2

def first_inputs(seed: int = 0) -> dict:
    key = jax.random.key(seed)
    ks = jax.random.split(key, 24)
    f32 = jnp.float32
    nrm = lambda k, shape, s: jax.random.normal(k, shape, f32) * s
    gain = lambda k, shape: 1.0 + 0.05 * jax.random.normal(k, shape, f32)
    return {
        "x": nrm(ks[0], (BATCH, SEQ, D_MODEL), 1.0),
        "c": nrm(ks[1], (BATCH, D_MODEL), 1.0),
        "ctx": nrm(ks[2], (BATCH, CTX_LEN, D_MODEL), 1.0),
        "c_ctx": nrm(ks[3], (D_MODEL,), 1.0),
        "w_ada": nrm(ks[4], (DEPTH, D_MODEL, 6 * D_MODEL), 0.5 * D_MODEL ** -0.5),
        "b_ada": nrm(ks[5], (DEPTH, 6 * D_MODEL), 0.02),
        "g_pre_mix": gain(ks[6], (DEPTH, D_MODEL)),
        "w_in": nrm(ks[7], (DEPTH, D_MODEL, IN_WIDTH), D_MODEL ** -0.5),
        "sink": nrm(ks[8], (DEPTH, N_Q_HEADS), 0.5),
        "w_sgu": nrm(ks[9], (DEPTH, N_SGU_HEADS, CHUNK, CHUNK), 0.5 * CHUNK ** -0.5),
        "b_sgu": gain(ks[10], (DEPTH, N_SGU_HEADS, CHUNK)),
        "g_sgu": gain(ks[11], (DEPTH, N_SGU_HEADS, SGU_HEAD_DIM)),
        "g_mix": gain(ks[12], (DEPTH, MIX_WIDTH)),
        "w_out": nrm(ks[13], (DEPTH, MIX_WIDTH, D_MODEL), MIX_WIDTH ** -0.5),
        "g_post_mix": gain(ks[14], (DEPTH, D_MODEL)),
        "g_pre_ff": gain(ks[15], (DEPTH, D_MODEL)),
        "w_ff1": nrm(ks[16], (DEPTH, D_MODEL, D_FF), D_MODEL ** -0.5),
        "w_ff2": nrm(ks[17], (DEPTH, D_FF, D_MODEL), D_FF ** -0.5),
        "g_post_ff": gain(ks[18], (DEPTH, D_MODEL)),
    }

def first_block(x, c, ctx, c_ctx, w_ada, b_ada, g_pre_mix, w_in, sink, w_sgu, b_sgu, g_sgu,
              g_mix, w_out, g_post_mix, g_pre_ff, w_ff1, w_ff2, g_post_ff):
    B, S, _ = x.shape
    ROWS = S // GRID_W
    cos, sin = axial_rope_tables(ROWS)
    h_ctx = ctx
    for l in range(DEPTH):
        last = l == DEPTH - 1
        mod_x = (jax.nn.silu(c) @ w_ada[l] + b_ada[l])[:, None, :]
        sh1, sc1, g1, sh2, sc2, g2 = jnp.split(mod_x, 6, axis=-1)
        mod_c = jax.nn.silu(c_ctx) @ w_ada[l] + b_ada[l]
        csh1, csc1, cg1, csh2, csc2, cg2 = jnp.split(mod_c, 6, axis=-1)

        hc = rmsnorm(h_ctx, g_pre_mix[l]) * (1.0 + csc1) + csh1
        if last:
            ckv = hc @ w_in[l][:, Q_END:V_END]
            ck, cv = jnp.split(ckv, 2, axis=-1)
        else:
            pc = hc @ w_in[l]
            cq, ck, cv, cu, cg, cf = jnp.split(pc, [Q_END, K_END, V_END, U_END, G_END], axis=-1)
        ck = ck.reshape(B, CTX_LEN, N_KV_HEADS, HEAD_DIM)
        cv = cv.reshape(B, CTX_LEN, N_KV_HEADS, HEAD_DIM)
        if not last:
            c_attn = context_attention(cq.reshape(B, CTX_LEN, N_Q_HEADS, HEAD_DIM), ck, cv, sink[l])
            c_sgu = spatial_gating(jax.nn.gelu(cu), jax.nn.gelu(cg), w_sgu[l], b_sgu[l], g_sgu[l])
            c_four = fourier_mix(cf)
            yc = merge_heads(c_attn, c_sgu, c_four, g_mix[l], w_out[l])
            h_ctx = h_ctx + cg1 * rmsnorm(yc, g_post_mix[l])
            hc2 = rmsnorm(h_ctx, g_pre_ff[l]) * (1.0 + csc2) + csh2
            h_ctx = h_ctx + cg2 * rmsnorm(squared_relu_mlp(hc2, w_ff1[l], w_ff2[l]), g_post_ff[l])

        hx = rmsnorm(x, g_pre_mix[l]) * (1.0 + sc1) + sh1
        px = hx @ w_in[l]
        q, k, v, u, gv, f = jnp.split(px, [Q_END, K_END, V_END, U_END, G_END], axis=-1)
        q = apply_rope(q.reshape(B, S, N_Q_HEADS, HEAD_DIM), cos, sin)
        k = apply_rope(k.reshape(B, S, N_KV_HEADS, HEAD_DIM), cos, sin)
        v = v.reshape(B, S, N_KV_HEADS, HEAD_DIM)
        attn = latent_window_attention(q, k, v, ck, cv, sink[l])
        sgu = spatial_gating(jax.nn.gelu(u), jax.nn.gelu(gv), w_sgu[l], b_sgu[l], g_sgu[l])
        four = fourier_mix(f)
        y = merge_heads(attn, sgu, four, g_mix[l], w_out[l])
        x = x + g1 * rmsnorm(y, g_post_mix[l])
        hx2 = rmsnorm(x, g_pre_ff[l]) * (1.0 + sc2) + sh2
        x = x + g2 * rmsnorm(squared_relu_mlp(hx2, w_ff1[l], w_ff2[l]), g_post_ff[l])
    return x


DEPTH_2 = 1

PLE_DIM = 256
LRU_WIDTH = D_MODEL
LRU_BLOCKS = 8
LRU_BLOCK = LRU_WIDTH // LRU_BLOCKS
CONV_WIDTH = 4
LRU_C = 8.0
LRU_A_MIN = 0.9
LRU_A_MAX = 0.999
GLA_HEADS = 4
GLA_DK = D_MODEL // 2 // GLA_HEADS
GLA_DV = D_MODEL // GLA_HEADS
GLA_RANK = 16
GLA_TAU = 16.0
GLA_CHUNK = 64
N_EXPERTS = 32
TOP_K = 4
D_FF_2 = D_MODEL
SWIGLU_LIMIT = 7.0
SWIGLU_ALPHA = 1.702
MOE_BLOCK = 128
LN_EPS = 1e-5
RMS_EPS = 1e-5
DEEPNORM_ALPHA = (2.0 * DEPTH_2) ** 0.25
DEEPNORM_BETA = (8.0 * DEPTH_2) ** -0.25

IN_WIDTHS = [LRU_WIDTH, LRU_WIDTH, GLA_HEADS * GLA_DK, GLA_HEADS * GLA_DK,
             GLA_HEADS * GLA_DV, GLA_HEADS * GLA_DV, GLA_RANK, D_MODEL, D_MODEL]
IN_TOTAL = int(sum(IN_WIDTHS))
IN_SPLITS = [int(s) for s in np.cumsum(IN_WIDTHS)[:-1]]


def layer_norm(x, g, b):
    xf = x.astype(jnp.float32)
    mu = jnp.mean(xf, axis=-1, keepdims=True)
    var = jnp.mean(jnp.square(xf - mu), axis=-1, keepdims=True)
    return ((xf - mu) * lax.rsqrt(var + LN_EPS) * g + b).astype(x.dtype)

def causal_depthwise_conv(x, w, b):
    s = x.shape[1]
    xp = jnp.pad(x, ((0, 0), (CONV_WIDTH - 1, 0), (0, 0)))
    out = xp[:, 0:s] * w[0]
    for k in range(1, CONV_WIDTH):
        out = out + xp[:, k:k + s] * w[k]
    return out + b

def rg_lru(x, w_r, b_r, w_i, b_i, lam):
    bsz, s, c = x.shape
    xb = x.reshape(bsz, s, LRU_BLOCKS, LRU_BLOCK)
    r = jax.nn.sigmoid(jnp.einsum('bsgc,gcd->bsgd', xb, w_r).reshape(bsz, s, c) + b_r)
    i = jax.nn.sigmoid(jnp.einsum('bsgc,gcd->bsgd', xb, w_i).reshape(bsz, s, c) + b_i)
    log_a = (-LRU_C * r * jax.nn.softplus(-lam)).astype(jnp.float32)
    a = jnp.exp(log_a)
    mult = jnp.sqrt(-jnp.expm1(2.0 * log_a))
    u = mult * (i * x).astype(jnp.float32)

    def combine(left, right):
        a1, b1 = left
        a2, b2 = right
        return a1 * a2, a2 * b1 + b2

    _, h = lax.associative_scan(combine, (a, u), axis=1)
    return h.astype(x.dtype)

def gla_chunked(q, k, v, log_g):
    bsz, s, h, dk = q.shape
    dv = v.shape[-1]
    n = s // GLA_CHUNK

    def to_chunks(t):
        t = t.astype(jnp.float32).reshape(bsz, n, GLA_CHUNK, h, t.shape[-1])
        return t.transpose(1, 0, 3, 2, 4)

    qc = to_chunks(q * (dk ** -0.5))
    kc, vc, gc = to_chunks(k), to_chunks(v), to_chunks(log_g)
    causal = jnp.tril(jnp.ones((GLA_CHUNK, GLA_CHUNK), dtype=bool))

    def step(state, inp):
        qn, kn, vn, gn = inp
        bcum = jnp.cumsum(gn, axis=2)
        o_inter = jnp.einsum('bhik,bhkv->bhiv', qn * jnp.exp(bcum), state)
        diff = bcum[:, :, :, None, :] - bcum[:, :, None, :, :]
        decay = jnp.exp(jnp.where(causal[:, :, None], diff, -jnp.inf))
        scores = jnp.einsum('bhijk,bhjk->bhij', qn[:, :, :, None, :] * decay, kn)
        o_intra = jnp.einsum('bhij,bhjv->bhiv', scores, vn)
        b_last = bcum[:, :, -1:, :]
        k_dec = kn * jnp.exp(b_last - bcum)
        state = (jnp.exp(b_last[:, :, 0, :])[..., None] * state
                 + jnp.einsum('bhjk,bhjv->bhkv', k_dec, vn))
        return state, o_inter + o_intra

    state0 = jnp.zeros((bsz, h, dk, dv), jnp.float32)
    _, o = lax.scan(step, state0, (qc, kc, vc, gc))
    o = o.transpose(1, 0, 3, 2, 4).reshape(bsz, s, h, dv)
    return o

def moe(x, w_router, b_router, w_up, b_up, w_down, b_down):
    bsz, s, d = x.shape
    t = bsz * s
    xt = x.reshape(t, d)
    logits = (xt @ w_router + b_router).astype(jnp.float32)
    top_val, top_idx = lax.top_k(logits, TOP_K)
    gates = jax.nn.softmax(top_val, axis=-1).astype(x.dtype)

    n_assign = t * TOP_K
    expert_flat = top_idx.reshape(n_assign)
    token_flat = (jnp.arange(n_assign, dtype=jnp.int32) // TOP_K).astype(jnp.int32)
    gate_flat = gates.reshape(n_assign)
    order = jnp.argsort(expert_flat)
    sorted_expert = expert_flat[order]
    counts = jnp.bincount(expert_flat, length=N_EXPERTS)
    start = jnp.cumsum(counts) - counts
    padded_counts = (counts + MOE_BLOCK - 1) // MOE_BLOCK * MOE_BLOCK
    padded_end = jnp.cumsum(padded_counts)
    padded_start = padded_end - padded_counts
    slot = padded_start[sorted_expert] + jnp.arange(n_assign) - start[sorted_expert]

    n_slots = n_assign + N_EXPERTS * MOE_BLOCK
    n_blocks = n_slots // MOE_BLOCK
    slot_token = jnp.full((n_slots,), t, jnp.int32).at[slot].set(token_flat[order])
    slot_gate = jnp.zeros((n_slots,), x.dtype).at[slot].set(gate_flat[order])
    block_expert = jnp.minimum(
        jnp.searchsorted(padded_end, jnp.arange(n_blocks) * MOE_BLOCK, side='right'),
        N_EXPERTS - 1)
    x_pad = jnp.concatenate([xt, jnp.zeros((1, d), xt.dtype)], axis=0)

    def expert_block(args):
        tok, g, e = args
        xb = x_pad[tok]
        hdn = xb @ w_up[e] + b_up[e]
        gate_h = jnp.minimum(hdn[:, :D_FF_2], SWIGLU_LIMIT)
        up_h = jnp.clip(hdn[:, D_FF_2:], -SWIGLU_LIMIT, SWIGLU_LIMIT)
        act = (up_h + 1.0) * gate_h * jax.nn.sigmoid(SWIGLU_ALPHA * gate_h)
        y = act @ w_down[e] + b_down[e]
        return y * g[:, None]

    y_slots = lax.map(expert_block, (slot_token.reshape(n_blocks, MOE_BLOCK),
                                     slot_gate.reshape(n_blocks, MOE_BLOCK),
                                     block_expert))
    out = jnp.zeros((t + 1, d), y_slots.dtype).at[slot_token].add(y_slots.reshape(n_slots, d))
    return out[:t].reshape(bsz, s, d)

def second_inputs(seed: int = 0) -> dict:
    key = jax.random.key(seed)
    ks = jax.random.split(key, 27)
    f32 = jnp.float32
    L = DEPTH_2

    def nrm(k, shape, scale):
        return jax.random.normal(k, shape, f32) * scale

    u = jax.random.uniform(ks[9], (L, LRU_WIDTH), f32, LRU_A_MIN, LRU_A_MAX)
    s_base = u ** (1.0 / LRU_C)
    lru_lambda = jnp.log(s_base) - jnp.log1p(-s_base)
    return {
        "x": nrm(ks[0], (BATCH, SEQ, D_MODEL), 1.0),
        "p": nrm(ks[1], (DEPTH_2, BATCH, SEQ, PLE_DIM), 1.0),
        "w_in": nrm(ks[2], (L, D_MODEL, IN_TOTAL), D_MODEL ** -0.5),
        "conv_w": nrm(ks[3], (L, CONV_WIDTH, LRU_WIDTH), CONV_WIDTH ** -0.5),
        "conv_b": nrm(ks[4], (L, LRU_WIDTH), 0.01),
        "lru_w_r": nrm(ks[5], (L, LRU_BLOCKS, LRU_BLOCK, LRU_BLOCK), LRU_BLOCK ** -0.5),
        "lru_b_r": nrm(ks[6], (L, LRU_WIDTH), 0.01),
        "lru_w_i": nrm(ks[7], (L, LRU_BLOCKS, LRU_BLOCK, LRU_BLOCK), LRU_BLOCK ** -0.5),
        "lru_b_i": nrm(ks[8], (L, LRU_WIDTH), 0.01),
        "lru_lambda": lru_lambda,
        "gla_w_gate": nrm(ks[10], (L, GLA_RANK, GLA_HEADS * GLA_DK), GLA_RANK ** -0.5),
        "gla_b_gate": nrm(ks[11], (L, GLA_HEADS * GLA_DK), 0.01),
        "gla_norm_g": 1.0 + nrm(ks[12], (L, GLA_DV), 0.02),
        "w_out": nrm(ks[13], (L, D_MODEL, D_MODEL), DEEPNORM_BETA * D_MODEL ** -0.5),
        "ln1_g": 1.0 + nrm(ks[14], (L, D_MODEL), 0.02),
        "ln1_b": nrm(ks[15], (L, D_MODEL), 0.01),
        "w_router": nrm(ks[16], (L, D_MODEL, N_EXPERTS), D_MODEL ** -0.5),
        "b_router": nrm(ks[17], (L, N_EXPERTS), 0.01),
        "w_up": nrm(ks[18], (L, N_EXPERTS, D_MODEL, 2 * D_FF_2), D_MODEL ** -0.5),
        "b_up": nrm(ks[19], (L, N_EXPERTS, 2 * D_FF_2), 0.01),
        "w_down": nrm(ks[20], (L, N_EXPERTS, D_FF_2, D_MODEL), DEEPNORM_BETA * D_FF_2 ** -0.5),
        "b_down": nrm(ks[21], (L, N_EXPERTS, D_MODEL), 0.01),
        "ln2_g": 1.0 + nrm(ks[22], (L, D_MODEL), 0.02),
        "ln2_b": nrm(ks[23], (L, D_MODEL), 0.01),
        "w_ple": nrm(ks[24], (L, PLE_DIM, D_MODEL), PLE_DIM ** -0.5),
        "w_ple_gate": nrm(ks[25], (L, D_MODEL, D_MODEL), D_MODEL ** -0.5),
        "b_ple_gate": nrm(ks[26], (L, D_MODEL), 0.01),
    }

def second_block(x, p, w_in, conv_w, conv_b, lru_w_r, lru_b_r, lru_w_i, lru_b_i, lru_lambda,
              gla_w_gate, gla_b_gate, gla_norm_g, w_out, ln1_g, ln1_b,
              w_router, b_router, w_up, b_up, w_down, b_down, ln2_g, ln2_b,
              w_ple, w_ple_gate, b_ple_gate):
    bsz, s, d = x.shape
    h = x
    for i in range(DEPTH_2):
        proj = h @ w_in[i]
        xa, ga, q, k, v, go, glr, ma, mb = jnp.split(proj, IN_SPLITS, axis=-1)

        xa = causal_depthwise_conv(xa, conv_w[i], conv_b[i])
        ya = rg_lru(xa, lru_w_r[i], lru_b_r[i], lru_w_i[i], lru_b_i[i], lru_lambda[i])
        ya = ya * jax.nn.gelu(ga)

        log_g = jax.nn.log_sigmoid(glr @ gla_w_gate[i] + gla_b_gate[i]) / GLA_TAU
        o = gla_chunked(q.reshape(bsz, s, GLA_HEADS, GLA_DK),
                        k.reshape(bsz, s, GLA_HEADS, GLA_DK),
                        v.reshape(bsz, s, GLA_HEADS, GLA_DV),
                        log_g.reshape(bsz, s, GLA_HEADS, GLA_DK))
        o = o * lax.rsqrt(jnp.mean(jnp.square(o), axis=-1, keepdims=True) + RMS_EPS) * gla_norm_g[i]
        yb = o.reshape(bsz, s, GLA_HEADS * GLA_DV).astype(h.dtype) * jax.nn.silu(go)

        y = jax.nn.sigmoid(ma) * ya + jax.nn.sigmoid(mb) * yb
        h = layer_norm(DEEPNORM_ALPHA * h + y @ w_out[i], ln1_g[i], ln1_b[i])

        m = moe(h, w_router[i], b_router[i], w_up[i], b_up[i], w_down[i], b_down[i])
        h = layer_norm(DEEPNORM_ALPHA * h + m, ln2_g[i], ln2_b[i])

        h = h + jax.nn.sigmoid(h @ w_ple_gate[i] + b_ple_gate[i]) * (p[i] @ w_ple[i])
    return h


_first_inputs = second_inputs


def second_inputs(seed=0):
    import zlib

    import numpy as np

    out = dict(_first_inputs(seed))
    spreads = {}
    factors = {'conv_b': 4.443,
     'lru_b_r': 182.534,
     'lru_b_i': 124.051,
     'gla_b_gate': 8.0,
     'gla_norm_g': 6.054,
     'ln1_b': 3.182,
     'b_router': 4.893,
     'b_up': 8.0,
     'b_down': 8.0,
     'ln2_g': 25.171,
     'ln2_b': 51.969,
     'b_ple_gate': 200.0}
    for name, (base, spread) in spreads.items():
        noise = np.random.default_rng([zlib.crc32(name.encode()), seed]).standard_normal(out[name].shape)
        drawn = base * np.exp(spread * noise) if base else spread * noise
        out[name] = __import__('jax').numpy.asarray(drawn.astype(out[name].dtype))
    for name, factor in factors.items():
        out[name] = (out[name] * factor).astype(out[name].dtype)
    return out


def setup_inputs(seed=0):
    out = dict(first_inputs(seed))
    for name, value in second_inputs(seed + 1).items():
        if name != "x":
            out[name + "_2"] = value
    return out


def reference(
    x, c, ctx, c_ctx, w_ada, b_ada, g_pre_mix, w_in, sink, w_sgu, b_sgu, g_sgu, g_mix, w_out,
    g_post_mix, g_pre_ff, w_ff1, w_ff2, g_post_ff, p_2, w_in_2, conv_w_2, conv_b_2, lru_w_r_2,
    lru_b_r_2, lru_w_i_2, lru_b_i_2, lru_lambda_2, gla_w_gate_2, gla_b_gate_2, gla_norm_g_2,
    w_out_2, ln1_g_2, ln1_b_2, w_router_2, b_router_2, w_up_2, b_up_2, w_down_2, b_down_2,
    ln2_g_2, ln2_b_2, w_ple_2, w_ple_gate_2, b_ple_gate_2,
):
    x = first_block(
        x, c, ctx, c_ctx, w_ada, b_ada, g_pre_mix, w_in, sink, w_sgu, b_sgu, g_sgu, g_mix,
        w_out, g_post_mix, g_pre_ff, w_ff1, w_ff2, g_post_ff,
    )
    return second_block(
        x, p_2, w_in_2, conv_w_2, conv_b_2, lru_w_r_2, lru_b_r_2, lru_w_i_2, lru_b_i_2,
        lru_lambda_2, gla_w_gate_2, gla_b_gate_2, gla_norm_g_2, w_out_2, ln1_g_2, ln1_b_2,
        w_router_2, b_router_2, w_up_2, b_up_2, w_down_2, b_down_2, ln2_g_2, ln2_b_2, w_ple_2,
        w_ple_gate_2, b_ple_gate_2,
    )


_drawn_inputs = setup_inputs


def setup_inputs(seed=0):
    import zlib

    import numpy as np

    out = dict(_drawn_inputs(seed))
    spreads = {}
    factors = {'sink': 8.0,
     'b_sgu': 7.235,
     'g_sgu': 36.945,
     'ln2_g_2': 8.696,
     'ln2_b_2': 8.138,
     'w_ple_gate_2': 23.648,
     'b_ple_gate_2': 200.0,
     'p_2': 5.972,
     'w_ple_2': 5.931}
    for name, (base, spread) in spreads.items():
        noise = np.random.default_rng([zlib.crc32(name.encode()), seed]).standard_normal(out[name].shape)
        drawn = base * np.exp(spread * noise) if base else spread * noise
        out[name] = __import__('jax').numpy.asarray(drawn.astype(out[name].dtype))
    for name, factor in factors.items():
        out[name] = (out[name] * factor).astype(out[name].dtype)
    return out
```

```python
import math
from contextlib import ExitStack

import numpy as np
import concourse.bass as bass
from concourse import mybir
from concourse.alu_op_type import AluOpType as ALU

F32 = mybir.dt.float32
ACT = mybir.ActivationFunctionType
AX = mybir.AxisListType

NEXP = 32
RING = 6
CW = 4096


def smalls(depth=2):
    one = [("cc", 16), ("ident", 128), ("ropec", 256), ("ropes", 256), ("rot", 128),
           ("bd", 256), ("dftc", 512), ("dfts", 512), ("band", 512)]
    for l in range(depth):
        one += [(f"b_ada{l}", 48), (f"g_pre_mix{l}", 8), (f"g_mix{l}", 8), (f"g_post_mix{l}", 8),
                (f"g_pre_ff{l}", 8), (f"g_post_ff{l}", 8), (f"sink{l}", 16), (f"b_sgu{l}", 256),
                (f"g_sgu{l}", 256), (f"w_sgu{l}", 512)]
    two = [("lev", 1024), ("conv_w", 32), ("conv_b", 8), ("lru_b_r", 8), ("lru_b_i", 8), ("lam", 8),
           ("gla_b", 4), ("gla_g", 2), ("ln1_g", 8), ("ln1_b", 8), ("ln2_g", 8), ("ln2_b", 8),
           ("b_ple", 8), ("b_router", 32), ("b_up", 512), ("w_router", 256), ("w_glr", 128),
           ("w_gate", 512), ("lru_w_r", 1024), ("lru_w_i", 1024), ("p", 512), ("w_ple", 2048)]
    out = []
    for fields in (one, two):
        at, table = 0, {}
        for n, w in fields:
            table[n] = (at, w)
            at += w
        out.append((table, at))
    return out


class Queue:

    def __init__(self, sem, depth=None):
        self.sem, self.n, self.items, self.seen, self.depth = sem, 0, [], {}, depth

    def wait(self, *toks):
        for t in toks:
            if t is None:
                continue
            if isinstance(t, list):
                self.wait(*t)
                continue
            s, v = t
            if self.seen.get(s.name, 0) < v:
                self.seen[s.name] = v
                self.items.append(lambda e, s=s, v=v: e.wait_ge(s, v))

    def do(self, fn, *toks):
        self.wait(*toks)
        if self.depth and self.n >= self.depth:
            self.wait((self.sem, self.n + 1 - self.depth))
        self.n += 1
        sem = self.sem
        self.items.append(lambda e: fn(e).then_inc(sem, 1))
        return (self.sem, self.n)

    def quiet(self, fn, *toks):
        self.wait(*toks)
        self.items.append(fn)

    def run(self, e):
        for i in self.items:
            i(e)


class Counter:
    def __init__(self, sem):
        self.sem, self.n = sem, 0


def build(nc, A, out):
    (T1, W1), (T2, W2) = smalls()
    ctx = ExitStack()
    with ctx:
        def sb(name, w, p=128):
            return ctx.enter_context(nc.sbuf_tensor(name, [p, w], F32))

        def sem(name):
            return ctx.enter_context(nc.semaphore(name))

        SM1 = sb("SM1", max(W1, W2 + 0))
        XS_ = sb("XS", 4096)
        HN_ = sb("HN", 4096)
        CAT_ = sb("CAT", 4096)
        BIG = sb("BIG", 16384)
        RG = sb("RG", 3 * CW)
        MISC = sb("MISC", 1100)
        MODT = sb("MODT", 96 * 2 + 16 * 6)
        STAT = sb("STAT", 512 * 3)
        BD = sb("BDN", 1024, 32)
        banks = [ctx.enter_context(nc.psum_tensor(f"B{i}", [128, 512], F32)) for i in range(8)]

        pe, act, dve, sp = Queue(sem("s_pe")), Queue(sem("s_act"), 1), Queue(sem("s_dve"), 1), Queue(sem("s_sp"))
        rel = Counter(sem("s_rel"))
        s_slot = [sem(f"s_slot{i}") for i in range(RING)]
        s_sm = sem("s_sm")
        s_sm2 = sem("s_sm2")
        s_in = sem("s_in")
        s_out = sem("s_out")

        def view(t, off, *dims):
            w = int(np.prod(dims))
            a = t[:, off:off + w]
            if len(dims) == 2:
                a = a.rearrange("p (a b) -> p a b", a=dims[0])
            elif len(dims) == 3:
                a = a.rearrange("p (a b c) -> p a b c", a=dims[0], b=dims[1])
            return a

        def s1(n, *dims):
            o, w = T1[n]
            return view(SM1, o, *(dims or (w,)))

        def s2(n, *dims):
            o, w = T2[n]
            return view(SM1, o, *(dims or (w,)))

        def mm(bank_ap, pairs, *waits, start=True, stop=True, last=None, check=True):
            n = len(pairs)
            tok = None
            pe.wait(*waits)
            for i, (l, r) in enumerate(pairs):
                st, sp_ = start and i == 0, stop and i == n - 1

                def f(e, l=l, r=r, st=st, sp_=sp_):
                    return e.matmul(bank_ap, l, r, start=st, stop=sp_, skip_group_check=not check)
                if i < n - 1:
                    pe.quiet(f)
                elif last is not None:
                    last.n += 1
                    pe.quiet(lambda e, f=f: f(e).then_inc(last.sem, 1))
                    tok = (last.sem, last.n)
                else:
                    tok = pe.do(f)
            return tok

        free = [None] * 8
        turn = [0]
        pool = list(range(8))

        def take():
            b = pool[turn[0] % len(pool)]
            turn[0] += 1
            return b

        last_use = {}
        chunks = []

        def chunk(src, slots, *extra):
            i = len(chunks)
            s = slots[0]
            chunks.append((s, None))
            prev = last_use.get(s)
            cnt = slot_cnt[s] = slot_cnt[s] + 16
            ap = ring(s)
            sp.wait(*extra)
            if prev is not None:
                sp.wait((rel.sem, prev + 1))
            sp.quiet(lambda e: e.dma_start(ap, src).then_inc(s_slot[s], 16))
            last_use[s] = i
            return s, (s_slot[s], cnt)

        slot_cnt = [0] * RING

        def ring(s):
            if s < 3:
                return RG[:, s * CW:(s + 1) * CW]
            return BIG[:, (s - 3) * CW:(s - 2) * CW]

        class Stream:

            def __init__(self):
                self.k = 0

            def next(self, src, *extra):
                s = self.order()
                self.k += 1
                return chunk(src, [s], *extra)

            def order(self):
                return self.k % 3 if not self.wide else self.seq[(self.k - self.base) % RING]

            wide = False

            def widen(self):
                self.wide, self.base = True, self.k
                a = self.k % 3
                self.seq = [a, (a + 1) % 3, (a + 2) % 3, 3, 4, 5]

        stream = Stream()

        sp.quiet(lambda e: e.dma_start(SM1[:, 0:W1], A["sm1"]).then_inc(s_sm, 16))
        sp.quiet(lambda e: e.dma_start(XS_[:, :], A["xs"]).then_inc(s_in, 16))
        t_sm, t_in = (s_sm, 16), (s_in, 16)

        XS = XS_[:, :].rearrange("p (k t) -> p k t", k=8)
        HN = HN_[:, :].rearrange("p (k t) -> p k t", k=8)
        CAT = CAT_[:, :].rearrange("p (k t) -> p k t", k=8)
        ones = MISC[:, 0:128]
        epsb = MISC[:, 128:129]
        o512, o256 = MISC[:, 130:258], MISC[:, 258:386]
        onet = MISC[:, 386:642]
        MX, DN, ES, NM, RD = (MISC[:, 642 + 4 * i:646 + 4 * i] for i in range(5))
        SV = MISC[:, 662:1100]
        t_c = []
        t_c.append(dve.do(lambda e: e.memset(ones, 1.0 / 1024)))
        t_c.append(dve.do(lambda e: e.memset(o512, 1.0 / 512)))
        t_c.append(dve.do(lambda e: e.memset(o256, 1.0 / 256)))
        t_c.append(dve.do(lambda e: e.memset(onet, 1.0)))
        t_const = t_c[-1]

        silc = MODT[:, 192:208].rearrange("p (k s) -> p k s", s=2)
        t_sil = act.do(lambda e: e.activation(MODT[:, 192:208], s1("cc"), ACT.Silu), t_sm)

        def mod(l):
            return MODT[:, 96 * l:96 * l + 96].rearrange("p (j s) -> p j s", s=2)

        def ada(l, c, src_free=None):
            s, tk = stream.next(A[f"w_ada{l}"][c])
            w = ring(s).rearrange("p (k n) -> p k n", k=8)
            b = take()
            tok = None
            for j in range(4):
                tok = mm(banks[b][:, 2 * j:2 * j + 2],
                         [(w[:, k, j * 128:(j + 1) * 128], silc[:, k, :]) for k in range(8)],
                         t_sil, tk, free[b], last=rel if j == 3 else None)
            dst = mod(l)[:, 4 * c:4 * c + 4, :]
            bias = s1(f"b_ada{l}")[:, 4 * c:4 * c + 4].rearrange("p (j o) -> p j o", o=1).broadcast_to([128, 4, 2])
            psv = banks[b][:, 0:8].rearrange("p (j s) -> p j s", s=2)
            t = dve.do(lambda e: e.tensor_tensor(dst, psv, bias, ALU.add), tok, t_sm)
            free[b] = t
            return t

        def coef(i):
            return MODT[:, 208 + 16 * i:224 + 16 * i].rearrange("p (k s) -> p k s", s=2)

        def gain(i, l, part, g, plus, tok):
            gv = s1(f"{g}{l}").rearrange("p (k o) -> p k o", o=1).broadcast_to([128, 8, 2])
            m = mod(l)[:, 8 * part:8 * part + 8, :]
            return dve.do(lambda e: e.scalar_tensor_tensor(coef(i), m, plus, gv, ALU.add, ALU.mult), tok)

        def rstd(bank, T, slot, tok, eps):
            r = STAT[:, 512 * slot:512 * slot + T]
            me = HOLD[:, 0:T]
            tm = HOLD[:, 512:512 + T]
            ps = banks[bank][:, 0:T]
            a = dve.do(lambda e: e.tensor_scalar(me, ps, eps, None, ALU.add), tok)
            free[bank] = a
            b = act.do(lambda e: e.activation(r, me, ACT.Sqrt), a)
            c = dve.do(lambda e: e.reciprocal(r, r), b)
            d = dve.do(lambda e: e.tensor_tensor(tm, r, r, ALU.mult), c)
            d = dve.do(lambda e: e.scalar_tensor_tensor(tm, tm, -0.5, me, ALU.mult, ALU.mult), d)
            d = dve.do(lambda e: e.scalar_tensor_tensor(r, tm, 1.5, r, ALU.add, ALU.mult), d)
            return r, d

        HOLD = sb("HOLD", 1024)

        def meansq(src, dst, ks, T, w, toks, dst_free=None, sl=slice(None)):
            b = take()
            ts = []
            for i, k in enumerate(ks):
                ts.append(act.do(lambda e, k=k: e.activation(dst[:, k, 0:T], src[:, k, 0:T], ACT.Square),
                                 toks[i], dst_free))
            for i, k in enumerate(ks):
                tok = mm(banks[b][:, 0:T], [(w, dst[:, k, 0:T])], ts[i], free[b], t_const,
                         start=i == 0, stop=i == len(ks) - 1)
            return b, tok

        def prenorm(l, T, toks, ca, part_sh, hn_free, eps=1e-6):
            b, tk = meansq(XS, HN, range(8), T, ones, toks, hn_free)
            r, tr = rstd(b, T, 0, tk, eps)
            m = mod(l)
            outt = []
            for k in range(8):
                tk2 = []
                for s in range(T // 256):
                    sl = slice(256 * s, 256 * s + 256)
                    a = dve.do(lambda e, k=k, s=s, sl=sl: e.scalar_tensor_tensor(
                        HN[:, k, sl], XS[:, k, sl], coef(ca)[:, k, s:s + 1], r[:, sl], ALU.mult, ALU.mult), tr, tk)
                    tk2.append(act.do(lambda e, k=k, s=s, sl=sl: e.activation(
                        HN[:, k, sl], HN[:, k, sl], ACT.Identity, bias=m[:, 8 * part_sh + k, s:s + 1]), a))
                outt.append(tk2[-1])
            return outt

        def post(l, T, Y, toks, cg, sqbuf, sq_free):
            b, tk = meansq(Y, sqbuf, range(8), T, ones, toks, sq_free)
            r, tr = rstd(b, T, 0, tk, 1e-6)
            outt = []
            for k in range(8):
                for s in range(T // 256):
                    sl = slice(256 * s, 256 * s + 256)
                    a = dve.do(lambda e, k=k, s=s, sl=sl: e.scalar_tensor_tensor(
                        Y[:, k, sl], Y[:, k, sl], coef(cg)[:, k, s:s + 1], r[:, sl], ALU.mult, ALU.mult), tr)
                a = dve.do(lambda e, k=k: e.tensor_tensor(XS[:, k, 0:T], XS[:, k, 0:T], Y[:, k, 0:T], ALU.add), a)
                outt.append(a)
            return outt, tk

        Q = view(BIG, 0, 4, 512)
        KT = view(BIG, 2048, 512)
        V = view(BIG, 2560, 4, 128)
        U = view(BIG, 3072, 2, 512)
        GV = view(BIG, 4096, 4, 256)
        FT = view(BIG, 5120, 2, 512)
        GF = view(BIG, 6144, 4, 2, 256)
        P = view(BIG, 8192, 4, 512)
        PT = view(BIG, 10240, 4, 512)
        TMPA = view(BIG, 12288, 1024)
        TMPB = view(BIG, 13312, 1024)
        FFH = view(BIG, 0, 32, 512)
        YM = view(BIG, 0, 8, 512)

        def linear(w, cols, src, T, toks, tk, emit, last_rel):
            for n, c in enumerate(cols):
                b = take()
                tok = mm(banks[b][:, 0:T], [(w[:, k, c:c + 128], src[:, k, 0:T]) for k in range(8)],
                         tk, toks, free[b], last=rel if last_rel and n == len(cols) - 1 else None)
                free[b] = emit(n, banks[b][:, 0:T], tok)

        def copy_to(dst, ps, tok, *w):
            return act.do(lambda e: e.activation(dst, ps, ACT.Copy), tok, *w)

        t_hn_free = None
        t_big_free = None
        t_cat_free = None
        x_toks = [t_in] * 8
        ada_t = {}
        for c in range(4):
            ada_t[0, c] = ada(0, c)
        ada1 = list(range(12))

        def layer(l):
            nonlocal t_hn_free, t_big_free, t_cat_free, x_toks
            T = 512 if l == 0 else 256
            NT = T // 128
            full = l == 0
            g = gain(0, l, 1, "g_pre_mix", 1.0, ada_t[l, 3])
            hn = prenorm(l, 512, x_toks, 0, 0, t_hn_free)
            dve.wait(g)
            s, tk = stream.next(A[f"w_in{l}"][0])
            w = ring(s).rearrange("p (k n) -> p k n", k=8)
            tq = []

            def e_q(n, ps, tok):
                t = copy_to(Q[:, n, 0:T], ps, tok, t_big_free)
                tq.append(t)
                return t
            linear(w, [0, 128, 256, 384], HN, T, hn, tk, e_q, True)
            s, tk = stream.next(A[f"w_in{l}"][1])
            w = ring(s).rearrange("p (k n) -> p k n", k=8)
            tkk = []

            def e_k(n, ps, tok):
                t = copy_to(KT[:, :], ps, tok)
                tkk.append(t)
                return t
            linear(w, [0], HN, 512, hn, tk, e_k, False)
            b = take()
            for tt in range(4):
                tok = mm(banks[b][:, tt * 128:tt * 128 + 128],
                         [(HN[:, k, tt * 128:tt * 128 + 128], w[:, k, 128:256]) for k in range(8)], free[b])
            tv = copy_to(V.rearrange("p a b -> p (a b)"), banks[b][:, :], tok)
            free[b] = tv
            tu = []

            def e_u(n, ps, tok):
                t = act.do(lambda e: e.activation(U[:, n, 0:T], ps, ACT.Gelu_apprx_tanh), tok)
                tu.append(t)
                return t
            linear(w, [256, 384], HN, T, hn, tk, e_u, True)
            s, tk = stream.next(A[f"w_in{l}"][2])
            w = ring(s).rearrange("p (k n) -> p k n", k=8)
            tgv = []
            for tt in range(NT):
                b = take()
                tok = mm(banks[b][:, 0:256],
                         [(HN[:, k, tt * 128:tt * 128 + 128], w[:, k, 0:256]) for k in range(8)], tk, free[b])
                t = act.do(lambda e, tt=tt, b=b: e.activation(GV[:, tt, :], banks[b][:, 0:256],
                                                             ACT.Gelu_apprx_tanh), tok)
                free[b] = t
                tgv.append(t)
            tf = []

            def e_f(n, ps, tok):
                t = copy_to(FT[:, n, 0:T], ps, tok)
                tf.append(t)
                return t
            linear(w, [256, 384], HN, T, hn, tk, e_f, True)

            for n in range(5):
                src = Q[:, n, 0:256] if n < 4 else KT[:, 0:256]
                t0 = tq[n] if n < 4 else tkk[0]
                b = take()
                tok = mm(banks[b][:, 0:256], [(s1("rot"), src)], t0, free[b])
                t = dve.do(lambda e, b=b: e.tensor_tensor(TMPA[:, 0:256], banks[b][:, 0:256], s1("ropes"), ALU.mult), tok)
                free[b] = t
                t2 = dve.do(lambda e, src=src: e.tensor_tensor(src, src, s1("ropec"), ALU.mult), t0, tok)
                t = dve.do(lambda e, src=src: e.tensor_tensor(src, src, TMPA[:, 0:256], ALU.add), t, t2)
                if n < 4:
                    tq[n] = t
                else:
                    tkk[0] = t
            G16 = NT * 4
            gvf = GV[:, 0:NT, :].rearrange("p a (h d) -> p (a h) d", d=64)
            tA = TMPB.rearrange("p (a d) -> p a d", d=64)[:, 0:G16, :]
            t = dve.do(lambda e: e.tensor_tensor(tA, gvf, gvf, ALU.mult), *tgv)
            t = dve.do(lambda e: e.tensor_reduce(SV[:, 0:G16], tA, AX.X, ALU.add), t)
            t = dve.do(lambda e: e.tensor_scalar(SV[:, 16:16 + G16], SV[:, 0:G16], 1.0 / 64, 1e-6, ALU.mult, ALU.add), t)
            t = act.do(lambda e: e.activation(SV[:, 32:32 + G16], SV[:, 16:16 + G16], ACT.Sqrt), t)
            t = dve.do(lambda e: e.reciprocal(SV[:, 48:48 + G16], SV[:, 32:32 + G16]), t)
            rb = SV[:, 48:48 + G16].rearrange("p (a o) -> p a o", o=1).broadcast_to([128, G16, 64])
            t = dve.do(lambda e: e.tensor_tensor(gvf, gvf, rb, ALU.mult), t)
            gb = s1(f"g_sgu{l}").rearrange("p (o c) -> p o c", o=1).broadcast_to([128, NT, 256])
            t_vh = dve.do(lambda e: e.tensor_tensor(GV[:, 0:NT, :], GV[:, 0:NT, :], gb, ALU.mult), t)
            wsT = s1(f"w_sgu{l}", 4, 128)
            bsg = s1(f"b_sgu{l}", 2, 128)
            cat_t = [None] * 8

            sinks = s1(f"sink{l}", 4, 4)
            band = s1("band", 2, 256)
            units = [(0, j) for j in range(4)] + ([(1, j) for j in range(4)] if full else [])
            SB, OTH = [0, 1, 2, 3], [4, 5, 6, 7]
            pool[:] = OTH
            t_exp = None
            t_pt_read = None
            t_p_read = None

            def scores(u):
                st, j = u
                toks = []
                for hf in range(2):
                    for qb in range(2):
                        i = hf * 2 + qb
                        pr = slice(64 * hf, 64 * hf + 64)
                        q = Q[pr, j, st * 256 + qb * 128:st * 256 + qb * 128 + 128]
                        ks = slice(0, 512) if st == 0 else slice(256, 512)
                        wd = 512 if st == 0 else 256
                        toks.append(mm(banks[SB[i]][:, 0:wd], [(q, KT[pr, ks])], tq[j], tkk[0], free[SB[i]]))
                return toks

            def soft(u, toks):
                st, j = u
                wd = 512 if st == 0 else 256
                ms = []
                for i in range(4):
                    bk = banks[SB[i]]
                    if st == 0:
                        t = dve.do(lambda e, bk=bk, i=i: e.tensor_tensor(bk[:, 0:256], bk[:, 0:256], band[:, i % 2, :], ALU.add), toks[i])
                    else:
                        t = toks[i]
                    ms.append(dve.do(lambda e, bk=bk, i=i: e.tensor_reduce(MX[:, i:i + 1], bk[:, 0:wd], AX.X, ALU.max), t, t_p_read))
                t = dve.do(lambda e: e.scalar_tensor_tensor(NM, MX, 0.125, sinks[:, j, :], ALU.mult, ALU.max), *ms)
                tn = dve.do(lambda e: e.tensor_scalar(MX, NM, -1.0, None, ALU.mult), t)
                td = dve.do(lambda e: e.tensor_tensor(NM, sinks[:, j, :], MX, ALU.add), tn)
                te = act.do(lambda e: e.activation(ES, NM, ACT.Exp), td)
                ex = []
                for i in range(4):
                    t = act.do(lambda e, i=i: e.activation(P[:, i, 0:wd], banks[SB[i]][:, 0:wd], ACT.Exp,
                                                          bias=MX[:, i:i + 1], scale=0.125,
                                                          accum_out=DN[:, i:i + 1]), tn, t_p_read)
                    free[SB[i]] = t
                    ex.append(t)
                t = dve.do(lambda e: e.tensor_tensor(RD, DN, ES, ALU.add), te, *ex)
                t = dve.do(lambda e: e.reciprocal(RD, RD), t)
                return [dve.do(lambda e, i=i: e.tensor_scalar(P[:, i, 0:wd], P[:, i, 0:wd], RD[:, i:i + 1], None, ALU.mult), t)
                        for i in range(4)]

            def values(u, pn):
                nonlocal t_pt_read, t_p_read
                st, j = u
                wd = 512 if st == 0 else 256
                nk = wd // 128
                cp = []
                for i in range(4):
                    b = take()
                    pe.wait(pn[i], free[b])
                    for kt in range(nk):
                        f = lambda e, b=b, kt=kt, i=i: e.transpose(banks[b][:, kt * 128:kt * 128 + 128],
                                                                  P[:, i, kt * 128:kt * 128 + 128], s1("ident"))
                        tok = pe.do(f) if kt == nk - 1 else pe.quiet(f)
                    eng = act if i % 2 else dve
                    if i % 2:
                        t = act.do(lambda e, b=b, i=i: e.activation(PT[:, i, 0:wd], banks[b][:, 0:wd], ACT.Copy), tok, t_pt_read)
                    else:
                        t = dve.do(lambda e, b=b, i=i: e.tensor_copy(PT[:, i, 0:wd], banks[b][:, 0:wd]), tok, t_pt_read)
                    free[b] = t
                    cp.append(t)
                t_p_read = tok
                b = take()
                pe.wait(free[b])
                for hf in range(2):
                    for qb in range(2):
                        i = hf * 2 + qb
                        pr = slice(64 * hf, 64 * hf + 64)
                        tok = mm(banks[b][pr, qb * 128:qb * 128 + 128],
                                 [(V[:, (kt if st == 0 else 2 + kt), 64 * hf:64 * hf + 64],
                                   PT[:, i, kt * 128:kt * 128 + 128]) for kt in range(nk)], cp[i], tv)
                t_pt_read = tok
                t = act.do(lambda e: e.activation(CAT[:, j, st * 256:st * 256 + 256], banks[b][:, 0:256], ACT.Copy),
                           tok, t_cat_free)
                free[b] = t
                cat_t[j] = t

            prev = None
            for u in units:
                tk_s = scores(u)
                if prev is not None:
                    values(*prev)
                prev = (u, soft(u, tk_s))
            values(*prev)
            pool[:] = list(range(8))

            for j in range(2):
                b = take()
                for hf in range(2):
                    h = 2 * j + hf
                    for tt in range(NT):
                        tok = mm(banks[b][64 * hf:64 * hf + 64, tt * 128:tt * 128 + 128],
                                 [(GV[:, tt, h * 64:h * 64 + 64], wsT[:, h, :])], t_vh, free[b])
                psv = banks[b][:, 0:T].rearrange("p (a t) -> p a t", t=128)
                bb = bsg[:, j:j + 1, :].broadcast_to([128, NT, 128])
                cv = CAT[:, 4 + j, 0:T].rearrange("p (a t) -> p a t", t=128)
                t = dve.do(lambda e, psv=psv, bb=bb, cv=cv: e.tensor_tensor(cv, psv, bb, ALU.add), tok, t_cat_free)
                free[b] = t
                cat_t[4 + j] = dve.do(lambda e, j=j: e.tensor_tensor(CAT[:, 4 + j, 0:T], CAT[:, 4 + j, 0:T], U[:, j, 0:T], ALU.mult), t, tu[j])
            bdm = s1("bd")
            tg = {}
            for tt in range(NT):
                b = take()
                for j in range(2):
                    tok = mm(banks[b][:, 256 * j:256 * j + 256], [(FT[:, j, tt * 128:tt * 128 + 128], bdm)], tf[j], free[b])
                t = act.do(lambda e, tt=tt, b=b: e.activation(GF[:, tt].rearrange("p a b -> p (a b)"), banks[b][:, :], ACT.Copy), tok)
                free[b] = t
                tg[tt] = t
            dc, ds = s1("dftc", 2, 256), s1("dfts", 2, 256)
            for j in range(2):
                b = take()
                for st in range(T // 256):
                    pairs = []
                    for ht in range(2):
                        pairs += [(GF[:, 2 * st + ht, j, 0:128], dc[:, ht, :]), (GF[:, 2 * st + ht, j, 128:256], ds[:, ht, :])]
                    tok = mm(banks[b][:, 256 * st:256 * st + 256], pairs, tg[2 * st], tg[2 * st + 1], free[b])
                t = act.do(lambda e, j=j, b=b: e.activation(CAT[:, 6 + j, 0:T], banks[b][:, 0:T], ACT.Copy), tok, t_cat_free)
                free[b] = t
                cat_t[6 + j] = t

            gm = s1(f"g_mix{l}")
            mt = []
            for i, (ks, w1_) in enumerate((((0, 1, 2, 3), o512), ((4, 5), o256), ((6, 7), o256))):
                b, tk_ = meansq(CAT, HN, ks, T, w1_, [cat_t[k] for k in ks])
                r, tr = rstd(b, T, i, tk_, 1e-6)
                for k in ks:
                    mt.append(dve.do(lambda e, k=k, r=r: e.scalar_tensor_tensor(
                        CAT[:, k, 0:T], CAT[:, k, 0:T], gm[:, k:k + 1], r, ALU.mult, ALU.mult), tr))
            if l == 0:
                for c in range(4, 12):
                    ada_t[0, c] = ada(0, c)
            y_t = []
            for c in range(2):
                s, tk = stream.next(A[f"w_out{l}"][c])
                w = ring(s).rearrange("p (k n) -> p k n", k=8)

                def e_y(n, ps, tok, c=c):
                    t = copy_to(YM[:, 4 * c + n, 0:T], ps, tok)
                    y_t.append(t)
                    return t
                linear(w, [0, 128, 256, 384], CAT, T, mt, tk, e_y, True)
            t_catread = (rel.sem, rel.n)
            g = gain(1, l, 2, "g_post_mix", 0.0, ada_t[l, 5])
            g = gain(2, l, 4, "g_pre_ff", 1.0, ada_t[l, 9])
            g = gain(3, l, 5, "g_post_ff", 0.0, ada_t[l, 11])
            dve.wait(g)
            x_toks, _ = post(l, T, YM, y_t, 1, HN, None)
            hn = prenorm(l, T, x_toks, 2, 3, None)
            h_t = []
            for c in range(8):
                s, tk = stream.next(A[f"w_ff1_{l}"][c])
                w = ring(s).rearrange("p (k n) -> p k n", k=8)

                def e_h(n, ps, tok, c=c):
                    k = 4 * c + n
                    a = act.do(lambda e: e.activation(FFH[:, k, 0:T], ps, ACT.Relu), tok, x_toks)
                    h_t.append(dve.do(lambda e: e.tensor_tensor(FFH[:, k, 0:T], FFH[:, k, 0:T], FFH[:, k, 0:T], ALU.mult), a))
                    return a
                linear(w, [0, 128, 256, 384], HN, T, hn, tk, e_h, True)
                if l == 0:
                    ada_t[1, c] = ada(1, c)
            y_t = []
            for c in range(8):
                s, tk = stream.next(A[f"w_ff2_{l}"][c])
                w = ring(s).rearrange("p (k n) -> p k n", k=32)
                b = take()
                tok = mm(banks[b][:, 0:T], [(w[:, k, :], FFH[:, k, 0:T]) for k in range(32)], tk, free[b], h_t, last=rel)
                t = copy_to(CAT[:, c, 0:T], banks[b][:, 0:T], tok, t_catread)
                free[b] = t
                y_t.append(t)
                if l == 0 and c < 4:
                    ada_t[1, 8 + c] = ada(1, 8 + c)
            t_big_free = (rel.sem, rel.n)
            x_toks, _ = post(l, T, CAT, y_t, 3, HN, None)
            t_cat_free = x_toks
            t_hn_free = None

        for l in range(2):
            layer(l)

        sp.wait(*x_toks)
        sp.wait((pe.sem, pe.n), (act.sem, act.n), (dve.sem, dve.n))
        sp.quiet(lambda e: e.dma_start(SM1[:, 0:W2], A["sm2"]).then_inc(s_sm2, 16))
        sp.quiet(lambda e: e.dma_start(BD[:, :], A["b_down"]).then_inc(s_sm2, 16))
        ID2 = MODT[:, 0:128]
        sp.quiet(lambda e: e.dma_start(ID2, A["ident"]).then_inc(s_sm2, 16))
        t_s2 = (s_sm2, 48)
        T = 256
        XAP = view(BIG, 0, 8, 260)
        XA = view(BIG, 2080, 8, 256)
        R = view(BIG, 4128, 8, 256)
        S_ = view(BIG, 6176, 8, 256)
        I_ = view(BIG, 8224, 8, 256)
        Q2 = view(BIG, 10272, 4, 256)
        K2 = view(BIG, 11296, 4, 256)
        V2 = view(BIG, 12320, 2, 1024)
        LG = view(BIG, 14368, 4, 256)
        GLR = view(BIG, 15392, 256)
        ET = HN_[:, 0:2048].rearrange("p (l t) -> p l t", l=8)
        KE = HN_[:, 2048:4096].rearrange("p (l t) -> p l t", l=8)
        QE = CAT_[:, 0:2048].rearrange("p (l t) -> p l t", l=8)
        YB = CAT_[:, 2048:4096].rearrange("p (k t) -> p k t", k=8)
        ACC = view(BIG, 0, 8, 256)
        H = XS[:, :, 0:256]
        SIDE = XS[:, :, 256:512]
        hsrc = x_toks

        def lin2(name, c, emit, T=256, src=XS, toks=None):
            s, tk = stream.next(A[name][c])
            w = ring(s).rearrange("p (k n) -> p k n", k=8)
            linear(w, [0, 128, 256, 384], src, T, hsrc if toks is None else toks, tk, emit, True)

        tz = dve.do(lambda e: e.memset(XAP[:, :, 0:3], 0.0), t_big_free)
        txa = [None] * 8
        cw, cb = s2("conv_w", 8, 4), s2("conv_b")
        for c in range(2):
            def e_xa(n, ps, tok, c=c):
                k = 4 * c + n
                t = act.do(lambda e: e.activation(XAP[:, k, 3:259], ps, ACT.Copy), tok, t_big_free)
                a = dve.do(lambda e: e.tensor_scalar(XA[:, k, :], XAP[:, k, 0:256], cw[:, k, 0:1], cb[:, k:k + 1],
                                                    ALU.mult, ALU.add), t, tz, t_s2)
                for i in range(1, 4):
                    a = dve.do(lambda e, i=i: e.scalar_tensor_tensor(XA[:, k, :], XAP[:, k, i:i + 256], cw[:, k, i:i + 1],
                                                                    XA[:, k, :], ALU.mult, ALU.add), a)
                txa[k] = a
                return t
            lin2("w_in_2", c, e_xa)
        tq2, tk2 = [None] * 4, [None] * 4

        def e_q2(n, ps, tok):
            tq2[n] = act.do(lambda e: e.activation(Q2[:, n, :], ps, ACT.Copy, scale=128.0 ** -0.5), tok)
            return tq2[n]
        lin2("w_in_2", 4, e_q2)

        def e_k2(n, ps, tok):
            tk2[n] = act.do(lambda e: e.activation(K2[:, n, :], ps, ACT.Copy), tok)
            return tk2[n]
        lin2("w_in_2", 5, e_k2)
        tv2 = []
        for c in range(2):
            s, tk = stream.next(A["w_in_2"][6 + c])
            w = ring(s).rearrange("p (k n) -> p k n", k=8)
            for tt in range(2):
                b = take()
                tok = mm(banks[b][:, :], [(XS[:, k, tt * 128:tt * 128 + 128], w[:, k, :]) for k in range(8)],
                         tk, free[b], last=rel if tt == 1 else None)
                t = copy_to(V2[:, tt, c * 512:c * 512 + 512], banks[b][:, :], tok)
                free[b] = t
                tv2.append(t)
        wr_, wi_ = s2("lru_w_r", 8, 128), s2("lru_w_i", 8, 128)
        br_, bi_ = s2("lru_b_r"), s2("lru_b_i")
        tr_, ti_ = [], []
        for k in range(8):
            b = take()
            tok = mm(banks[b][:, 0:256], [(wr_[:, k, :], XA[:, k, :])], txa[k], free[b], t_s2)
            t = act.do(lambda e, k=k, b=b: e.activation(R[:, k, :], banks[b][:, 0:256], ACT.Sigmoid, bias=br_[:, k:k + 1]), tok, t_s2)
            free[b] = t
            tr_.append(t)
            b = take()
            tok = mm(banks[b][:, 0:256], [(wi_[:, k, :], XA[:, k, :])], free[b])
            t = act.do(lambda e, k=k, b=b: e.activation(I_[:, k, :], banks[b][:, 0:256], ACT.Sigmoid, bias=bi_[:, k:k + 1]), tok)
            free[b] = t
            ti_.append(t)
        lam = s2("lam")
        c0, c1, c2, c3, c4 = (SV[:, 64 + 8 * i:72 + 8 * i] for i in range(5))
        t = act.do(lambda e: e.activation(c0, lam, ACT.Abs), t_s2)
        t = act.do(lambda e: e.activation(c0, c0, ACT.Exp, scale=-1.0), t)
        t = dve.do(lambda e: e.tensor_scalar(c1, c0, 2.0, None, ALU.add), t)
        t = dve.do(lambda e: e.reciprocal(c1, c1), t)
        t = dve.do(lambda e: e.tensor_tensor(c1, c1, c0, ALU.mult), t)
        t = dve.do(lambda e: e.tensor_tensor(c2, c1, c1, ALU.mult), t)
        t = dve.do(lambda e: e.tensor_scalar(c3, c2, 1.0 / 17, 1.0 / 15, ALU.mult, ALU.add), t)
        for i in (13, 11, 9, 7, 5, 3, 1):
            t = dve.do(lambda e: e.tensor_tensor(c3, c3, c2, ALU.mult), t)
            t = dve.do(lambda e, i=i: e.tensor_scalar(c3, c3, 1.0 / i, None, ALU.add), t)
        t = dve.do(lambda e: e.scalar_tensor_tensor(c3, c3, 2.0, c1, ALU.mult, ALU.mult), t)
        t = dve.do(lambda e: e.tensor_scalar(c4, lam, -1.0, 0.0, ALU.mult, ALU.max), t)
        t = dve.do(lambda e: e.tensor_tensor(c3, c3, c4, ALU.add), t)
        t = dve.do(lambda e: e.tensor_scalar(c4, c3, 8.0, None, ALU.mult), t)
        t_cl = dve.do(lambda e: e.tensor_scalar(c3, c3, -8.0, None, ALU.mult), t)
        ts_ = []
        for k in range(8):
            ts_.append(act.do(lambda e, k=k: e.activation(S_[:, k, :], R[:, k, :], ACT.Tanh, scale=c4[:, k:k + 1]), t_cl, tr_[k]))
        ta_ = []
        for k in range(8):
            ta_.append(act.do(lambda e, k=k: e.activation(R[:, k, :], R[:, k, :], ACT.Exp, scale=c3[:, k:k + 1]), ts_[k]))
        ya_t = []
        tsq = []
        for k in range(8):
            t = dve.do(lambda e, k=k: e.tensor_scalar(XAP[:, k, 0:256], S_[:, k, :], 1.0, None, ALU.add), ts_[k], txa[k])
            t = dve.do(lambda e, k=k: e.reciprocal(XAP[:, k, 0:256], XAP[:, k, 0:256]), t)
            t = dve.do(lambda e, k=k: e.scalar_tensor_tensor(S_[:, k, :], S_[:, k, :], 2.0, XAP[:, k, 0:256], ALU.mult, ALU.mult), t)
            tsq.append(act.do(lambda e, k=k: e.activation(S_[:, k, :], S_[:, k, :], ACT.Sqrt), t))
        for k in range(8):
            t = dve.do(lambda e, k=k: e.tensor_tensor(I_[:, k, :], I_[:, k, :], XA[:, k, :], ALU.mult), ti_[k])
            t = dve.do(lambda e, k=k: e.tensor_tensor(I_[:, k, :], I_[:, k, :], S_[:, k, :], ALU.mult), t, tsq[k])
            ya_t.append(dve.do(lambda e, k=k: e.tensor_tensor_scan(S_[:, k, :], R[:, k, :], I_[:, k, :], 0.0, ALU.mult, ALU.add), t, ta_[k]))
        YA = S_

        wgl = s2("w_glr", 8, 16)
        b = take()
        tok = mm(banks[b][0:16, 0:256], [(wgl[:, k, :], XS[:, k, 0:256]) for k in range(8)], free[b], t_s2)
        t = copy_to(GLR[0:16, :], banks[b][0:16, 0:256], tok)
        free[b] = t
        wg = s2("w_gate", 4, 128)
        gb_ = s2("gla_b")
        G4 = ET.rearrange("p l t -> p (l t)")[:, 0:1024].rearrange("p (h t) -> p h t", h=4)
        A4 = ET.rearrange("p l t -> p (l t)")[:, 1024:2048].rearrange("p (h t) -> p h t", h=4)
        tab, tz_ = [], []
        tgl = t
        for h in range(4):
            b = take()
            tok = mm(banks[b][:, 0:256], [(wg[0:16, h, :], GLR[0:16, :])], tgl, free[b])
            tz_.append(dve.do(lambda e, h=h, b=b: e.tensor_scalar(G4[:, h, :], banks[b][:, 0:256], gb_[:, h:h + 1], None, ALU.add), tok))
            free[b] = tz_[-1]
        t = act.do(lambda e: e.activation(A4, G4, ACT.Abs), *tz_)
        t = act.do(lambda e: e.activation(A4, A4, ACT.Exp, scale=-1.0), t)
        t = act.do(lambda e: e.activation(A4, A4, ACT.Ln, bias=1.0), t)
        t = dve.do(lambda e: e.scalar_tensor_tensor(G4, G4, 0.0, A4, ALU.min, ALU.subtract), t)
        t = dve.do(lambda e: e.tensor_scalar(G4, G4, 1.0 / 16, None, ALU.mult), t)
        tlg = []
        for h in range(4):
            tlg.append(dve.do(lambda e, h=h: e.tensor_tensor_scan(LG[:, h, :], onet, G4[:, h, :], 0.0, ALU.mult, ALU.add), t))

        GA = SIDE

        def gate(c0_, fn, put):
            for c in range(2):
                def em(n, ps, tok, c=c):
                    return put(4 * c + n, ps, tok)
                lin2("w_in_2", c0_ + c, em)

        tya = [None] * 8

        def put_ga(k, ps, tok):
            a = act.do(lambda e: e.activation(GA[:, k, :], ps, ACT.Gelu_apprx_tanh), tok)
            tya[k] = dve.do(lambda e: e.tensor_tensor(YA[:, k, :], YA[:, k, :], GA[:, k, :], ALU.mult), a, ya_t[k])
            return a
        gate(2, None, put_ga)

        def put_ma(k, ps, tok):
            a = act.do(lambda e: e.activation(XAP[:, k, 0:256], ps, ACT.Sigmoid), tok, ya_t[k])
            tya[k] = dve.do(lambda e: e.tensor_tensor(YA[:, k, :], YA[:, k, :], XAP[:, k, 0:256], ALU.mult), a, tya[k])
            return a
        gate(10, None, put_ma)
        GB = GA
        tgo = [None] * 8

        def put_go(k, ps, tok):
            tgo[k] = act.do(lambda e: e.activation(GB[:, k, :], ps, ACT.Silu), tok, tya[k])
            return tgo[k]
        gate(8, None, put_go)

        def put_mb(k, ps, tok):
            a = act.do(lambda e: e.activation(XAP[:, k, 0:256], ps, ACT.Sigmoid), tok, tya[k])
            tgo[k] = dve.do(lambda e: e.tensor_tensor(GB[:, k, :], GB[:, k, :], XAP[:, k, 0:256], ALU.mult), a, tgo[k])
            return a
        gate(12, None, put_mb)

        lev = s2("lev", 8, 128)
        gg = s2("gla_g")
        STT = XA.rearrange("p k t -> p (k t)")
        SMK = R.rearrange("p k t -> p (k t)")
        ST = STT[:, 0:384]
        SQO = STT[:, 512:1024].rearrange("p (a t) -> p a t", a=2)
        OC = STT[:, 1024:1536].rearrange("p (a t) -> p a t", a=2)
        t_ke = t_et = None
        t_smr = None
        t_st = None
        yb_t = [None] * 8
        for h in range(4):
            dts = []
            for l in range(8):
                Bq = 1 << l
                nb = 256 // (2 * Bq)
                bv = LG[:, h, :].rearrange("p (n b) -> p n b", b=2 * Bq)
                ref = bv[:, :, Bq - 1:Bq].broadcast_to([128, nb, 2 * Bq])
                dv = ET[:, l, :].rearrange("p (n b) -> p n b", b=2 * Bq)
                dts.append(dve.do(lambda e, dv=dv, bv=bv, ref=ref: e.tensor_tensor(dv, bv, ref, ALU.subtract), tlg, t_et))
            t = act.do(lambda e: e.activation(ET, ET, ACT.Abs), dts[-1])
            t = act.do(lambda e: e.activation(ET, ET, ACT.Exp, scale=-1.0), t)
            qb_ = Q2[:, h:h + 1, :].broadcast_to([128, 8, 256])
            kb_ = K2[:, h:h + 1, :].broadcast_to([128, 8, 256])
            tqe = dve.do(lambda e, qb_=qb_: e.tensor_tensor(QE, ET, qb_, ALU.mult), t, tq2[h], t_ke)
            tke = dve.do(lambda e, kb_=kb_: e.tensor_tensor(KE, ET, kb_, ALU.mult), t, tk2[h], t_ke)
            t_et = tke
            for tt in range(2):
                sl = slice(tt * 128, tt * 128 + 128)
                bs = [take(), take()]
                toks = []
                for l in range(8):
                    lh, rh = (KE[:, l, sl], QE[:, l, sl]) if l < 7 else (K2[:, h, sl], Q2[:, h, sl])
                    toks.append(mm(banks[bs[l // 4]][:, (l % 4) * 128:(l % 4) * 128 + 128], [(lh, rh)], tqe, tke, free[bs[l // 4]]))
                for i in range(2):
                    t = dve.do(lambda e, i=i, bs=bs: e.tensor_tensor(SMK[:, 512 * i:512 * i + 512], banks[bs[i]][:, :],
                                                             lev[:, 4 * i:4 * i + 4, :].rearrange("p a b -> p (a b)"), ALU.mult), toks[4 * i + 3], t_smr)
                    free[bs[i]] = t
                t_smr = t = dve.do(lambda e, tt=tt: e.tensor_reduce(ST[:, tt * 128:tt * 128 + 128],
                                                    SMK[:, 0:1024].rearrange("p (l i) -> p i l", l=8), AX.X, ALU.add), t, t_st)
                if tt == 0:
                    ts0 = t
            b = take()
            tok = mm(banks[b][:, 0:128], [(KE[:, 7, 0:128], QE[:, 7, 128:256])], free[b])
            t_ke = tok
            ts2 = dve.do(lambda e, b=b: e.tensor_copy(ST[:, 256:384], banks[b][:, 0:128]), tok)
            free[b] = ts2
            b = take()
            for vt in range(2):
                cs = slice(h * 256 + vt * 128, h * 256 + vt * 128 + 128)
                mm(banks[b][:, vt * 256:vt * 256 + 128], [(V2[:, 0, cs], ST[:, 0:128])], ts2, t_smr, free[b], tv2)
                tok = mm(banks[b][:, vt * 256 + 128:vt * 256 + 256],
                         [(V2[:, 0, cs], ST[:, 256:384]), (V2[:, 1, cs], ST[:, 128:256])])
            t_st = tok
            ov = banks[b][:, :].rearrange("p (a t) -> p a t", a=2)
            tc = act.do(lambda e, ov=ov: e.activation(OC, ov, ACT.Copy), tok, yb_t[2 * h - 1] if h else None)
            free[b] = tc
            bq, tk_ = meansq(OC, SQO, range(2), 256, o256, [tc, tc])
            r, tr = rstd(bq, 256, 0, tk_, 1e-5)
            for vt in range(2):
                k = 2 * h + vt
                t = dve.do(lambda e, vt=vt, k=k, r=r: e.scalar_tensor_tensor(YB[:, k, :], OC[:, vt, :], gg[:, vt:vt + 1], r, ALU.mult, ALU.mult), tr)
                yb_t[k] = dve.do(lambda e, k=k: e.tensor_tensor(YB[:, k, :], YB[:, k, :], GB[:, k, :], ALU.mult), t, tgo[k])
        ym_t = []
        for k in range(8):
            ym_t.append(dve.do(lambda e, k=k: e.tensor_tensor(YB[:, k, :], YB[:, k, :], YA[:, k, :], ALU.add), yb_t[k], tya[k]))

        AL = 2.0 ** 0.25
        H1 = HN[:, :, 0:256]
        H1f = HN

        def layernorm(Z, zt, dst, g_, b_, sq, extra):
            b = take()
            for k in range(8):
                tok = mm(banks[b][:, 0:256], [(ones, Z[:, k, 0:256])], zt[k], free[b], start=k == 0, stop=k == 7)
            t = dve.do(lambda e, b=b: e.tensor_copy(HOLD[:, 0:256], banks[b][:, 0:256]), tok)
            free[b] = t
            zc = []
            for k in range(8):
                zc.append(dve.do(lambda e, k=k: e.tensor_tensor(Z[:, k, 0:256], Z[:, k, 0:256], HOLD[:, 0:256], ALU.subtract), t))
            b, tk_ = meansq(Z, sq, range(8), 256, ones, zc, extra)
            r, tr = rstd(b, 256, 0, tk_, 1e-5)
            o = []
            for k in range(8):
                a = dve.do(lambda e, k=k: e.scalar_tensor_tensor(Z[:, k, 0:256], Z[:, k, 0:256], s2(g_)[:, k:k + 1], r, ALU.mult, ALU.mult), tr)
                o.append(act.do(lambda e, k=k: e.activation(dst[:, k, 0:256], Z[:, k, 0:256], ACT.Identity, bias=s2(b_)[:, k:k + 1]), a, extra))
            return o

        ztk = []
        for c in range(2):
            def e_z(n, ps, tok, c=c):
                k = 4 * c + n
                t = dve.do(lambda e: e.scalar_tensor_tensor(XS[:, k, 0:256], XS[:, k, 0:256], AL, ps, ALU.mult, ALU.add), tok)
                ztk.append(t)
                return t
            lin2("w_out_2", c, e_z, src=YB, toks=ym_t)
        h1 = layernorm(XS, ztk, HN, "ln1_g", "ln1_b", SIDE, None)

        b = take()
        wro = s2("w_router", 8, 32)
        for tt in range(2):
            tok = mm(banks[b][:, tt * 32:tt * 32 + 32], [(HN[:, k, tt * 128:tt * 128 + 128], wro[:, k, :]) for k in range(8)], h1, free[b])
        LGT = SV[:, 0:64].rearrange("p (a e) -> p a e", a=2)
        MSK = SV[:, 128:192].rearrange("p (a e) -> p a e", a=2)
        TM = SV[:, 192:256].rearrange("p (a e) -> p a e", a=2)
        GTE = SV[:, 256:320].rearrange("p (a e) -> p a e", a=2)
        EQ = SV[:, 320:384].rearrange("p (a e) -> p a e", a=2)
        M8 = SV[:, 384:400].rearrange("p (a e) -> p a e", a=2)
        c4b = SV[:, 400:408].rearrange("p (a e) -> p a e", a=2)
        brt = s2("b_router").rearrange("p (o e) -> p o e", o=1).broadcast_to([128, 2, 32])
        psl = banks[b][:, 0:64].rearrange("p (a e) -> p a e", a=2)
        t0 = dve.do(lambda e: e.tensor_tensor(LGT, psl, brt, ALU.add), tok)
        free[b] = t0
        GT = SV
        gtk = []
        for tt in range(2):
            t = dve.do(lambda e, tt=tt: e.max(M8[:, tt, :], LGT[:, tt, :]), t0)
            v4, v1 = M8[:, tt, 3:4], M8[:, tt, 0:1]
            ta = dve.do(lambda e, tt=tt, v4=v4: e.tensor_scalar(MSK[:, tt, :], LGT[:, tt, :], v4, None, ALU.is_gt), t)
            tb = dve.do(lambda e, tt=tt, v4=v4: e.tensor_scalar(EQ[:, tt, :], LGT[:, tt, :], v4, None, ALU.is_equal), t)
            tn = dve.do(lambda e, tt=tt: e.tensor_reduce(c4b[:, tt, 0:1], MSK[:, tt, :], AX.X, ALU.add), ta)
            tn = dve.do(lambda e, tt=tt: e.tensor_scalar(c4b[:, tt, 1:2], c4b[:, tt, 0:1], -1.0, 4.0, ALU.mult, ALU.add), tn)
            tc = dve.do(lambda e, tt=tt: e.tensor_tensor_scan(TM[:, tt, :], onet[:, 0:32], EQ[:, tt, :], 0.0, ALU.mult, ALU.add), tb)
            t = dve.do(lambda e, tt=tt: e.scalar_tensor_tensor(EQ[:, tt, :], TM[:, tt, :], c4b[:, tt, 1:2], EQ[:, tt, :], ALU.is_le, ALU.mult), tc, tn)
            t = dve.do(lambda e, tt=tt: e.tensor_tensor(MSK[:, tt, :], MSK[:, tt, :], EQ[:, tt, :], ALU.add), t)
            tn = dve.do(lambda e, tt=tt, v1=v1: e.tensor_scalar(c4b[:, tt, 2:3], v1, -1.0, None, ALU.mult), t)
            te = act.do(lambda e, tt=tt: e.activation(TM[:, tt, :], LGT[:, tt, :], ACT.Exp, bias=c4b[:, tt, 2:3]), tn)
            t = dve.do(lambda e, tt=tt: e.tensor_tensor(GTE[:, tt, :], TM[:, tt, :], MSK[:, tt, :], ALU.mult), te)
            t = dve.do(lambda e, tt=tt: e.tensor_reduce(c4b[:, tt, 3:4], GTE[:, tt, :], AX.X, ALU.add), t)
            t = dve.do(lambda e, tt=tt: e.reciprocal(c4b[:, tt, 3:4], c4b[:, tt, 3:4]), t)
            gtk.append(dve.do(lambda e, tt=tt: e.tensor_scalar(GTE[:, tt, :], GTE[:, tt, :], c4b[:, tt, 3:4], None, ALU.mult), t))
        b = take()
        for tt in range(2):
            pe.wait(gtk[tt], free[b])
            tok = pe.do(lambda e, tt=tt, b=b: e.transpose(banks[b][0:32, tt * 128:tt * 128 + 128], GTE[:, tt, :], ID2[:, :]))
        GTT = STAT[0:32, 1024:1280]
        t_gt = copy_to(GTT, banks[b][0:32, 0:256], tok)
        free[b] = t_gt

        acc_b = [0, 1, 2, 3]
        pe.wait(*[free[i] for i in range(4)])
        pool[:] = [4, 5, 6, 7]
        turn[0] = 0
        stream.widen()
        ACTT = CAT_[:, 0:2048].rearrange("p (k t) -> p k t", k=8)
        GBC = CAT_[:, 2048:2560].rearrange("p (a t) -> p a t", a=2)
        GH = CAT_[:, 2560:3072].rearrange("p (a t) -> p a t", a=2)
        SG = CAT_[:, 3072:3584].rearrange("p (a t) -> p a t", a=2)
        UH = CAT_[:, 3584:4096].rearrange("p (a t) -> p a t", a=2)
        bup = s2("b_up", 32, 16)
        t_bigdone = [(act.sem, act.n), (dve.sem, dve.n), (pe.sem, pe.n), (rel.sem, rel.n)]
        first_wide = [True] * 6

        def nxt(src):
            s = stream.order()
            extra = t_bigdone if s >= 3 else []
            return stream.next(src, *extra)

        def accap(d):
            return banks[acc_b[d // 2]][:, (d % 2) * 256:(d % 2) * 256 + 256]

        for d in range(8):
            mm(accap(d), [(BD[0:32, d * 128:d * 128 + 128], GTT)], t_gt, t_s2, start=d % 2 == 0, stop=False, check=False)
        a_read = None
        par = 0
        gh_free = [None, None]
        for ex in range(NEXP):
            b = take()
            selw = ID2[0:32, ex:ex + 1].broadcast_to([32, 128])
            tok = mm(banks[b][:, 0:256], [(selw, GTT)], free[b], t_s2)
            tgb = copy_to(GBC[:, ex % 2, :], banks[b][:, 0:256], tok, (dve.sem, dve.n))
            free[b] = tgb
            at = []
            for c in range(4):
                s, tk = nxt(A["w_up"][ex, c])
                w = ring(s).rearrange("p (k n) -> p k n", k=8)
                for j in range(2):
                    f = 2 * c + j
                    bg = take()
                    tg_ = mm(banks[bg][:, 0:256], [(w[:, k, j * 128:j * 128 + 128], HN[:, k, 0:256]) for k in range(8)], tk, free[bg])
                    bu = take()
                    tu_ = mm(banks[bu][:, 0:256], [(w[:, k, 256 + j * 128:384 + j * 128], HN[:, k, 0:256]) for k in range(8)],
                             free[bu], last=rel if j == 1 else None)
                    q = par = par ^ 1
                    t1 = dve.do(lambda e, bg=bg, q=q, ex=ex, f=f: e.tensor_scalar(GH[:, q, :], banks[bg][:, 0:256], bup[:, ex, f:f + 1], 7.0, ALU.add, ALU.min), tg_)
                    free[bg] = t1
                    t2 = act.do(lambda e, q=q: e.activation(SG[:, q, :], GH[:, q, :], ACT.Sigmoid, scale=1.702), t1, gh_free[q])
                    t3 = dve.do(lambda e, bu=bu, q=q, ex=ex, f=f: e.tensor_scalar(UH[:, q, :], banks[bu][:, 0:256], bup[:, ex, 8 + f:9 + f], 7.0, ALU.add, ALU.min), tu_)
                    free[bu] = t3
                    t3 = dve.do(lambda e, q=q: e.tensor_scalar(UH[:, q, :], UH[:, q, :], -7.0, 1.0, ALU.max, ALU.add), t3)
                    t3 = dve.do(lambda e, q=q: e.tensor_tensor(UH[:, q, :], UH[:, q, :], GH[:, q, :], ALU.mult), t3)
                    t4 = dve.do(lambda e, q=q, ex=ex: e.tensor_tensor(SG[:, q, :], SG[:, q, :], GBC[:, ex % 2, :], ALU.mult), t2, tgb)
                    t5 = dve.do(lambda e, q=q, f=f: e.tensor_tensor(ACTT[:, f, :], UH[:, q, :], SG[:, q, :], ALU.mult), t3, t4, a_read)
                    gh_free[q] = t5
                    at.append(t5)
            for c in range(2):
                s, tk = nxt(A["w_down"][ex, c])
                w = ring(s).rearrange("p (k n) -> p k n", k=8)
                for j in range(4):
                    d = 4 * c + j
                    tok = mm(accap(d), [(w[:, k, j * 128:j * 128 + 128], ACTT[:, k, :]) for k in range(8)], tk, at,
                             start=False, stop=ex == NEXP - 1, check=False, last=rel if j == 3 else None)
            a_read = (rel.sem, rel.n)
        t_acc = (rel.sem, rel.n)

        Z2 = XS
        zt = []
        for k in range(8):
            zt.append(dve.do(lambda e, k=k: e.scalar_tensor_tensor(XS[:, k, 0:256], HN[:, k, 0:256], AL, accap(k), ALU.mult, ALU.add), t_acc))
        for i in range(4):
            free[i] = zt[-1]
        pool[:] = list(range(8))
        h2 = layernorm(XS, zt, HN, "ln2_g", "ln2_b", SIDE, zt[-1])
        ZO = CAT_[:, 0:2048].rearrange("p (k t) -> p k t", k=8)
        OUTB = XS[:, :, 0:256]
        pT = s2("p", 2, 256)
        wp = s2("w_ple", 2, 1024)
        fin = []
        for c in range(2):
            s, tk = nxt(A["w_ple_gate"][c])
            w = ring(s).rearrange("p (k n) -> p k n", k=8)

            def e_p(n, ps, tok, c=c):
                k = 4 * c + n
                a = act.do(lambda e: e.activation(ZO[:, k, :], ps, ACT.Sigmoid, bias=s2("b_ple")[:, k:k + 1]), tok, t_acc)
                b = take()
                tok2 = mm(banks[b][:, 0:256], [(wp[:, i, k * 128:k * 128 + 128], pT[:, i, :]) for i in range(2)], free[b])
                t = dve.do(lambda e: e.tensor_tensor(ZO[:, k, :], ZO[:, k, :], banks[b][:, 0:256], ALU.mult), a, tok2)
                free[b] = t
                fin.append(dve.do(lambda e: e.tensor_tensor(ZO[:, k, :], ZO[:, k, :], HN[:, k, 0:256], ALU.add), t))
                return a
            linear(w, [0, 128, 256, 384], HN, 256, h2, tk, e_p, True)
            sp.wait(fin[-1])
            sp.quiet(lambda e, c=c: e.dma_start(out[:, 4 * c:4 * c + 4, :], ZO[:, 4 * c:4 * c + 4, :]).then_inc(s_out, 16))
        sp.wait((s_out, 32))

        block = ctx.enter_context(nc.Block())

        @block.sync
        def _(e):
            sp.run(e)

        @block.scalar
        def _(e):
            act.run(e)

        @block.vector
        def _(e):
            dve.run(e)

        @block.tensor
        def _(e):
            pe.run(e)


def constants():
    c = {}
    c["ident"] = np.eye(128)
    pos = np.arange(256)
    row, col = (pos // 64).astype(np.float32), (pos % 64).astype(np.float32)
    inv = (np.float32(10000.0) ** (-np.arange(16, dtype=np.float32) / np.float32(16))).astype(np.float32)
    ar, ac = row[:, None] * inv[None], col[:, None] * inv[None]
    ang = np.concatenate([ar, ar, ac, ac], 1).astype(np.float64)
    c["ropec"] = np.tile(np.cos(ang).T, (2, 1))
    c["ropes"] = np.tile(np.sin(ang).T, (2, 1))
    rot = np.zeros((128, 128))
    for b in (0, 64):
        for i in range(16):
            rot[b + 16 + i, b + i] = -1
            rot[b + i, b + 16 + i] = 1
            rot[b + 48 + i, b + 32 + i] = -1
            rot[b + 32 + i, b + 48 + i] = 1
    c["rot"] = rot
    k = np.arange(64)
    a64 = 2 * np.pi * ((k[:, None] * k[None]) % 64) / 64
    z = np.zeros((64, 64))
    cb, sb_ = np.cos(a64) / 128, np.sin(a64) / 128
    c["bd"] = np.concatenate([np.block([[cb, z], [z, cb]]), np.block([[sb_, z], [z, sb_]])], 1)
    t = np.arange(256)
    a = 2 * np.pi * ((t[:, None] * t[None]) % 256) / 256
    c["dftc"] = np.cos(a).reshape(2, 128, 256).transpose(1, 0, 2)
    c["dfts"] = -np.sin(a).reshape(2, 128, 256).transpose(1, 0, 2)
    q = np.arange(256).reshape(2, 128)
    c["band"] = np.where(np.abs(q[:, :, None] - t[None, None]) <= 128, 0.0, -8e30).transpose(1, 0, 2)
    lev = np.zeros((128, 8, 128))
    for j in range(128):
        for i in range(j, 128):
            lev[j, 7 if i == j else int(i ^ j).bit_length() - 1, i] = 1
    c["lev"] = lev
    return c


def pack(table, width, vals):
    sm = np.zeros((128, width), np.float32)
    for n, (o, w) in table.items():
        v = np.asarray(vals[n])
        v = v.reshape(v.shape[0], -1)
        assert v.shape[1] == w, (n, v.shape, w)
        sm[:v.shape[0], o:o + w] = v
    return sm


def col(v):
    return v.reshape(-1, 128).T


def tiles8(w):
    n = w.shape[1] // 512
    return np.ascontiguousarray(w.reshape(8, 128, n, 512).transpose(2, 1, 0, 3)).reshape(n, 128, 4096)


def layout(inp):
    f = {k: np.asarray(v) for k, v in inp.items()}
    con = constants()
    (T1, W1), (T2, W2) = smalls()
    perm = np.concatenate([np.concatenate([np.arange(64 * j, 64 * j + 64), np.arange(64 * (j + 4), 64 * (j + 4) + 64)]) for j in range(4)])
    rows = np.concatenate([perm, np.arange(512, 1024)])
    v = dict(con)
    v["cc"] = np.stack([col(f["c"][0]), col(f["c_ctx"])], -1)
    A = {}
    for l in range(2):
        v[f"b_ada{l}"] = col(f["b_ada"][l])
        for n in ("g_pre_mix", "g_post_mix", "g_pre_ff", "g_post_ff"):
            v[f"{n}{l}"] = col(f[n][l])
        v[f"g_mix{l}"] = col(f["g_mix"][l][rows])
        sk = f["sink"][l].reshape(2, 4).T
        v[f"sink{l}"] = np.broadcast_to(np.repeat(sk, 2, axis=1).reshape(1, 16), (128, 16))
        v[f"b_sgu{l}"] = np.repeat(f["b_sgu"][l].reshape(2, 2, 128).transpose(1, 0, 2), 64, axis=0)
        v[f"g_sgu{l}"] = np.broadcast_to(f["g_sgu"][l].reshape(1, 256), (128, 256))
        v[f"w_sgu{l}"] = f["w_sgu"][l].transpose(2, 0, 1)
        A[f"w_ada{l}"] = tiles8(f["w_ada"][l])
        wi = f["w_in"][l]
        A[f"w_in{l}"] = tiles8(np.concatenate([wi[:, perm], wi[:, 512:]], 1))
        A[f"w_out{l}"] = tiles8(f["w_out"][l][rows])
        A[f"w_ff1_{l}"] = tiles8(f["w_ff1"][l])
        A[f"w_ff2_{l}"] = np.ascontiguousarray(f["w_ff2"][l].reshape(32, 128, 8, 128).transpose(2, 1, 0, 3)).reshape(8, 128, 4096)
    A["sm1"] = pack(T1, W1, v)
    xs = np.concatenate([f["x"][0], f["ctx"][0]], 0)
    A["xs"] = np.ascontiguousarray(xs.T.reshape(8, 128, 512).transpose(1, 0, 2)).reshape(128, 4096)
    A["ident"] = con["ident"].astype(np.float32)
    w2 = f["w_in_2"][0]
    A["w_in_2"] = tiles8(np.concatenate([w2[:, :5120], w2[:, 5136:]], 1))
    u = {"lev": con["lev"]}
    u["conv_w"] = f["conv_w_2"][0].reshape(4, 8, 128).transpose(2, 1, 0)
    for n, s in (("conv_b", "conv_b_2"), ("lru_b_r", "lru_b_r_2"), ("lru_b_i", "lru_b_i_2"), ("lam", "lru_lambda_2"),
                 ("gla_b", "gla_b_gate_2"), ("gla_g", "gla_norm_g_2"), ("ln1_g", "ln1_g_2"), ("ln1_b", "ln1_b_2"),
                 ("ln2_g", "ln2_g_2"), ("ln2_b", "ln2_b_2"), ("b_ple", "b_ple_gate_2")):
        u[n] = col(f[s][0])
    u["b_router"] = np.broadcast_to(f["b_router_2"][0][None], (128, 32))
    u["b_up"] = f["b_up_2"][0].reshape(32, 16, 128).transpose(2, 0, 1)
    u["w_router"] = f["w_router_2"][0].reshape(8, 128, 32).transpose(1, 0, 2)
    u["w_glr"] = w2[:, 5120:5136].reshape(8, 128, 16).transpose(1, 0, 2)
    u["w_gate"] = f["gla_w_gate_2"][0]
    u["lru_w_r"] = f["lru_w_r_2"][0].transpose(1, 0, 2)
    u["lru_w_i"] = f["lru_w_i_2"][0].transpose(1, 0, 2)
    u["p"] = f["p_2"][0, 0].T.reshape(2, 128, 256).transpose(1, 0, 2)
    u["w_ple"] = f["w_ple_2"][0].reshape(2, 128, 1024).transpose(1, 0, 2)
    A["sm2"] = pack(T2, W2, u)
    A["b_down"] = f["b_down_2"][0]
    A["w_out_2"] = tiles8(f["w_out_2"][0])
    A["w_ple_gate"] = tiles8(f["w_ple_gate_2"][0])
    up = f["w_up_2"][0].reshape(32, 8, 128, 2, 4, 256).transpose(0, 4, 2, 1, 3, 5)
    A["w_up"] = np.ascontiguousarray(up).reshape(32, 4, 128, 4096)
    dn = f["w_down_2"][0].reshape(32, 8, 128, 2, 512).transpose(0, 3, 2, 1, 4)
    A["w_down"] = np.ascontiguousarray(dn).reshape(32, 2, 128, 4096)
    return A


def kernel(**inputs):
    import concourse.bacc as bacc
    from concourse.bass_utils import run_bass_kernel_spmd as run

    arrays = {k: np.ascontiguousarray(a) for k, a in layout(inputs).items()}
    nc = bacc.Bacc("TRN2", target_bir_lowering=False, num_devices=1)
    A = {n: nc.dram_tensor(f"in_{n}", a.shape, mybir.dt.from_np(a.dtype), kind="ExternalInput").ap() for n, a in arrays.items()}
    out = nc.dram_tensor("out_t", (128, 8, 256), F32, kind="ExternalOutput").ap()
    build(nc, A, out)
    r = run(nc, [{f"in_{n}": a for n, a in arrays.items()}], core_ids=[0])
    o = r.results[0]["out_t"]
    return np.ascontiguousarray(o.transpose(2, 1, 0).reshape(1, 256, 1024))
```

```python
import math
from contextlib import ExitStack

import numpy as np
import concourse.bass as bass
from concourse import mybir
from concourse.alu_op_type import AluOpType as ALU

F32 = mybir.dt.float32
ACT = mybir.ActivationFunctionType
AX = mybir.AxisListType

NEXP = 32
RING = 6
CW = 4096


def smalls(depth=2):
    one = [("cc", 16), ("ident", 128), ("ropec", 256), ("ropes", 256), ("rot", 128),
           ("bd", 256), ("dftc", 512), ("dfts", 512), ("band", 512)]
    for l in range(depth):
        one += [(f"b_ada{l}", 48), (f"g_pre_mix{l}", 8), (f"g_mix{l}", 8), (f"g_post_mix{l}", 8),
                (f"g_pre_ff{l}", 8), (f"g_post_ff{l}", 8), (f"sink{l}", 16), (f"b_sgu{l}", 256),
                (f"g_sgu{l}", 256), (f"w_sgu{l}", 512)]
    two = [("lev", 1024), ("conv_w", 32), ("conv_b", 8), ("lru_b_r", 8), ("lru_b_i", 8), ("lam", 8),
           ("gla_b", 4), ("gla_g", 2), ("ln1_g", 8), ("ln1_b", 8), ("ln2_g", 8), ("ln2_b", 8),
           ("b_ple", 8), ("b_router", 32), ("b_up", 512), ("w_router", 256), ("w_glr", 128),
           ("w_gate", 512), ("lru_w_r", 1024), ("lru_w_i", 1024), ("p", 512), ("w_ple", 2048)]
    out = []
    for fields in (one, two):
        at, table = 0, {}
        for n, w in fields:
            table[n] = (at, w)
            at += w
        out.append((table, at))
    return out


class Queue:

    def __init__(self, name, sem, depth=None):
        self.name = name
        self.sem, self.n, self.items, self.seen, self.depth = sem, 0, [], {}, depth

    def wait(self, *toks):
        for t in toks:
            if t is None:
                continue
            if isinstance(t, list):
                self.wait(*t)
                continue
            s, v = t
            if self.seen.get(s.name, 0) < v:
                self.seen[s.name] = v
                self.items.append(lambda e, s=s, v=v: e.wait_ge(s, v))

    def do(self, fn, *toks):
        self.wait(*toks)
        if self.depth and self.n >= self.depth:
            self.wait((self.sem, self.n + 1 - self.depth))
        self.n += 1
        sem = self.sem
        self.items.append(lambda e: fn(e).then_inc(sem, 1))
        return (self.sem, self.n)

    def quiet(self, fn, *toks):
        self.wait(*toks)
        self.items.append(fn)

    def run(self, e):
        self.regs = [e.alloc_register(f"{self.name}_f{i}") for i in range(NEXP)]
        self.over = e.alloc_register(f"{self.name}_over")
        self.emit(e, self.items)

    def emit(self, e, items):
        for i in items:
            if isinstance(i, tuple):
                reg, zero, other = i
                with e.If_cmp(self.over if reg is None else self.regs[reg], 0, "IS_EQ"):
                    self.emit(e, zero)
                with e.Else():
                    self.emit(e, other)
            else:
                i(e)


class Counter:
    def __init__(self, sem):
        self.sem, self.n = sem, 0


def build(nc, A, out):
    (T1, W1), (T2, W2) = smalls()
    ctx = ExitStack()
    with ctx:
        def sb(name, w, p=128):
            return ctx.enter_context(nc.sbuf_tensor(name, [p, w], F32))

        def sem(name):
            return ctx.enter_context(nc.semaphore(name))

        SM1 = sb("SM1", max(W1, W2 + 0))
        XS_ = sb("XS", 4096)
        HN_ = sb("HN", 4096)
        CAT_ = sb("CAT", 4096)
        BIG = sb("BIG", 16384)
        RG = sb("RG", 3 * CW)
        STAT = sb("STAT", 512 * 3)
        MISC = sb("MISC", 1100)
        HOLD = sb("HOLD", 1024)
        SILK = SM1[:, W1:W1 + 256]
        MODT = sb("MODT", 96 * 2 + 16 * 6)
        BD = sb("BDN", 1024, 32)
        banks = [ctx.enter_context(nc.psum_tensor(f"B{i}", [128, 512], F32)) for i in range(8)]

        pe, act, dve = Queue("pe", sem("s_pe")), Queue("act", sem("s_act"), 1), Queue("dve", sem("s_dve"), 1)
        sp = Queue("sp", sem("s_sp"))
        rel = Counter(sem("s_rel"))
        s_slot = [sem(f"s_slot{i}") for i in range(RING)]
        s_sm = sem("s_sm")
        s_sm2 = sem("s_sm2")
        s_in = sem("s_in")
        s_sm3 = sem("s_sm3")
        FLAG = ctx.enter_context(nc.sbuf_tensor("FLAG", [1, 40], mybir.dt.int32))
        s_out = sem("s_out")

        def view(t, off, *dims):
            w = int(np.prod(dims))
            a = t[:, off:off + w]
            if len(dims) == 2:
                a = a.rearrange("p (a b) -> p a b", a=dims[0])
            elif len(dims) == 3:
                a = a.rearrange("p (a b c) -> p a b c", a=dims[0], b=dims[1])
            return a

        def s1(n, *dims):
            o, w = T1[n]
            return view(SM1, o, *(dims or (w,)))

        def s2(n, *dims):
            o, w = T2[n]
            return view(SM1, o, *(dims or (w,)))

        def mm(bank_ap, pairs, *waits, start=True, stop=True, last=None, check=True):
            n = len(pairs)
            tok = None
            pe.wait(*waits)
            for i, (l, r) in enumerate(pairs):
                st, sp_ = start and i == 0, stop and i == n - 1

                def f(e, l=l, r=r, st=st, sp_=sp_):
                    return e.matmul(bank_ap, l, r, start=st, stop=sp_, skip_group_check=not check)
                if i < n - 1:
                    pe.quiet(f)
                elif last is not None:
                    last.n += 1
                    pe.quiet(lambda e, f=f: f(e).then_inc(last.sem, 1))
                    tok = (last.sem, last.n)
                else:
                    tok = pe.do(f)
            return tok

        free = [None] * 8
        turn = [0]
        pool = list(range(8))

        def take():
            b = pool[turn[0] % len(pool)]
            turn[0] += 1
            return b

        last_use = {}
        chunks = []

        def chunk(src, slots, *extra):
            i = len(chunks)
            s = slots[0]
            chunks.append((s, None))
            prev = last_use.get(s)
            cnt = slot_cnt[s] = slot_cnt[s] + 16
            ap = ring(s)
            sp.wait(*extra)
            if prev is not None:
                sp.wait((rel.sem, prev + 1))
            sp.quiet(lambda e: e.dma_start(ap, src).then_inc(s_slot[s], 16))
            last_use[s] = i
            return s, (s_slot[s], cnt)

        slot_cnt = [0] * RING

        def ring(s):
            if s < 3:
                return RG[:, s * CW:(s + 1) * CW]
            return BIG[:, (s - 3) * CW:(s - 2) * CW]

        class Stream:

            def __init__(self):
                self.k = 0

            def next(self, src, *extra):
                s = self.order()
                self.k += 1
                return chunk(src, [s], *extra)

            def order(self):
                return self.k % 3 if not self.wide else self.seq[(self.k - self.base) % RING]

            wide = False

            def widen(self):
                self.wide, self.base = True, self.k
                a = self.k % 3
                self.seq = [a, (a + 1) % 3, (a + 2) % 3, 3, 4, 5]

        stream = Stream()

        sp.quiet(lambda e: e.dma_start(SM1[:, 0:W1], A["sm1"]).then_inc(s_sm, 16))
        sp.quiet(lambda e: e.dma_start(XS_[:, :], A["xs"]).then_inc(s_in, 16))
        t_sm, t_in = (s_sm, 16), (s_in, 16)

        XS = XS_[:, :].rearrange("p (k t) -> p k t", k=8)
        HN = HN_[:, :].rearrange("p (k t) -> p k t", k=8)
        CAT = CAT_[:, :].rearrange("p (k t) -> p k t", k=8)
        ones = MISC[:, 0:128]
        epsb = MISC[:, 128:129]
        o512, o256 = MISC[:, 130:258], MISC[:, 258:386]
        onet = MISC[:, 386:642]
        MX, DN, ES, NM, RD = (MISC[:, 642 + 4 * i:646 + 4 * i] for i in range(5))
        SV = MISC[:, 662:1100]
        t_c = []
        t_c.append(dve.do(lambda e: e.memset(ones, 1.0 / 1024)))
        t_c.append(dve.do(lambda e: e.memset(o512, 1.0 / 512)))
        t_c.append(dve.do(lambda e: e.memset(o256, 1.0 / 256)))
        t_c.append(dve.do(lambda e: e.memset(onet, 1.0)))
        t_const = t_c[-1]

        SILP = HOLD[:, 0:256].rearrange("p (k s) -> p k s", s=32)
        ROW = view(SM1, W1 + 256, 2, 512)
        t = dve.do(lambda e: e.memset(HOLD[:, 0:256], 0.0))
        t_sil = act.do(lambda e: e.activation(SILP[:, :, 0:2], s1("cc", 8, 2), ACT.Silu), t_sm, t)
        t_sil = act.do(lambda e: e.activation(SILK, HOLD[:, 0:256], ACT.Copy), t_sil)
        row_free = [None, None]
        n_ada = [0]

        def mod(l):
            return MODT[:, 96 * l:96 * l + 96].rearrange("p (j s) -> p j s", s=2)

        def ada(l, c):
            s, tk = stream.next(A[f"w_ada{l}"][c])
            w = ring(s).rearrange("p (k n) -> p k n", k=8)
            b = take()
            pe.wait(t_sil, tk, free[b])
            for k in range(8):
                g = k % 4
                f = (lambda e, k=k, g=g, b=b, w=w: e.matmul(banks[b][32 * g:32 * g + 32, :],
                                                            SILK[:, 32 * k:32 * k + 32],
                                                            w[:, k, :], start=k < 4, stop=k >= 4))
                if k < 7:
                    pe.quiet(f)
                else:
                    rel.n += 1
                    pe.quiet(lambda e, f=f: f(e).then_inc(rel.sem, 1))
            q = n_ada[0] % 2
            n_ada[0] += 1
            t = act.do(lambda e: e.activation(ROW[:, q, :], banks[b][:, :], ACT.Copy), (rel.sem, rel.n), row_free[q])
            free[b] = t
            b2 = take()
            pe.wait(t, free[b2])
            for j in range(4):
                f = lambda e, j=j: e.transpose(banks[b2][:, 128 * j:128 * j + 128], ROW[:, q, 128 * j:128 * j + 128], s1("ident"))
                tok = pe.do(f) if j == 3 else pe.quiet(f)
            row_free[q] = tok
            dst = mod(l)[:, 4 * c:4 * c + 4, :]
            bias = s1(f"b_ada{l}")[:, 4 * c:4 * c + 4].rearrange("p (j o) -> p j o", o=1).broadcast_to([128, 4, 2])
            part = banks[b2][:, :].rearrange("p (j g s) -> p j g s", j=4, g=4)
            sums = MODT[:, 192:200].rearrange("p (j s) -> p j s", s=2)
            t = dve.do(lambda e: e.tensor_reduce(sums, part[:, :, :, 0:2].rearrange("p j g s -> p j s g"), AX.X, ALU.add), tok)
            free[b2] = t
            return dve.do(lambda e: e.tensor_tensor(dst, sums, bias, ALU.add), t)

        def coef(i):
            return MODT[:, 208 + 16 * i:224 + 16 * i].rearrange("p (k s) -> p k s", s=2)

        def gain(i, l, part, g, plus, tok):
            gv = s1(f"{g}{l}").rearrange("p (k o) -> p k o", o=1).broadcast_to([128, 8, 2])
            m = mod(l)[:, 8 * part:8 * part + 8, :]
            return dve.do(lambda e: e.scalar_tensor_tensor(coef(i), m, plus, gv, ALU.add, ALU.mult), tok)

        def rstd(bank, T, slot, tok, eps):
            r = STAT[:, 512 * slot:512 * slot + T]
            me = HOLD[:, 0:T]
            tm = HOLD[:, 512:512 + T]
            ps = banks[bank][:, 0:T]
            a = dve.do(lambda e: e.tensor_scalar(me, ps, eps, None, ALU.add), tok)
            free[bank] = a
            b = act.do(lambda e: e.activation(r, me, ACT.Sqrt), a)
            c = dve.do(lambda e: e.reciprocal(r, r), b)
            d = dve.do(lambda e: e.tensor_tensor(tm, r, r, ALU.mult), c)
            d = dve.do(lambda e: e.scalar_tensor_tensor(tm, tm, -0.5, me, ALU.mult, ALU.mult), d)
            d = dve.do(lambda e: e.scalar_tensor_tensor(r, tm, 1.5, r, ALU.add, ALU.mult), d)
            return r, d

        def meansq(src, dst, ks, T, w, toks, dst_free=None, sl=slice(None)):
            b = take()
            ts = []
            for i, k in enumerate(ks):
                ts.append(act.do(lambda e, k=k: e.activation(dst[:, k, 0:T], src[:, k, 0:T], ACT.Square),
                                 toks[i], dst_free))
            for i, k in enumerate(ks):
                tok = mm(banks[b][:, 0:T], [(w, dst[:, k, 0:T])], ts[i], free[b], t_const,
                         start=i == 0, stop=i == len(ks) - 1)
            return b, tok

        def prenorm(l, T, toks, ca, part_sh, hn_free, eps=1e-6):
            b, tk = meansq(XS, HN, range(8), T, ones, toks, hn_free)
            r, tr = rstd(b, T, 0, tk, eps)
            m = mod(l)
            outt = []
            for k in range(8):
                tk2 = []
                for s in range(T // 256):
                    sl = slice(256 * s, 256 * s + 256)
                    a = dve.do(lambda e, k=k, s=s, sl=sl: e.scalar_tensor_tensor(
                        HN[:, k, sl], XS[:, k, sl], coef(ca)[:, k, s:s + 1], r[:, sl], ALU.mult, ALU.mult), tr, tk)
                    tk2.append(act.do(lambda e, k=k, s=s, sl=sl: e.activation(
                        HN[:, k, sl], HN[:, k, sl], ACT.Identity, bias=m[:, 8 * part_sh + k, s:s + 1]), a))
                outt.append(tk2[-1])
            return outt

        def post(l, T, Y, toks, cg, sqbuf, sq_free):
            b, tk = meansq(Y, sqbuf, range(8), T, ones, toks, sq_free)
            r, tr = rstd(b, T, 0, tk, 1e-6)
            outt = []
            for k in range(8):
                for s in range(T // 256):
                    sl = slice(256 * s, 256 * s + 256)
                    a = dve.do(lambda e, k=k, s=s, sl=sl: e.scalar_tensor_tensor(
                        Y[:, k, sl], Y[:, k, sl], coef(cg)[:, k, s:s + 1], r[:, sl], ALU.mult, ALU.mult), tr)
                a = dve.do(lambda e, k=k: e.tensor_tensor(XS[:, k, 0:T], XS[:, k, 0:T], Y[:, k, 0:T], ALU.add), a)
                outt.append(a)
            return outt, tk

        Q = view(BIG, 0, 4, 512)
        KT = view(BIG, 2048, 512)
        V = view(BIG, 2560, 4, 128)
        U = view(BIG, 3072, 2, 512)
        GV = view(BIG, 4096, 4, 256)
        FT = view(BIG, 5120, 2, 512)
        GF = view(BIG, 6144, 4, 2, 256)
        P = view(BIG, 8192, 4, 512)
        PT = view(BIG, 10240, 4, 512)
        TMPA = view(BIG, 12288, 1024)
        TMPB = view(BIG, 13312, 1024)
        FFH = view(BIG, 0, 32, 512)
        YM = view(BIG, 0, 8, 512)

        def linear(w, cols, src, T, toks, tk, emit, last_rel):
            for n, c in enumerate(cols):
                b = take()
                tok = mm(banks[b][:, 0:T], [(w[:, k, c:c + 128], src[:, k, 0:T]) for k in range(8)],
                         tk, toks, free[b], last=rel if last_rel and n == len(cols) - 1 else None)
                free[b] = emit(n, banks[b][:, 0:T], tok)

        def copy_to(dst, ps, tok, *w):
            return act.do(lambda e: e.activation(dst, ps, ACT.Copy), tok, *w)

        t_hn_free = None
        t_big_free = None
        t_cat_free = None
        x_toks = [t_in] * 8
        ada_t = {}
        for c in range(4):
            ada_t[0, c] = ada(0, c)
        ada1 = list(range(12))

        def layer(l):
            nonlocal t_hn_free, t_big_free, t_cat_free, x_toks
            T = 512 if l == 0 else 256
            NT = T // 128
            full = l == 0
            g = gain(0, l, 1, "g_pre_mix", 1.0, ada_t[l, 3])
            hn = prenorm(l, 512, x_toks, 0, 0, t_hn_free)
            dve.wait(g)
            s, tk = stream.next(A[f"w_in{l}"][0])
            w = ring(s).rearrange("p (k n) -> p k n", k=8)
            tq = []

            def e_q(n, ps, tok):
                t = copy_to(Q[:, n, 0:T], ps, tok, t_big_free)
                tq.append(t)
                return t
            linear(w, [0, 128, 256, 384], HN, T, hn, tk, e_q, True)
            s, tk = stream.next(A[f"w_in{l}"][1])
            w = ring(s).rearrange("p (k n) -> p k n", k=8)
            tkk = []

            def e_k(n, ps, tok):
                t = copy_to(KT[:, :], ps, tok)
                tkk.append(t)
                return t
            linear(w, [0], HN, 512, hn, tk, e_k, False)
            b = take()
            for tt in range(4):
                tok = mm(banks[b][:, tt * 128:tt * 128 + 128],
                         [(HN[:, k, tt * 128:tt * 128 + 128], w[:, k, 128:256]) for k in range(8)], free[b])
            tv = copy_to(V.rearrange("p a b -> p (a b)"), banks[b][:, :], tok)
            free[b] = tv
            tu = []

            def e_u(n, ps, tok):
                t = act.do(lambda e: e.activation(U[:, n, 0:T], ps, ACT.Gelu_apprx_tanh), tok)
                tu.append(t)
                return t
            linear(w, [256, 384], HN, T, hn, tk, e_u, True)
            s, tk = stream.next(A[f"w_in{l}"][2])
            w = ring(s).rearrange("p (k n) -> p k n", k=8)
            tgv = []
            for tt in range(NT):
                b = take()
                tok = mm(banks[b][:, 0:256],
                         [(HN[:, k, tt * 128:tt * 128 + 128], w[:, k, 0:256]) for k in range(8)], tk, free[b])
                t = act.do(lambda e, tt=tt, b=b: e.activation(GV[:, tt, :], banks[b][:, 0:256],
                                                             ACT.Gelu_apprx_tanh), tok)
                free[b] = t
                tgv.append(t)
            tf = []

            def e_f(n, ps, tok):
                t = copy_to(FT[:, n, 0:T], ps, tok)
                tf.append(t)
                return t
            linear(w, [256, 384], HN, T, hn, tk, e_f, True)

            for n in range(5):
                src = Q[:, n, 0:256] if n < 4 else KT[:, 0:256]
                t0 = tq[n] if n < 4 else tkk[0]
                b = take()
                tok = mm(banks[b][:, 0:256], [(s1("rot"), src)], t0, free[b])
                t = dve.do(lambda e, b=b: e.tensor_tensor(TMPA[:, 0:256], banks[b][:, 0:256], s1("ropes"), ALU.mult), tok)
                free[b] = t
                t2 = dve.do(lambda e, src=src: e.tensor_tensor(src, src, s1("ropec"), ALU.mult), t0, tok)
                t = dve.do(lambda e, src=src: e.tensor_tensor(src, src, TMPA[:, 0:256], ALU.add), t, t2)
                if n < 4:
                    tq[n] = t
                else:
                    tkk[0] = t
            G16 = NT * 4
            gvf = GV[:, 0:NT, :].rearrange("p a (h d) -> p (a h) d", d=64)
            tA = TMPB.rearrange("p (a d) -> p a d", d=64)[:, 0:G16, :]
            t = dve.do(lambda e: e.tensor_tensor(tA, gvf, gvf, ALU.mult), *tgv)
            t = dve.do(lambda e: e.tensor_reduce(SV[:, 0:G16], tA, AX.X, ALU.add), t)
            t = dve.do(lambda e: e.tensor_scalar(SV[:, 16:16 + G16], SV[:, 0:G16], 1.0 / 64, 1e-6, ALU.mult, ALU.add), t)
            t = act.do(lambda e: e.activation(SV[:, 32:32 + G16], SV[:, 16:16 + G16], ACT.Sqrt), t)
            t = dve.do(lambda e: e.reciprocal(SV[:, 48:48 + G16], SV[:, 32:32 + G16]), t)
            rb = SV[:, 48:48 + G16].rearrange("p (a o) -> p a o", o=1).broadcast_to([128, G16, 64])
            t = dve.do(lambda e: e.tensor_tensor(gvf, gvf, rb, ALU.mult), t)
            gb = s1(f"g_sgu{l}").rearrange("p (o c) -> p o c", o=1).broadcast_to([128, NT, 256])
            t_vh = dve.do(lambda e: e.tensor_tensor(GV[:, 0:NT, :], GV[:, 0:NT, :], gb, ALU.mult), t)
            wsT = s1(f"w_sgu{l}", 4, 128)
            bsg = s1(f"b_sgu{l}", 2, 128)
            cat_t = [None] * 8

            sinks = s1(f"sink{l}", 4, 4)
            band = s1("band", 2, 256)
            units = [(0, j) for j in range(4)] + ([(1, j) for j in range(4)] if full else [])
            SB, OTH = [0, 1, 2, 3], [4, 5, 6, 7]
            pool[:] = OTH
            t_exp = None
            t_pt_read = None
            t_p_read = None

            def scores(u):
                st, j = u
                toks = []
                for hf in range(2):
                    for qb in range(2):
                        i = hf * 2 + qb
                        pr = slice(64 * hf, 64 * hf + 64)
                        q = Q[pr, j, st * 256 + qb * 128:st * 256 + qb * 128 + 128]
                        ks = slice(0, 512) if st == 0 else slice(256, 512)
                        wd = 512 if st == 0 else 256
                        toks.append(mm(banks[SB[i]][:, 0:wd], [(q, KT[pr, ks])], tq[j], tkk[0], free[SB[i]]))
                return toks

            def soft(u, toks):
                st, j = u
                wd = 512 if st == 0 else 256
                ms = []
                for i in range(4):
                    bk = banks[SB[i]]
                    if st == 0:
                        t = dve.do(lambda e, bk=bk, i=i: e.tensor_tensor(bk[:, 0:256], bk[:, 0:256], band[:, i % 2, :], ALU.add), toks[i])
                    else:
                        t = toks[i]
                    ms.append(dve.do(lambda e, bk=bk, i=i: e.tensor_reduce(MX[:, i:i + 1], bk[:, 0:wd], AX.X, ALU.max), t, t_p_read))
                t = dve.do(lambda e: e.scalar_tensor_tensor(NM, MX, 0.125, sinks[:, j, :], ALU.mult, ALU.max), *ms)
                tn = dve.do(lambda e: e.tensor_scalar(MX, NM, -1.0, None, ALU.mult), t)
                td = dve.do(lambda e: e.tensor_tensor(NM, sinks[:, j, :], MX, ALU.add), tn)
                te = act.do(lambda e: e.activation(ES, NM, ACT.Exp), td)
                ex = []
                for i in range(4):
                    t = act.do(lambda e, i=i: e.activation(P[:, i, 0:wd], banks[SB[i]][:, 0:wd], ACT.Exp,
                                                          bias=MX[:, i:i + 1], scale=0.125,
                                                          accum_out=DN[:, i:i + 1]), tn, t_p_read)
                    free[SB[i]] = t
                    ex.append(t)
                t = dve.do(lambda e: e.tensor_tensor(RD, DN, ES, ALU.add), te, *ex)
                t = dve.do(lambda e: e.reciprocal(RD, RD), t)
                return [dve.do(lambda e, i=i: e.tensor_scalar(P[:, i, 0:wd], P[:, i, 0:wd], RD[:, i:i + 1], None, ALU.mult), t)
                        for i in range(4)]

            def values(u, pn):
                nonlocal t_pt_read, t_p_read
                st, j = u
                wd = 512 if st == 0 else 256
                nk = wd // 128
                cp = []
                for i in range(4):
                    b = take()
                    pe.wait(pn[i], free[b])
                    for kt in range(nk):
                        f = lambda e, b=b, kt=kt, i=i: e.transpose(banks[b][:, kt * 128:kt * 128 + 128],
                                                                  P[:, i, kt * 128:kt * 128 + 128], s1("ident"))
                        tok = pe.do(f) if kt == nk - 1 else pe.quiet(f)
                    eng = act if i % 2 else dve
                    if i % 2:
                        t = act.do(lambda e, b=b, i=i: e.activation(PT[:, i, 0:wd], banks[b][:, 0:wd], ACT.Copy), tok, t_pt_read)
                    else:
                        t = dve.do(lambda e, b=b, i=i: e.tensor_copy(PT[:, i, 0:wd], banks[b][:, 0:wd]), tok, t_pt_read)
                    free[b] = t
                    cp.append(t)
                t_p_read = tok
                b = take()
                pe.wait(free[b])
                for hf in range(2):
                    for qb in range(2):
                        i = hf * 2 + qb
                        pr = slice(64 * hf, 64 * hf + 64)
                        tok = mm(banks[b][pr, qb * 128:qb * 128 + 128],
                                 [(V[:, (kt if st == 0 else 2 + kt), 64 * hf:64 * hf + 64],
                                   PT[:, i, kt * 128:kt * 128 + 128]) for kt in range(nk)], cp[i], tv)
                t_pt_read = tok
                t = act.do(lambda e: e.activation(CAT[:, j, st * 256:st * 256 + 256], banks[b][:, 0:256], ACT.Copy),
                           tok, t_cat_free)
                free[b] = t
                cat_t[j] = t

            prev = None
            for u in units:
                tk_s = scores(u)
                if prev is not None:
                    values(*prev)
                prev = (u, soft(u, tk_s))
            values(*prev)
            pool[:] = list(range(8))

            for j in range(2):
                b = take()
                for hf in range(2):
                    h = 2 * j + hf
                    for tt in range(NT):
                        tok = mm(banks[b][64 * hf:64 * hf + 64, tt * 128:tt * 128 + 128],
                                 [(GV[:, tt, h * 64:h * 64 + 64], wsT[:, h, :])], t_vh, free[b])
                psv = banks[b][:, 0:T].rearrange("p (a t) -> p a t", t=128)
                bb = bsg[:, j:j + 1, :].broadcast_to([128, NT, 128])
                cv = CAT[:, 4 + j, 0:T].rearrange("p (a t) -> p a t", t=128)
                t = dve.do(lambda e, psv=psv, bb=bb, cv=cv: e.tensor_tensor(cv, psv, bb, ALU.add), tok, t_cat_free)
                free[b] = t
                cat_t[4 + j] = dve.do(lambda e, j=j: e.tensor_tensor(CAT[:, 4 + j, 0:T], CAT[:, 4 + j, 0:T], U[:, j, 0:T], ALU.mult), t, tu[j])
            bdm = s1("bd")
            tg = {}
            for tt in range(NT):
                b = take()
                for j in range(2):
                    tok = mm(banks[b][:, 256 * j:256 * j + 256], [(FT[:, j, tt * 128:tt * 128 + 128], bdm)], tf[j], free[b])
                t = act.do(lambda e, tt=tt, b=b: e.activation(GF[:, tt].rearrange("p a b -> p (a b)"), banks[b][:, :], ACT.Copy), tok)
                free[b] = t
                tg[tt] = t
            dc, ds = s1("dftc", 2, 256), s1("dfts", 2, 256)
            for j in range(2):
                b = take()
                for st in range(T // 256):
                    pairs = []
                    for ht in range(2):
                        pairs += [(GF[:, 2 * st + ht, j, 0:128], dc[:, ht, :]), (GF[:, 2 * st + ht, j, 128:256], ds[:, ht, :])]
                    tok = mm(banks[b][:, 256 * st:256 * st + 256], pairs, tg[2 * st], tg[2 * st + 1], free[b])
                t = act.do(lambda e, j=j, b=b: e.activation(CAT[:, 6 + j, 0:T], banks[b][:, 0:T], ACT.Copy), tok, t_cat_free)
                free[b] = t
                cat_t[6 + j] = t

            gm = s1(f"g_mix{l}")
            mt = []
            for i, (ks, w1_) in enumerate((((0, 1, 2, 3), o512), ((4, 5), o256), ((6, 7), o256))):
                b, tk_ = meansq(CAT, HN, ks, T, w1_, [cat_t[k] for k in ks])
                r, tr = rstd(b, T, i, tk_, 1e-6)
                for k in ks:
                    mt.append(dve.do(lambda e, k=k, r=r: e.scalar_tensor_tensor(
                        CAT[:, k, 0:T], CAT[:, k, 0:T], gm[:, k:k + 1], r, ALU.mult, ALU.mult), tr))
            if l == 0:
                for c in range(4, 12):
                    ada_t[0, c] = ada(0, c)
            y_t = []
            for c in range(2):
                s, tk = stream.next(A[f"w_out{l}"][c])
                w = ring(s).rearrange("p (k n) -> p k n", k=8)

                def e_y(n, ps, tok, c=c):
                    t = copy_to(YM[:, 4 * c + n, 0:T], ps, tok)
                    y_t.append(t)
                    return t
                linear(w, [0, 128, 256, 384], CAT, T, mt, tk, e_y, True)
            t_catread = (rel.sem, rel.n)
            g = gain(1, l, 2, "g_post_mix", 0.0, ada_t[l, 5])
            g = gain(2, l, 4, "g_pre_ff", 1.0, ada_t[l, 9])
            g = gain(3, l, 5, "g_post_ff", 0.0, ada_t[l, 11])
            dve.wait(g)
            x_toks, _ = post(l, T, YM, y_t, 1, HN, None)
            hn = prenorm(l, T, x_toks, 2, 3, None)
            h_t = []
            for c in range(8):
                s, tk = stream.next(A[f"w_ff1_{l}"][c])
                w = ring(s).rearrange("p (k n) -> p k n", k=8)

                def e_h(n, ps, tok, c=c):
                    k = 4 * c + n
                    a = act.do(lambda e: e.activation(FFH[:, k, 0:T], ps, ACT.Relu), tok, x_toks)
                    h_t.append(dve.do(lambda e: e.tensor_tensor(FFH[:, k, 0:T], FFH[:, k, 0:T], FFH[:, k, 0:T], ALU.mult), a))
                    return a
                linear(w, [0, 128, 256, 384], HN, T, hn, tk, e_h, True)
                if l == 0:
                    ada_t[1, c] = ada(1, c)
            y_t = []
            for c in range(8):
                s, tk = stream.next(A[f"w_ff2_{l}"][c])
                w = ring(s).rearrange("p (k n) -> p k n", k=32)
                b = take()
                tok = mm(banks[b][:, 0:T], [(w[:, k, :], FFH[:, k, 0:T]) for k in range(32)], tk, free[b], h_t, last=rel)
                t = copy_to(CAT[:, c, 0:T], banks[b][:, 0:T], tok, t_catread)
                free[b] = t
                y_t.append(t)
                if l == 0 and c < 4:
                    ada_t[1, 8 + c] = ada(1, 8 + c)
            t_big_free = (rel.sem, rel.n)
            x_toks, _ = post(l, T, CAT, y_t, 3, HN, None)
            t_cat_free = x_toks
            t_hn_free = None

        for l in range(2):
            layer(l)

        sp.wait(*x_toks)
        sp.wait((pe.sem, pe.n), (act.sem, act.n), (dve.sem, dve.n))
        sp.quiet(lambda e: e.dma_start(SM1[:, 0:W2], A["sm2"]).then_inc(s_sm2, 16))
        sp.quiet(lambda e: e.dma_start(BD[:, :], A["b_down"]).then_inc(s_sm2, 16))
        ID2 = MODT[:, 0:128]
        sp.quiet(lambda e: e.dma_start(ID2, A["ident"]).then_inc(s_sm2, 16))
        t_s2 = (s_sm2, 48)
        T = 256
        XAP = view(BIG, 0, 8, 260)
        XA = view(BIG, 2080, 8, 256)
        R = view(BIG, 4128, 8, 256)
        S_ = view(BIG, 6176, 8, 256)
        I_ = view(BIG, 8224, 8, 256)
        Q2 = view(BIG, 10272, 4, 256)
        K2 = view(BIG, 11296, 4, 256)
        V2 = view(BIG, 12320, 2, 1024)
        LG = view(BIG, 14368, 4, 256)
        GLR = view(BIG, 15392, 256)
        ET = HN_[:, 0:2048].rearrange("p (l t) -> p l t", l=8)
        KE = HN_[:, 2048:4096].rearrange("p (l t) -> p l t", l=8)
        QE = CAT_[:, 0:2048].rearrange("p (l t) -> p l t", l=8)
        YB = CAT_[:, 2048:4096].rearrange("p (k t) -> p k t", k=8)
        ACC = view(BIG, 0, 8, 256)
        H = XS[:, :, 0:256]
        SIDE = XS[:, :, 256:512]
        hsrc = x_toks

        def lin2(name, c, emit, T=256, src=XS, toks=None):
            s, tk = stream.next(A[name][c])
            w = ring(s).rearrange("p (k n) -> p k n", k=8)
            linear(w, [0, 128, 256, 384], src, T, hsrc if toks is None else toks, tk, emit, True)

        tz = dve.do(lambda e: e.memset(XAP[:, :, 0:3], 0.0), t_big_free)
        txa = [None] * 8
        cw, cb = s2("conv_w", 8, 4), s2("conv_b")
        for c in range(2):
            def e_xa(n, ps, tok, c=c):
                k = 4 * c + n
                t = act.do(lambda e: e.activation(XAP[:, k, 3:259], ps, ACT.Copy), tok, t_big_free)
                a = dve.do(lambda e: e.tensor_scalar(XA[:, k, :], XAP[:, k, 0:256], cw[:, k, 0:1], cb[:, k:k + 1],
                                                    ALU.mult, ALU.add), t, tz, t_s2)
                for i in range(1, 4):
                    a = dve.do(lambda e, i=i: e.scalar_tensor_tensor(XA[:, k, :], XAP[:, k, i:i + 256], cw[:, k, i:i + 1],
                                                                    XA[:, k, :], ALU.mult, ALU.add), a)
                txa[k] = a
                return t
            lin2("w_in_2", c, e_xa)
        tq2, tk2 = [None] * 4, [None] * 4

        def e_q2(n, ps, tok):
            tq2[n] = act.do(lambda e: e.activation(Q2[:, n, :], ps, ACT.Copy, scale=128.0 ** -0.5), tok)
            return tq2[n]
        lin2("w_in_2", 4, e_q2)

        def e_k2(n, ps, tok):
            tk2[n] = act.do(lambda e: e.activation(K2[:, n, :], ps, ACT.Copy), tok)
            return tk2[n]
        lin2("w_in_2", 5, e_k2)
        tv2 = []
        for c in range(2):
            s, tk = stream.next(A["w_in_2"][6 + c])
            w = ring(s).rearrange("p (k n) -> p k n", k=8)
            for tt in range(2):
                b = take()
                tok = mm(banks[b][:, :], [(XS[:, k, tt * 128:tt * 128 + 128], w[:, k, :]) for k in range(8)],
                         tk, free[b], last=rel if tt == 1 else None)
                t = copy_to(V2[:, tt, c * 512:c * 512 + 512], banks[b][:, :], tok)
                free[b] = t
                tv2.append(t)
        wr_, wi_ = s2("lru_w_r", 8, 128), s2("lru_w_i", 8, 128)
        br_, bi_ = s2("lru_b_r"), s2("lru_b_i")
        tr_, ti_ = [], []
        for k in range(8):
            b = take()
            tok = mm(banks[b][:, 0:256], [(wr_[:, k, :], XA[:, k, :])], txa[k], free[b], t_s2)
            t = act.do(lambda e, k=k, b=b: e.activation(R[:, k, :], banks[b][:, 0:256], ACT.Sigmoid, bias=br_[:, k:k + 1]), tok, t_s2)
            free[b] = t
            tr_.append(t)
            b = take()
            tok = mm(banks[b][:, 0:256], [(wi_[:, k, :], XA[:, k, :])], free[b])
            t = act.do(lambda e, k=k, b=b: e.activation(I_[:, k, :], banks[b][:, 0:256], ACT.Sigmoid, bias=bi_[:, k:k + 1]), tok)
            free[b] = t
            ti_.append(t)
        lam = s2("lam")
        c0, c1, c2, c3, c4 = (SV[:, 64 + 8 * i:72 + 8 * i] for i in range(5))
        t = act.do(lambda e: e.activation(c0, lam, ACT.Abs), t_s2)
        t = act.do(lambda e: e.activation(c0, c0, ACT.Exp, scale=-1.0), t)
        t = dve.do(lambda e: e.tensor_scalar(c1, c0, 2.0, None, ALU.add), t)
        t = dve.do(lambda e: e.reciprocal(c1, c1), t)
        t = dve.do(lambda e: e.tensor_tensor(c1, c1, c0, ALU.mult), t)
        t = dve.do(lambda e: e.tensor_tensor(c2, c1, c1, ALU.mult), t)
        t = dve.do(lambda e: e.tensor_scalar(c3, c2, 1.0 / 17, 1.0 / 15, ALU.mult, ALU.add), t)
        for i in (13, 11, 9, 7, 5, 3, 1):
            t = dve.do(lambda e: e.tensor_tensor(c3, c3, c2, ALU.mult), t)
            t = dve.do(lambda e, i=i: e.tensor_scalar(c3, c3, 1.0 / i, None, ALU.add), t)
        t = dve.do(lambda e: e.scalar_tensor_tensor(c3, c3, 2.0, c1, ALU.mult, ALU.mult), t)
        t = dve.do(lambda e: e.tensor_scalar(c4, lam, -1.0, 0.0, ALU.mult, ALU.max), t)
        t = dve.do(lambda e: e.tensor_tensor(c3, c3, c4, ALU.add), t)
        t = dve.do(lambda e: e.tensor_scalar(c4, c3, 8.0, None, ALU.mult), t)
        t_cl = dve.do(lambda e: e.tensor_scalar(c3, c3, -8.0, None, ALU.mult), t)
        ts_ = []
        for k in range(8):
            ts_.append(act.do(lambda e, k=k: e.activation(S_[:, k, :], R[:, k, :], ACT.Tanh, scale=c4[:, k:k + 1]), t_cl, tr_[k]))
        ta_ = []
        for k in range(8):
            ta_.append(act.do(lambda e, k=k: e.activation(R[:, k, :], R[:, k, :], ACT.Exp, scale=c3[:, k:k + 1]), ts_[k]))
        ya_t = []
        tsq = []
        for k in range(8):
            t = dve.do(lambda e, k=k: e.tensor_scalar(XAP[:, k, 0:256], S_[:, k, :], 1.0, None, ALU.add), ts_[k], txa[k])
            t = dve.do(lambda e, k=k: e.reciprocal(XAP[:, k, 0:256], XAP[:, k, 0:256]), t)
            t = dve.do(lambda e, k=k: e.scalar_tensor_tensor(S_[:, k, :], S_[:, k, :], 2.0, XAP[:, k, 0:256], ALU.mult, ALU.mult), t)
            tsq.append(act.do(lambda e, k=k: e.activation(S_[:, k, :], S_[:, k, :], ACT.Sqrt), t))
        for k in range(8):
            t = dve.do(lambda e, k=k: e.tensor_tensor(I_[:, k, :], I_[:, k, :], XA[:, k, :], ALU.mult), ti_[k])
            t = dve.do(lambda e, k=k: e.tensor_tensor(I_[:, k, :], I_[:, k, :], S_[:, k, :], ALU.mult), t, tsq[k])
            ya_t.append(dve.do(lambda e, k=k: e.tensor_tensor_scan(S_[:, k, :], R[:, k, :], I_[:, k, :], 0.0, ALU.mult, ALU.add), t, ta_[k]))
        YA = S_

        wgl = s2("w_glr", 8, 16)
        b = take()
        tok = mm(banks[b][0:16, 0:256], [(wgl[:, k, :], XS[:, k, 0:256]) for k in range(8)], free[b], t_s2)
        t = copy_to(GLR[0:16, :], banks[b][0:16, 0:256], tok)
        free[b] = t
        wg = s2("w_gate", 4, 128)
        gb_ = s2("gla_b")
        G4 = ET.rearrange("p l t -> p (l t)")[:, 0:1024].rearrange("p (h t) -> p h t", h=4)
        A4 = ET.rearrange("p l t -> p (l t)")[:, 1024:2048].rearrange("p (h t) -> p h t", h=4)
        tab, tz_ = [], []
        tgl = t
        for h in range(4):
            b = take()
            tok = mm(banks[b][:, 0:256], [(wg[0:16, h, :], GLR[0:16, :])], tgl, free[b])
            tz_.append(dve.do(lambda e, h=h, b=b: e.tensor_scalar(G4[:, h, :], banks[b][:, 0:256], gb_[:, h:h + 1], None, ALU.add), tok))
            free[b] = tz_[-1]
        t = act.do(lambda e: e.activation(A4, G4, ACT.Abs), *tz_)
        t = act.do(lambda e: e.activation(A4, A4, ACT.Exp, scale=-1.0), t)
        t = act.do(lambda e: e.activation(A4, A4, ACT.Ln, bias=1.0), t)
        t = dve.do(lambda e: e.scalar_tensor_tensor(G4, G4, 0.0, A4, ALU.min, ALU.subtract), t)
        t = dve.do(lambda e: e.tensor_scalar(G4, G4, 1.0 / 16, None, ALU.mult), t)
        tlg = []
        for h in range(4):
            tlg.append(dve.do(lambda e, h=h: e.tensor_tensor_scan(LG[:, h, :], onet, G4[:, h, :], 0.0, ALU.mult, ALU.add), t))

        GA = SIDE

        def gate(c0_, fn, put):
            for c in range(2):
                def em(n, ps, tok, c=c):
                    return put(4 * c + n, ps, tok)
                lin2("w_in_2", c0_ + c, em)

        tya = [None] * 8

        def put_ga(k, ps, tok):
            a = act.do(lambda e: e.activation(GA[:, k, :], ps, ACT.Gelu_apprx_tanh), tok)
            tya[k] = dve.do(lambda e: e.tensor_tensor(YA[:, k, :], YA[:, k, :], GA[:, k, :], ALU.mult), a, ya_t[k])
            return a
        gate(2, None, put_ga)

        def put_ma(k, ps, tok):
            a = act.do(lambda e: e.activation(XAP[:, k, 0:256], ps, ACT.Sigmoid), tok, ya_t[k])
            tya[k] = dve.do(lambda e: e.tensor_tensor(YA[:, k, :], YA[:, k, :], XAP[:, k, 0:256], ALU.mult), a, tya[k])
            return a
        gate(10, None, put_ma)
        GB = GA
        tgo = [None] * 8

        def put_go(k, ps, tok):
            tgo[k] = act.do(lambda e: e.activation(GB[:, k, :], ps, ACT.Silu), tok, tya[k])
            return tgo[k]
        gate(8, None, put_go)

        def put_mb(k, ps, tok):
            a = act.do(lambda e: e.activation(XAP[:, k, 0:256], ps, ACT.Sigmoid), tok, tya[k])
            tgo[k] = dve.do(lambda e: e.tensor_tensor(GB[:, k, :], GB[:, k, :], XAP[:, k, 0:256], ALU.mult), a, tgo[k])
            return a
        gate(12, None, put_mb)

        lev = s2("lev", 8, 128)
        gg = s2("gla_g")
        STT = XA.rearrange("p k t -> p (k t)")
        SMK = R.rearrange("p k t -> p (k t)")
        ST = STT[:, 0:384]
        SQO = STT[:, 512:1024].rearrange("p (a t) -> p a t", a=2)
        OC = STT[:, 1024:1536].rearrange("p (a t) -> p a t", a=2)
        t_ke = t_et = None
        t_smr = None
        t_st = None
        yb_t = [None] * 8
        for h in range(4):
            dts = []
            for l in range(8):
                Bq = 1 << l
                nb = 256 // (2 * Bq)
                bv = LG[:, h, :].rearrange("p (n b) -> p n b", b=2 * Bq)
                ref = bv[:, :, Bq - 1:Bq].broadcast_to([128, nb, 2 * Bq])
                dv = ET[:, l, :].rearrange("p (n b) -> p n b", b=2 * Bq)
                dts.append(dve.do(lambda e, dv=dv, bv=bv, ref=ref: e.tensor_tensor(dv, bv, ref, ALU.subtract), tlg, t_et))
            t = act.do(lambda e: e.activation(ET, ET, ACT.Abs), dts[-1])
            t = act.do(lambda e: e.activation(ET, ET, ACT.Exp, scale=-1.0), t)
            qb_ = Q2[:, h:h + 1, :].broadcast_to([128, 8, 256])
            kb_ = K2[:, h:h + 1, :].broadcast_to([128, 8, 256])
            tqe = dve.do(lambda e, qb_=qb_: e.tensor_tensor(QE, ET, qb_, ALU.mult), t, tq2[h], t_ke)
            tke = dve.do(lambda e, kb_=kb_: e.tensor_tensor(KE, ET, kb_, ALU.mult), t, tk2[h], t_ke)
            t_et = tke
            for tt in range(2):
                sl = slice(tt * 128, tt * 128 + 128)
                bs = [take(), take()]
                toks = []
                for l in range(8):
                    lh, rh = (KE[:, l, sl], QE[:, l, sl]) if l < 7 else (K2[:, h, sl], Q2[:, h, sl])
                    toks.append(mm(banks[bs[l // 4]][:, (l % 4) * 128:(l % 4) * 128 + 128], [(lh, rh)], tqe, tke, free[bs[l // 4]]))
                for i in range(2):
                    t = dve.do(lambda e, i=i, bs=bs: e.tensor_tensor(SMK[:, 512 * i:512 * i + 512], banks[bs[i]][:, :],
                                                             lev[:, 4 * i:4 * i + 4, :].rearrange("p a b -> p (a b)"), ALU.mult), toks[4 * i + 3], t_smr)
                    free[bs[i]] = t
                t_smr = t = dve.do(lambda e, tt=tt: e.tensor_reduce(ST[:, tt * 128:tt * 128 + 128],
                                                    SMK[:, 0:1024].rearrange("p (l i) -> p i l", l=8), AX.X, ALU.add), t, t_st)
                if tt == 0:
                    ts0 = t
            b = take()
            tok = mm(banks[b][:, 0:128], [(KE[:, 7, 0:128], QE[:, 7, 128:256])], free[b])
            t_ke = tok
            ts2 = dve.do(lambda e, b=b: e.tensor_copy(ST[:, 256:384], banks[b][:, 0:128]), tok)
            free[b] = ts2
            b = take()
            for vt in range(2):
                cs = slice(h * 256 + vt * 128, h * 256 + vt * 128 + 128)
                mm(banks[b][:, vt * 256:vt * 256 + 128], [(V2[:, 0, cs], ST[:, 0:128])], ts2, t_smr, free[b], tv2)
                tok = mm(banks[b][:, vt * 256 + 128:vt * 256 + 256],
                         [(V2[:, 0, cs], ST[:, 256:384]), (V2[:, 1, cs], ST[:, 128:256])])
            t_st = tok
            ov = banks[b][:, :].rearrange("p (a t) -> p a t", a=2)
            tc = act.do(lambda e, ov=ov: e.activation(OC, ov, ACT.Copy), tok, yb_t[2 * h - 1] if h else None)
            free[b] = tc
            bq, tk_ = meansq(OC, SQO, range(2), 256, o256, [tc, tc])
            r, tr = rstd(bq, 256, 0, tk_, 1e-5)
            for vt in range(2):
                k = 2 * h + vt
                t = dve.do(lambda e, vt=vt, k=k, r=r: e.scalar_tensor_tensor(YB[:, k, :], OC[:, vt, :], gg[:, vt:vt + 1], r, ALU.mult, ALU.mult), tr)
                yb_t[k] = dve.do(lambda e, k=k: e.tensor_tensor(YB[:, k, :], YB[:, k, :], GB[:, k, :], ALU.mult), t, tgo[k])
        ym_t = []
        for k in range(8):
            ym_t.append(dve.do(lambda e, k=k: e.tensor_tensor(YB[:, k, :], YB[:, k, :], YA[:, k, :], ALU.add), yb_t[k], tya[k]))

        AL = 2.0 ** 0.25
        H1 = HN[:, :, 0:256]
        H1f = HN

        def layernorm(Z, zt, dst, g_, b_, sq, extra):
            b = take()
            for k in range(8):
                tok = mm(banks[b][:, 0:256], [(ones, Z[:, k, 0:256])], zt[k], free[b], start=k == 0, stop=k == 7)
            t = dve.do(lambda e, b=b: e.tensor_copy(HOLD[:, 0:256], banks[b][:, 0:256]), tok)
            free[b] = t
            zc = []
            for k in range(8):
                zc.append(dve.do(lambda e, k=k: e.tensor_tensor(Z[:, k, 0:256], Z[:, k, 0:256], HOLD[:, 0:256], ALU.subtract), t))
            b, tk_ = meansq(Z, sq, range(8), 256, ones, zc, extra)
            r, tr = rstd(b, 256, 0, tk_, 1e-5)
            o = []
            for k in range(8):
                a = dve.do(lambda e, k=k: e.scalar_tensor_tensor(Z[:, k, 0:256], Z[:, k, 0:256], s2(g_)[:, k:k + 1], r, ALU.mult, ALU.mult), tr)
                o.append(act.do(lambda e, k=k: e.activation(dst[:, k, 0:256], Z[:, k, 0:256], ACT.Identity, bias=s2(b_)[:, k:k + 1]), a, extra))
            return o

        ztk = []
        for c in range(2):
            def e_z(n, ps, tok, c=c):
                k = 4 * c + n
                t = dve.do(lambda e: e.scalar_tensor_tensor(XS[:, k, 0:256], XS[:, k, 0:256], AL, ps, ALU.mult, ALU.add), tok)
                ztk.append(t)
                return t
            lin2("w_out_2", c, e_z, src=YB, toks=ym_t)
        h1 = layernorm(XS, ztk, HN, "ln1_g", "ln1_b", SIDE, None)

        b = take()
        wro = s2("w_router", 8, 32)
        for tt in range(2):
            tok = mm(banks[b][:, tt * 32:tt * 32 + 32], [(HN[:, k, tt * 128:tt * 128 + 128], wro[:, k, :]) for k in range(8)], h1, free[b])
        LGT = SV[:, 0:64].rearrange("p (a e) -> p a e", a=2)
        MSK = SV[:, 128:192].rearrange("p (a e) -> p a e", a=2)
        TM = SV[:, 192:256].rearrange("p (a e) -> p a e", a=2)
        GTE = SV[:, 256:320].rearrange("p (a e) -> p a e", a=2)
        EQ = SV[:, 320:384].rearrange("p (a e) -> p a e", a=2)
        M8 = SV[:, 384:400].rearrange("p (a e) -> p a e", a=2)
        c4b = SV[:, 400:408].rearrange("p (a e) -> p a e", a=2)
        brt = s2("b_router").rearrange("p (o e) -> p o e", o=1).broadcast_to([128, 2, 32])
        psl = banks[b][:, 0:64].rearrange("p (a e) -> p a e", a=2)
        t0 = dve.do(lambda e: e.tensor_tensor(LGT, psl, brt, ALU.add), tok)
        free[b] = t0
        GT = SV
        gtk = []
        for tt in range(2):
            t = dve.do(lambda e, tt=tt: e.max(M8[:, tt, :], LGT[:, tt, :]), t0)
            v4, v1 = M8[:, tt, 3:4], M8[:, tt, 0:1]
            ta = dve.do(lambda e, tt=tt, v4=v4: e.tensor_scalar(MSK[:, tt, :], LGT[:, tt, :], v4, None, ALU.is_gt), t)
            tb = dve.do(lambda e, tt=tt, v4=v4: e.tensor_scalar(EQ[:, tt, :], LGT[:, tt, :], v4, None, ALU.is_equal), t)
            tn = dve.do(lambda e, tt=tt: e.tensor_reduce(c4b[:, tt, 0:1], MSK[:, tt, :], AX.X, ALU.add), ta)
            tn = dve.do(lambda e, tt=tt: e.tensor_scalar(c4b[:, tt, 1:2], c4b[:, tt, 0:1], -1.0, 4.0, ALU.mult, ALU.add), tn)
            tc = dve.do(lambda e, tt=tt: e.tensor_tensor_scan(TM[:, tt, :], onet[:, 0:32], EQ[:, tt, :], 0.0, ALU.mult, ALU.add), tb)
            t = dve.do(lambda e, tt=tt: e.scalar_tensor_tensor(EQ[:, tt, :], TM[:, tt, :], c4b[:, tt, 1:2], EQ[:, tt, :], ALU.is_le, ALU.mult), tc, tn)
            t = dve.do(lambda e, tt=tt: e.tensor_tensor(MSK[:, tt, :], MSK[:, tt, :], EQ[:, tt, :], ALU.add), t)
            tn = dve.do(lambda e, tt=tt, v1=v1: e.tensor_scalar(c4b[:, tt, 2:3], v1, -1.0, None, ALU.mult), t)
            te = act.do(lambda e, tt=tt: e.activation(TM[:, tt, :], LGT[:, tt, :], ACT.Exp, bias=c4b[:, tt, 2:3]), tn)
            t = dve.do(lambda e, tt=tt: e.tensor_tensor(GTE[:, tt, :], TM[:, tt, :], MSK[:, tt, :], ALU.mult), te)
            t = dve.do(lambda e, tt=tt: e.tensor_reduce(c4b[:, tt, 3:4], GTE[:, tt, :], AX.X, ALU.add), t)
            t = dve.do(lambda e, tt=tt: e.reciprocal(c4b[:, tt, 3:4], c4b[:, tt, 3:4]), t)
            gtk.append(dve.do(lambda e, tt=tt: e.tensor_scalar(GTE[:, tt, :], GTE[:, tt, :], c4b[:, tt, 3:4], None, ALU.mult), t))
        b = take()
        for tt in range(2):
            pe.wait(gtk[tt], free[b])
            tok = pe.do(lambda e, tt=tt, b=b: e.transpose(banks[b][0:32, tt * 128:tt * 128 + 128], GTE[:, tt, :], ID2[:, :]))
        GTT = STAT[0:32, 1024:1280]
        t_gt = copy_to(GTT, banks[b][0:32, 0:256], tok)
        free[b] = t_gt

        acc_b = [0, 1, 2, 3]
        pe.wait(*[free[i] for i in range(4)])
        pool[:] = [4, 5, 6, 7]
        turn[0] = 0
        stream.widen()
        ACTT = CAT_[:, 0:2048].rearrange("p (k t) -> p k t", k=8)
        GBC = CAT_[:, 2048:2560].rearrange("p (a t) -> p a t", a=2)
        GH = CAT_[:, 2560:3072].rearrange("p (a t) -> p a t", a=2)
        SG = CAT_[:, 3072:3584].rearrange("p (a t) -> p a t", a=2)
        UH = CAT_[:, 3584:4096].rearrange("p (a t) -> p a t", a=2)
        bup = s2("b_up", 32, 16)
        t = dve.do(lambda e: e.memset(view(BIG, 12288, 2048), 0.0), (act.sem, act.n), (pe.sem, pe.n), (rel.sem, rel.n))
        sp.wait((act.sem, act.n), (dve.sem, dve.n), (pe.sem, pe.n), (rel.sem, rel.n))
        sp.quiet(lambda e: e.dma_start(BIG[0:32, 12288:14336], A["b_up_rows"]).then_inc(s_sm3, 16))
        sp.quiet(lambda e: e.dma_start(HOLD[:, 256:512], A["iota"]).then_inc(s_sm3, 16))
        sp.quiet(lambda e: e.dma_start(HOLD[:, 768:896], A["tri"]).then_inc(s_sm3, 16))
        t_bupr = [t, (s_sm3, 48)]
        IOTA, IOTA2, TRI, ONE1 = HOLD[:, 256:384], HOLD[:, 384:512], HOLD[:, 768:896], onet[:, 0:128]
        for q in (pe, dve):
            q.wait(t_bupr)
        t_bigdone = [(act.sem, act.n), (dve.sem, dve.n), (pe.sem, pe.n), (rel.sem, rel.n)]
        first_wide = [True] * 6

        def nxt(src):
            s = stream.order()
            extra = t_bigdone if s >= 3 else []
            return stream.next(src, *extra)

        def accap(d):
            return banks[acc_b[d // 2]][:, (d % 2) * 256:(d % 2) * 256 + 256]

        for d in range(8):
            mm(accap(d), [(BD[0:32, d * 128:d * 128 + 128], GTT)], t_gt, t_s2, start=d % 2 == 0, stop=False, check=False)
        rel0 = rel.n
        load = [[nxt(A["w_up"][ex, c]) for c in range(4)] + [nxt(A["w_down"][ex, c]) for c in range(2)]
                for ex in range(NEXP)]

        def dense():
            gbc_free = None
            a_read = None
            par = 0
            gh_free = [None, None]
            for ex in range(NEXP):
                b = take()
                selw = ID2[0:32, ex:ex + 1].broadcast_to([32, 128])
                tok = mm(banks[b][:, 0:256], [(selw, GTT)], free[b], t_s2)
                tgb = copy_to(GBC[:, ex % 2, :], banks[b][:, 0:256], tok, gbc_free)
                free[b] = tgb
                at = []
                for c in range(4):
                    s, tk = load[ex][c]
                    w = ring(s).rearrange("p (k n) -> p k n", k=8)
                    for j in range(2):
                        f = 2 * c + j
                        bg = take()
                        tg_ = mm(banks[bg][:, 0:256], [(w[:, k, j * 256:j * 256 + 128], HN[:, k, 0:256]) for k in range(8)], tk, free[bg])
                        bu = take()
                        tu_ = mm(banks[bu][:, 0:256], [(w[:, k, j * 256 + 128:j * 256 + 256], HN[:, k, 0:256]) for k in range(8)],
                                 free[bu], last=rel if j == 1 else None)
                        q = par = par ^ 1
                        t1 = dve.do(lambda e, bg=bg, q=q, ex=ex, f=f: e.tensor_scalar(GH[:, q, :], banks[bg][:, 0:256], bup[:, ex, f:f + 1], 7.0, ALU.add, ALU.min), tg_)
                        free[bg] = t1
                        t2 = act.do(lambda e, q=q: e.activation(SG[:, q, :], GH[:, q, :], ACT.Sigmoid, scale=1.702), t1, gh_free[q])
                        t3 = dve.do(lambda e, bu=bu, q=q, ex=ex, f=f: e.tensor_scalar(UH[:, q, :], banks[bu][:, 0:256], bup[:, ex, 8 + f:9 + f], 7.0, ALU.add, ALU.min), tu_)
                        free[bu] = t3
                        t3 = dve.do(lambda e, q=q: e.tensor_scalar(UH[:, q, :], UH[:, q, :], -7.0, 1.0, ALU.max, ALU.add), t3)
                        t3 = dve.do(lambda e, q=q: e.tensor_tensor(UH[:, q, :], UH[:, q, :], GH[:, q, :], ALU.mult), t3)
                        t4 = dve.do(lambda e, q=q, ex=ex: e.tensor_tensor(SG[:, q, :], SG[:, q, :], GBC[:, ex % 2, :], ALU.mult), t2, tgb)
                        t5 = dve.do(lambda e, q=q, f=f: e.tensor_tensor(ACTT[:, f, :], UH[:, q, :], SG[:, q, :], ALU.mult), t3, t4, a_read)
                        gh_free[q] = t5
                        at.append(t5)
                gbc_free = at[-1]
                for c in range(2):
                    s, tk = load[ex][4 + c]
                    w = ring(s).rearrange("p (k n) -> p k n", k=8)
                    for j in range(4):
                        d = 4 * c + j
                        mm(accap(d), [(w[:, k, j * 128:j * 128 + 128], ACTT[:, k, :]) for k in range(8)], tk, at,
                           start=False, stop=ex == NEXP - 1, check=False, last=rel if j == 3 else None)
                a_read = (rel.sem, rel.n)

        HTM = XS_[:, 0:2048].rearrange("p (a d) -> p a d", a=2)
        XG = [XS_[:, 2048 + 1024 * i:3072 + 1024 * i].rearrange("p (k s) -> p k s", k=8) for i in range(2)]
        AV = CAT_[:, 0:1024]
        AVT = CAT_[:, 1024:2048]
        YV = CAT_[:, 2048:3072]
        SEL = CAT_[:, 3072:3328].rearrange("p (a s) -> p a s", a=2)
        SELG = CAT_[:, 3328:3584].rearrange("p (a s) -> p a s", a=2)
        SCZ = CAT_[:, 3584:4096].rearrange("p (h t) -> p h t", h=2)
        SCF = view(BIG, 15872, 256)
        G1_, S1_, U1_ = (view(BIG, 14336 + 512 * i, 2, 256) for i in range(3))
        BUPR = view(BIG, 12288, 2048)
        LENS = NEXP

        def select(ex, free_s):
            t = free_s
            for tt in range(2):
                t = dve.do(lambda e, tt=tt: e.tensor_scalar(SEL[:, tt, :], IOTA, POS[:, tt, ex:ex + 1], MSK[:, tt, ex:ex + 1],
                                                           ALU.is_equal, ALU.mult), t)
            return t

        def gather(ex, ts, x_free):
            X = XG[ex % 2]
            out_ = []
            for half in range(2):
                b = take()
                for kk in range(4):
                    k = 4 * half + kk
                    tok = mm(banks[b][:, kk * 128:kk * 128 + 128],
                             [(HTM[:, tt, k * 128:k * 128 + 128], SEL[:, tt, :]) for tt in range(2)], ts, free[b], t_htm)
                t = act.do(lambda e, X=X, half=half, b=b: e.activation(
                    X[:, 4 * half:4 * half + 4, :].rearrange("p k s -> p (k s)"), banks[b][:, :], ACT.Copy), tok, x_free)
                free[b] = t
                out_.append(t)
            return out_, tok

        def expert(ex, wide, st):
            xg_t, sel_read, scat_read = st["xg"], st["sel_read"], st["scat"]
            X = XG[ex % 2]
            C = 128 if wide else 64
            t = sel_read
            iot = IOTA if wide else IOTA2
            for tt in range(2):
                t = dve.do(lambda e, tt=tt: e.tensor_scalar(SELG[:, tt, :], iot, POS[:, tt, ex:ex + 1], GTE[:, tt, ex:ex + 1],
                                                           ALU.is_equal, ALU.mult), t)
            t_selg = t
            ts_next = select(ex + 1, sel_read) if ex + 1 < NEXP else None
            av = []
            for c in range(4):
                s, tk = load[ex][c]
                w = ring(s).rearrange("p (k n) -> p k n", k=8)
                b = take()
                pe.wait(tk, free[b], xg_t, t_bupr)
                onehot = ID2[:, ex:ex + 1].broadcast_to([128, C])
                for k in range(9):
                    for h in range(1 if wide else 2):
                        lh = X[:, k, 0:C] if k < 8 else onehot
                        if wide:
                            o_ = banks[b][:, :]
                            rh = w[:, k, :] if k < 8 else BUPR[:, c * 512:c * 512 + 512]
                        else:
                            o_ = banks[b][64 * h:64 * h + 64, 0:256]
                            rh = w[:, k, h * 256:h * 256 + 256] if k < 8 else BUPR[:, c * 512 + h * 256:c * 512 + h * 256 + 256]
                        f = lambda e, o_=o_, lh=lh, rh=rh, k=k: e.matmul(o_, lh, rh, start=k == 0, stop=k == 8)
                        if k == 8 and h == (0 if wide else 1):
                            rel.n += 1
                            pe.quiet(lambda e, f=f: f(e).then_inc(rel.sem, 1))
                        else:
                            pe.quiet(f)
                tok = (rel.sem, rel.n)
                H_ = 2 if wide else 1
                ps = banks[b][:, 0:256 * H_].rearrange("p (h g n) -> p h g n", h=H_, g=2)
                q = c % 2
                gh, sg, uh = (x_[:, q, 0:128 * H_].rearrange("p (h n) -> p h n", h=H_) for x_ in (G1_, S1_, U1_))
                AVc = AV.rearrange("p (c n) -> p c n", c=4)[:, c, 0:128 * H_].rearrange("p (h n) -> p h n", h=H_)
                t1 = dve.do(lambda e, gh=gh, ps=ps: e.tensor_scalar(gh, ps[:, :, 0, :], 7.0, None, ALU.min), tok)
                t2 = act.do(lambda e, gh=gh, sg=sg: e.activation(sg, gh, ACT.Sigmoid, scale=1.702), t1)
                t3 = dve.do(lambda e, uh=uh, ps=ps: e.tensor_scalar(uh, ps[:, :, 1, :], 7.0, -7.0, ALU.min, ALU.max), tok)
                free[b] = t3
                t3 = dve.do(lambda e, uh=uh, gh=gh: e.scalar_tensor_tensor(uh, uh, 1.0, gh, ALU.add, ALU.mult), t3)
                av.append(dve.do(lambda e, uh=uh, sg=sg, AVc=AVc: e.tensor_tensor(AVc, uh, sg, ALU.mult), t3, t2, st["avt"]))
            b = take()
            pe.wait(t_selg, free[b])
            for tt in range(2):
                f = lambda e, tt=tt, b=b: e.transpose(banks[b][:, tt * 128:tt * 128 + 128], SELG[:, tt, :], ID2)
                tok = pe.do(f) if tt else pe.quiet(f)
            for h in range(2):
                pr = slice(64 * h, 64 * h + 64)
                dst = SCF[pr, :] if wide else SCZ[pr, h, :]
                t_sc = dve.do(lambda e, b=b, pr=pr, dst=dst: e.tensor_copy(dst, banks[b][pr, 0:256]), tok, scat_read)
            free[b] = t_sc
            if ex + 1 < NEXP:
                st["xg"], _ = gather(ex + 1, ts_next, st["x_read"])
            st["sel_read"] = (pe.sem, pe.n)
            st["x_read"] = (rel.sem, rel.n)
            at = []
            for half in range(2):
                b = take()
                pe.wait(av[2 * half + 1], free[b])
                W_ = 512 if wide else 256
                for i in range(W_ // 128):
                    c, hh = (2 * half + i // 2, i % 2) if wide else (2 * half + i, 0)
                    src = AV[:, c * 256 + hh * 128:c * 256 + hh * 128 + 128]
                    f = lambda e, b=b, i=i, src=src: e.transpose(banks[b][:, i * 128:i * 128 + 128], src, ID2)
                    tok = pe.do(f) if i == W_ // 128 - 1 else pe.quiet(f)
                dst = AVT[:, half * W_:half * W_ + W_]
                t = dve.do(lambda e, b=b, dst=dst: e.tensor_copy(dst, banks[b][:, 0:W_]), tok, st["down"])
                free[b] = t
                at.append(t)
            st["avt"] = tok
            T_ = AVT[:, 0:8 * C].rearrange("p (k s) -> p k s", k=8)
            yt = []
            for c in range(2):
                s, tk = load[ex][4 + c]
                w = ring(s).rearrange("p (k n) -> p k n", k=8)
                b = take()
                pe.wait(tk, free[b], at)
                for k in range(8):
                    for h in range(1 if wide else 2):
                        if wide:
                            o_, rh = banks[b][:, :], w[:, k, :]
                        else:
                            o_, rh = banks[b][64 * h:64 * h + 64, 0:256], w[:, k, h * 256:h * 256 + 256]
                        f = lambda e, o_=o_, lh=T_[:, k, :], rh=rh, k=k: e.matmul(o_, lh, rh, start=k == 0, stop=k == 7)
                        if k == 7 and h == (0 if wide else 1):
                            rel.n += 1
                            pe.quiet(lambda e, f=f: f(e).then_inc(rel.sem, 1))
                        else:
                            pe.quiet(f)
                W_ = 512 if wide else 256
                t = act.do(lambda e, b=b, c=c: e.activation(YV[:, c * W_:c * W_ + W_], banks[b][:, 0:W_], ACT.Copy),
                           (rel.sem, rel.n), scat_read)
                free[b] = t
                yt.append(t)
            st["down"] = (rel.sem, rel.n)
            for d in range(8):
                c, j = d // 4, d % 4
                if wide:
                    lh, rh = YV[:, d * 128:d * 128 + 128], SCF
                else:
                    lh, rh = YV[:, c * 256 + (j % 2) * 128:c * 256 + (j % 2) * 128 + 128], SCZ[:, j // 2, :]
                tok = mm(accap(d), [(lh, rh)], t_sc, yt[c], start=False, stop=ex == NEXP - 1, check=False)
            st["scat"] = tok

        queues = (pe, act, dve)

        def snap():
            return [(q, q.n, dict(q.seen)) for q in queues], rel.n, list(free), turn[0]

        def restore(sn):
            for q, n, seen in sn[0]:
                q.n, q.seen, q.items = n, dict(seen), []
            rel.n, turn[0] = sn[1], sn[3]
            free[:] = sn[2]

        def fork(reg, zero, other, same):
            before = [q.items for q in queues]
            sn = snap()
            restore(sn)
            zero()
            one, end1 = [q.items for q in queues], snap()
            restore(sn)
            other()
            two, end2 = [q.items for q in queues], snap()
            if same:
                assert [x[1] for x in end1[0]] == [x[1] for x in end2[0]] and end1[1:] == end2[1:]
            for q, b_, i1, i2, e1, e2 in zip(queues, before, one, two, end1[0], end2[0]):
                q.seen = {k: min(v, e2[2].get(k, 0)) for k, v in e1[2].items()}
                q.items = b_ + [(reg, i1, i2)]

        bq_ = take()
        tok = mm(banks[bq_][:, 0:32], [(TRI, MSK[:, 0, :])], gtk, free[bq_], t_s2)
        tok = mm(banks[bq_][:, 32:64], [(ONE1, MSK[:, 0, :]), (TRI, MSK[:, 1, :])], start=True)
        tok = mm(banks[bq_][:, 64:96], [(ONE1, MSK[:, 0, :]), (ONE1, MSK[:, 1, :])], start=True)
        POS = SV[:, 0:64].rearrange("p (a e) -> p a e", a=2)
        t = dve.do(lambda e: e.tensor_copy(SV[:, 0:64], banks[bq_][:, 0:64]), tok)
        CNT = SV[0:1, 408:440 - 2]
        t = dve.do(lambda e: e.tensor_reduce(SV[0:1, 410:411], banks[bq_][0:1, 64:96], AX.X, ALU.max), t)
        t = dve.do(lambda e: e.tensor_scalar(FLAG[0:1, 32:33], SV[0:1, 410:411], 128.0, None, ALU.is_gt), t)
        t_flag = dve.do(lambda e: e.tensor_scalar(FLAG[0:1, 0:32], banks[bq_][0:1, 64:96], 64.0, None, ALU.is_gt), t)
        free[bq_] = t_flag
        tks = []
        for tt in range(2):
            for half in range(2):
                b = take()
                pe.wait(h1, free[b])
                for i in range(4):
                    k = 4 * half + i
                    f = lambda e, b=b, i=i, k=k, tt=tt: e.transpose(banks[b][:, i * 128:i * 128 + 128], HN[:, k, tt * 128:tt * 128 + 128], ID2)
                    tok = pe.do(f) if i == 3 else pe.quiet(f)
                t = act.do(lambda e, b=b, half=half, tt=tt: e.activation(HTM[:, tt, 512 * half:512 * half + 512], banks[b][:, :], ACT.Copy), tok)
                free[b] = t
                tks.append(t)
        t_htm = tks
        for q in queues:
            q.wait(t_flag, (pe.sem, pe.n), (act.sem, act.n), (dve.sem, dve.n))

            def ld(e, q=q):
                e.load(q.regs, FLAG[0:1, 0:32])
                return e.load(q.over, FLAG[0:1, 32:33])
            q.quiet(ld)

        def sparse():
            for h in range(2):
                t = dve.do(lambda e, h=h: e.memset(SCZ[64 - 64 * h:128 - 64 * h, h, :], 0.0))
            st = {"xg": None, "sel_read": None, "scat": None, "avt": None, "down": None, "x_read": None}
            ts = select(0, None)
            st["xg"], st["sel_read"] = gather(0, ts, None)
            pe.wait(t)
            for ex in range(NEXP):
                ends = []
                st0 = dict(st)

                def go(wide):
                    s_ = dict(st0)
                    expert(ex, wide, s_)
                    ends.append(s_)
                fork(ex, lambda: go(False), lambda: go(True), True)
                assert ends[0] == ends[1]
                st = ends[0]

        base = {q: (q.sem, q.n) for q in queues}
        after = {q: sem(f"s_{q.name}_z") for q in queues}

        def path(body, tag):
            for q in queues:
                q.sem, q.n = sems[tag][q], 0
            body()
            for q in queues:
                q.wait((q.sem, q.n))
                q.quiet(lambda e: e.sem_inc(s_join, 1))

        sems = {tag: {q: sem(f"s_{q.name}_{tag}") for q in queues} for tag in ("f", "g")}
        s_join = sem("s_join")
        for i in range(8):
            free[i] = None
        fork(None, lambda: path(sparse, "f"), lambda: path(dense, "g"), False)
        rel.n = rel0 + 6 * NEXP
        for q in queues:
            q.sem, q.n = after[q], 0
            q.wait((s_join, 3), (rel.sem, rel.n))
        for i in range(8):
            free[i] = None
        t_acc = (rel.sem, rel.n)

        Z2 = XS
        zt = []
        for k in range(8):
            zt.append(dve.do(lambda e, k=k: e.scalar_tensor_tensor(XS[:, k, 0:256], HN[:, k, 0:256], AL, accap(k), ALU.mult, ALU.add), t_acc))
        for i in range(4):
            free[i] = zt[-1]
        pool[:] = list(range(8))
        h2 = layernorm(XS, zt, HN, "ln2_g", "ln2_b", SIDE, zt[-1])
        ZO = CAT_[:, 0:2048].rearrange("p (k t) -> p k t", k=8)
        OUTB = XS[:, :, 0:256]
        pT = s2("p", 2, 256)
        wp = s2("w_ple", 2, 1024)
        fin = []
        for c in range(2):
            s, tk = nxt(A["w_ple_gate"][c])
            w = ring(s).rearrange("p (k n) -> p k n", k=8)

            def e_p(n, ps, tok, c=c):
                k = 4 * c + n
                a = act.do(lambda e: e.activation(ZO[:, k, :], ps, ACT.Sigmoid, bias=s2("b_ple")[:, k:k + 1]), tok, t_acc)
                b = take()
                tok2 = mm(banks[b][:, 0:256], [(wp[:, i, k * 128:k * 128 + 128], pT[:, i, :]) for i in range(2)], free[b])
                t = dve.do(lambda e: e.tensor_tensor(ZO[:, k, :], ZO[:, k, :], banks[b][:, 0:256], ALU.mult), a, tok2)
                free[b] = t
                fin.append(dve.do(lambda e: e.tensor_tensor(ZO[:, k, :], ZO[:, k, :], HN[:, k, 0:256], ALU.add), t))
                return a
            linear(w, [0, 128, 256, 384], HN, 256, h2, tk, e_p, True)
            sp.wait(fin[-1])
            sp.quiet(lambda e, c=c: e.dma_start(out[:, 4 * c:4 * c + 4, :], ZO[:, 4 * c:4 * c + 4, :]).then_inc(s_out, 16))
        sp.wait((s_out, 32))

        block = ctx.enter_context(nc.Block())

        @block.sync
        def _(e):
            sp.emit(e, sp.items)

        @block.scalar
        def _(e):
            act.run(e)

        @block.vector
        def _(e):
            dve.run(e)

        @block.tensor
        def _(e):
            pe.run(e)


def constants():
    c = {}
    c["ident"] = np.eye(128)
    pos = np.arange(256)
    row, col = (pos // 64).astype(np.float32), (pos % 64).astype(np.float32)
    inv = (np.float32(10000.0) ** (-np.arange(16, dtype=np.float32) / np.float32(16))).astype(np.float32)
    ar, ac = row[:, None] * inv[None], col[:, None] * inv[None]
    ang = np.concatenate([ar, ar, ac, ac], 1).astype(np.float64)
    c["ropec"] = np.tile(np.cos(ang).T, (2, 1))
    c["ropes"] = np.tile(np.sin(ang).T, (2, 1))
    rot = np.zeros((128, 128))
    for b in (0, 64):
        for i in range(16):
            rot[b + 16 + i, b + i] = -1
            rot[b + i, b + 16 + i] = 1
            rot[b + 48 + i, b + 32 + i] = -1
            rot[b + 32 + i, b + 48 + i] = 1
    c["rot"] = rot
    k = np.arange(64)
    a64 = 2 * np.pi * ((k[:, None] * k[None]) % 64) / 64
    z = np.zeros((64, 64))
    cb, sb_ = np.cos(a64) / 128, np.sin(a64) / 128
    c["bd"] = np.concatenate([np.block([[cb, z], [z, cb]]), np.block([[sb_, z], [z, sb_]])], 1)
    t = np.arange(256)
    a = 2 * np.pi * ((t[:, None] * t[None]) % 256) / 256
    c["dftc"] = np.cos(a).reshape(2, 128, 256).transpose(1, 0, 2)
    c["dfts"] = -np.sin(a).reshape(2, 128, 256).transpose(1, 0, 2)
    q = np.arange(256).reshape(2, 128)
    c["band"] = np.where(np.abs(q[:, :, None] - t[None, None]) <= 128, 0.0, -8e30).transpose(1, 0, 2)
    lev = np.zeros((128, 8, 128))
    for j in range(128):
        for i in range(j, 128):
            lev[j, 7 if i == j else int(i ^ j).bit_length() - 1, i] = 1
    c["lev"] = lev
    return c


def pack(table, width, vals):
    sm = np.zeros((128, width), np.float32)
    for n, (o, w) in table.items():
        v = np.asarray(vals[n])
        v = v.reshape(v.shape[0], -1)
        assert v.shape[1] == w, (n, v.shape, w)
        sm[:v.shape[0], o:o + w] = v
    return sm


def col(v):
    return v.reshape(-1, 128).T


def tiles8(w):
    n = w.shape[1] // 512
    return np.ascontiguousarray(w.reshape(8, 128, n, 512).transpose(2, 1, 0, 3)).reshape(n, 128, 4096)


def layout(inp):
    f = {k: np.asarray(v) for k, v in inp.items()}
    con = constants()
    (T1, W1), (T2, W2) = smalls()
    perm = np.concatenate([np.concatenate([np.arange(64 * j, 64 * j + 64), np.arange(64 * (j + 4), 64 * (j + 4) + 64)]) for j in range(4)])
    rows = np.concatenate([perm, np.arange(512, 1024)])
    v = dict(con)
    v["cc"] = np.stack([col(f["c"][0]), col(f["c_ctx"])], -1)
    A = {}
    for l in range(2):
        v[f"b_ada{l}"] = col(f["b_ada"][l])
        for n in ("g_pre_mix", "g_post_mix", "g_pre_ff", "g_post_ff"):
            v[f"{n}{l}"] = col(f[n][l])
        v[f"g_mix{l}"] = col(f["g_mix"][l][rows])
        sk = f["sink"][l].reshape(2, 4).T
        v[f"sink{l}"] = np.broadcast_to(np.repeat(sk, 2, axis=1).reshape(1, 16), (128, 16))
        v[f"b_sgu{l}"] = np.repeat(f["b_sgu"][l].reshape(2, 2, 128).transpose(1, 0, 2), 64, axis=0)
        v[f"g_sgu{l}"] = np.broadcast_to(f["g_sgu"][l].reshape(1, 256), (128, 256))
        v[f"w_sgu{l}"] = f["w_sgu"][l].transpose(2, 0, 1)
        A[f"w_ada{l}"] = tiles8(f["w_ada"][l])
        wi = f["w_in"][l]
        A[f"w_in{l}"] = tiles8(np.concatenate([wi[:, perm], wi[:, 512:]], 1))
        A[f"w_out{l}"] = tiles8(f["w_out"][l][rows])
        A[f"w_ff1_{l}"] = tiles8(f["w_ff1"][l])
        A[f"w_ff2_{l}"] = np.ascontiguousarray(f["w_ff2"][l].reshape(32, 128, 8, 128).transpose(2, 1, 0, 3)).reshape(8, 128, 4096)
    A["sm1"] = pack(T1, W1, v)
    xs = np.concatenate([f["x"][0], f["ctx"][0]], 0)
    A["xs"] = np.ascontiguousarray(xs.T.reshape(8, 128, 512).transpose(1, 0, 2)).reshape(128, 4096)
    A["ident"] = con["ident"].astype(np.float32)
    w2 = f["w_in_2"][0]
    A["w_in_2"] = tiles8(np.concatenate([w2[:, :5120], w2[:, 5136:]], 1))
    u = {"lev": con["lev"]}
    u["conv_w"] = f["conv_w_2"][0].reshape(4, 8, 128).transpose(2, 1, 0)
    for n, s in (("conv_b", "conv_b_2"), ("lru_b_r", "lru_b_r_2"), ("lru_b_i", "lru_b_i_2"), ("lam", "lru_lambda_2"),
                 ("gla_b", "gla_b_gate_2"), ("gla_g", "gla_norm_g_2"), ("ln1_g", "ln1_g_2"), ("ln1_b", "ln1_b_2"),
                 ("ln2_g", "ln2_g_2"), ("ln2_b", "ln2_b_2"), ("b_ple", "b_ple_gate_2")):
        u[n] = col(f[s][0])
    u["b_router"] = np.broadcast_to(f["b_router_2"][0][None], (128, 32))
    u["b_up"] = f["b_up_2"][0].reshape(32, 16, 128).transpose(2, 0, 1)
    u["w_router"] = f["w_router_2"][0].reshape(8, 128, 32).transpose(1, 0, 2)
    u["w_glr"] = w2[:, 5120:5136].reshape(8, 128, 16).transpose(1, 0, 2)
    u["w_gate"] = f["gla_w_gate_2"][0]
    u["lru_w_r"] = f["lru_w_r_2"][0].transpose(1, 0, 2)
    u["lru_w_i"] = f["lru_w_i_2"][0].transpose(1, 0, 2)
    u["p"] = f["p_2"][0, 0].T.reshape(2, 128, 256).transpose(1, 0, 2)
    u["w_ple"] = f["w_ple_2"][0].reshape(2, 128, 1024).transpose(1, 0, 2)
    A["sm2"] = pack(T2, W2, u)
    A["b_down"] = f["b_down_2"][0]
    A["b_up_rows"] = f["b_up_2"][0].reshape(32, 2, 4, 2, 128).transpose(0, 2, 3, 1, 4).reshape(32, 2048)
    i = np.arange(128)
    A["iota"] = np.broadcast_to(np.concatenate([i, i % 64])[None], (128, 256)).astype(np.float32)
    A["tri"] = (i[:, None] < i[None]).astype(np.float32)
    A["w_out_2"] = tiles8(f["w_out_2"][0])
    A["w_ple_gate"] = tiles8(f["w_ple_gate_2"][0])
    up = f["w_up_2"][0].reshape(32, 8, 128, 2, 4, 2, 128).transpose(0, 4, 2, 1, 5, 3, 6)
    A["w_up"] = np.ascontiguousarray(up).reshape(32, 4, 128, 4096)
    dn = f["w_down_2"][0].reshape(32, 8, 128, 2, 512).transpose(0, 3, 2, 1, 4)
    A["w_down"] = np.ascontiguousarray(dn).reshape(32, 2, 128, 4096)
    return A


def kernel(**inputs):
    import concourse.bacc as bacc
    from concourse.bass_utils import run_bass_kernel_spmd as run

    arrays = {k: np.ascontiguousarray(a) for k, a in layout(inputs).items()}
    nc = bacc.Bacc("TRN2", target_bir_lowering=False, num_devices=1)
    A = {n: nc.dram_tensor(f"in_{n}", a.shape, mybir.dt.from_np(a.dtype), kind="ExternalInput").ap() for n, a in arrays.items()}
    out = nc.dram_tensor("out_t", (128, 8, 256), F32, kind="ExternalOutput").ap()
    build(nc, A, out)
    r = run(nc, [{f"in_{n}": a for n, a in arrays.items()}], core_ids=[0])
    o = r.results[0]["out_t"]
    return np.ascontiguousarray(o.transpose(2, 1, 0).reshape(1, 256, 1024))
```

```python
import math
from contextlib import ExitStack

import numpy as np
import concourse.bass as bass
from concourse import mybir
from concourse.alu_op_type import AluOpType as ALU

F32 = mybir.dt.float32
ACT = mybir.ActivationFunctionType
AX = mybir.AxisListType

NEXP = 32
RING = 6
CW = 4096


def smalls(depth=2):
    one = [("cc", 16), ("ident", 128), ("ropec", 256), ("ropes", 256), ("rot", 128),
           ("bd", 256), ("dftc", 512), ("dfts", 512), ("band", 512)]
    for l in range(depth):
        one += [(f"b_ada{l}", 48), (f"g_pre_mix{l}", 8), (f"g_mix{l}", 8), (f"g_post_mix{l}", 8),
                (f"g_pre_ff{l}", 8), (f"g_post_ff{l}", 8), (f"sink{l}", 16), (f"b_sgu{l}", 256),
                (f"g_sgu{l}", 256), (f"w_sgu{l}", 512)]
    two = [("lev", 1024), ("conv_w", 32), ("conv_b", 8), ("lru_b_r", 8), ("lru_b_i", 8), ("lam", 8),
           ("gla_b", 4), ("gla_g", 2), ("ln1_g", 8), ("ln1_b", 8), ("ln2_g", 8), ("ln2_b", 8),
           ("b_ple", 8), ("b_router", 32), ("b_up", 512), ("w_router", 256), ("w_glr", 128),
           ("w_gate", 512), ("lru_w_r", 1024), ("lru_w_i", 1024), ("p", 512), ("w_ple", 2048)]
    out = []
    for fields in (one, two):
        at, table = 0, {}
        for n, w in fields:
            table[n] = (at, w)
            at += w
        out.append((table, at))
    return out


class Queue:

    def __init__(self, name, sem, depth=None):
        self.name = name
        self.sem, self.n, self.items, self.seen, self.depth = sem, 0, [], {}, depth

    def wait(self, *toks):
        for t in toks:
            if t is None:
                continue
            if isinstance(t, list):
                self.wait(*t)
                continue
            s, v = t
            if self.seen.get(s.name, 0) < v:
                self.seen[s.name] = v
                self.items.append(lambda e, s=s, v=v: e.wait_ge(s, v))

    def do(self, fn, *toks):
        self.wait(*toks)
        if self.depth and self.n >= self.depth:
            self.wait((self.sem, self.n + 1 - self.depth))
        self.n += 1
        sem = self.sem
        self.items.append(lambda e: fn(e).then_inc(sem, 1))
        return (self.sem, self.n)

    def quiet(self, fn, *toks):
        self.wait(*toks)
        self.items.append(fn)

    def run(self, e):
        self.regs = [e.alloc_register(f"{self.name}_f{i}") for i in range(NEXP)]
        self.over = e.alloc_register(f"{self.name}_over")
        self.emit(e, self.items)

    def emit(self, e, items):
        for i in items:
            if isinstance(i, tuple):
                reg, zero, other = i
                with e.If_cmp(self.over if reg is None else self.regs[reg], 0, "IS_EQ"):
                    self.emit(e, zero)
                with e.Else():
                    self.emit(e, other)
            else:
                i(e)


class Counter:
    def __init__(self, sem):
        self.sem, self.n = sem, 0


def build(nc, A, out):
    (T1, W1), (T2, W2) = smalls()
    ctx = ExitStack()
    with ctx:
        def sb(name, w, p=128):
            return ctx.enter_context(nc.sbuf_tensor(name, [p, w], F32))

        def sem(name):
            return ctx.enter_context(nc.semaphore(name))

        SM1 = sb("SM1", max(W1, W2 + 0))
        XS_ = sb("XS", 4096)
        HN_ = sb("HN", 4096)
        CAT_ = sb("CAT", 4096)
        BIG = sb("BIG", 16384)
        RG = sb("RG", 3 * CW)
        STAT = sb("STAT", 512 * 3)
        MISC = sb("MISC", 1100)
        HOLD = sb("HOLD", 1024)
        SILK = SM1[:, W1:W1 + 256]
        MODT = sb("MODT", 96 * 2 + 16 * 6)
        BD = sb("BDN", 1024, 32)
        PS = ctx.enter_context(nc.psum_tensor("PS", [128, 4096], F32))
        banks = [PS[:, 512 * i:512 * i + 512] for i in range(8)]

        pe, act, dve = Queue("pe", sem("s_pe")), Queue("act", sem("s_act"), 1), Queue("dve", sem("s_dve"), 1)
        sp = Queue("sp", sem("s_sp"))
        rel = Counter(sem("s_rel"))
        s_slot = [sem(f"s_slot{i}") for i in range(RING)]
        s_sm = sem("s_sm")
        s_sm2 = sem("s_sm2")
        s_in = sem("s_in")
        s_sm3 = sem("s_sm3")
        s_cc = sem("s_cc")
        FLAG = ctx.enter_context(nc.sbuf_tensor("FLAG", [1, 40], mybir.dt.int32))
        s_out = sem("s_out")

        def view(t, off, *dims):
            w = int(np.prod(dims))
            a = t[:, off:off + w]
            if len(dims) == 2:
                a = a.rearrange("p (a b) -> p a b", a=dims[0])
            elif len(dims) == 3:
                a = a.rearrange("p (a b c) -> p a b c", a=dims[0], b=dims[1])
            return a

        def s1(n, *dims):
            o, w = T1[n]
            return view(SM1, o, *(dims or (w,)))

        def s2(n, *dims):
            o, w = T2[n]
            return view(SM1, o, *(dims or (w,)))

        def mm(bank_ap, pairs, *waits, start=True, stop=True, last=None, check=True, each=()):
            n = len(pairs)
            tok = None
            pe.wait(*waits)
            for i, (l, r) in enumerate(pairs):
                st, sp_ = start and i == 0, stop and i == n - 1
                pe.wait(each[i] if each else None)

                def f(e, l=l, r=r, st=st, sp_=sp_):
                    return e.matmul(bank_ap, l, r, start=st, stop=sp_, skip_group_check=not check)
                if i < n - 1:
                    pe.quiet(f)
                elif last is not None:
                    last.n += 1
                    pe.quiet(lambda e, f=f: f(e).then_inc(last.sem, 1))
                    tok = (last.sem, last.n)
                else:
                    tok = pe.do(f)
            return tok

        free = [None] * 8
        turn = [0]
        pool = list(range(8))

        opened = set()

        def take():
            while True:
                b = pool[turn[0] % len(pool)]
                turn[0] += 1
                if b not in opened or free[b] is not wait_of[b]:
                    opened.add(b)
                    wait_of[b] = free[b] = ("open", free[b])
                    return b

        def takes(n):
            while True:
                b = pool[turn[0] % len(pool)]
                if b % n == 0 and all(x not in opened or free[x] is not wait_of[x] for x in range(b, b + n)):
                    return [take() for _ in range(n)]
                turn[0] += 1

        wait_of = [None] * 8

        def fr(b):
            return free[b][1] if isinstance(free[b], tuple) and free[b][0] == "open" else free[b]

        slot_cnt = [0] * RING
        slot_rel = [(0, None)] * 3 + [(1 << 30, None)] * 3
        held = set()

        def ring(s):
            if s < 3:
                return RG[:, s * CW:(s + 1) * CW]
            return BIG[:, (s - 3) * CW:(s - 2) * CW]

        def load_chunk(src, wide=False, extra=(), at=None):
            s = min((x for x in range(RING if wide else 3) if x not in held), key=lambda x: slot_rel[x][0])
            n, tok = slot_rel[s]
            if n == 1 << 30:
                sp.wait(*extra)
            sp.wait(tok)
            slot_cnt[s] += 16
            sp.quiet(lambda e: e.dma_start(ring(s), src).then_inc(s_slot[s], 16))
            if at is None:
                held.add(s)
            else:
                slot_rel[s] = (at, (rel.sem, at))
            return s, (s_slot[s], slot_cnt[s])

        class Last:

            def __init__(self, tk):
                self.s = [x.name for x in s_slot].index(tk[0].name)
                self.sem = rel.sem

            @property
            def n(self):
                return rel.n

            @n.setter
            def n(self, v):
                rel.n = v
                held.discard(self.s)
                slot_rel[self.s] = (v, (rel.sem, v))

        sp.quiet(lambda e: e.dma_start(SM1[:, 0:144], A["sm1"][:, 0:144]).then_inc(s_cc, 16))
        act.quiet(lambda e: e.dma_start(XS_[:, :], A["xs"]).then_inc(s_in, 16))
        t_sm, t_in = (s_sm, 16), (s_in, 16)

        XS = XS_[:, :].rearrange("p (k t) -> p k t", k=8)
        HN = HN_[:, :].rearrange("p (k t) -> p k t", k=8)
        CAT = CAT_[:, :].rearrange("p (k t) -> p k t", k=8)
        ones = MISC[:, 0:128]
        epsb = MISC[:, 128:129]
        o512, o256 = MISC[:, 130:258], MISC[:, 258:386]
        onet = MISC[:, 386:642]
        MX, DN, ES, NM, RD = (MISC[:, 642 + 4 * i:646 + 4 * i] for i in range(5))
        SV = MISC[:, 662:1100]
        t_c = []
        t_c.append(dve.do(lambda e: e.memset(ones, 1.0 / 1024)))
        t_c.append(dve.do(lambda e: e.memset(o512, 1.0 / 512)))
        t_c.append(dve.do(lambda e: e.memset(o256, 1.0 / 256)))
        t_c.append(dve.do(lambda e: e.memset(onet, 1.0)))
        t_const = t_c[-1]

        SILP = HOLD[:, 0:256].rearrange("p (k s) -> p k s", s=32)
        ROW = view(SM1, W1 + 256, 2, 512)
        t = dve.do(lambda e: e.memset(HOLD[:, 0:256], 0.0))
        t_sil = act.do(lambda e: e.activation(SILP[:, :, 0:2], s1("cc", 8, 2), ACT.Silu), (s_cc, 16), t)
        t_sil = act.do(lambda e: e.activation(SILK, HOLD[:, 0:256], ACT.Copy), t_sil)
        row_free = [None, None]
        n_ada = [0]

        def mod(l):
            return MODT[:, 96 * l:96 * l + 96].rearrange("p (j s) -> p j s", s=2)

        def ada(l, c):
            s, tk = load_chunk(A[f"w_ada{l}"][c])
            w = ring(s).rearrange("p (k n) -> p k n", k=8)
            b = take()
            pe.wait(t_sil, tk, fr(b))
            for k in range(8):
                g = k % 4
                f = (lambda e, k=k, g=g, b=b, w=w: e.matmul(banks[b][32 * g:32 * g + 32, :],
                                                            SILK[:, 32 * k:32 * k + 32],
                                                            w[:, k, :], start=k < 4, stop=k >= 4))
                if k < 7:
                    pe.quiet(f)
                else:
                    Last(tk).n += 1
                    pe.quiet(lambda e, f=f: f(e).then_inc(rel.sem, 1))
            q = n_ada[0] % 2
            n_ada[0] += 1
            t = act.do(lambda e: e.activation(ROW[:, q, :], banks[b][:, :], ACT.Copy), (rel.sem, rel.n), row_free[q])
            free[b] = t
            yield 3
            b2 = take()
            pe.wait(t, fr(b2))
            for j in range(4):
                f = lambda e, j=j: e.transpose(banks[b2][:, 128 * j:128 * j + 128], ROW[:, q, 128 * j:128 * j + 128], s1("ident"))
                tok = pe.do(f) if j == 3 else pe.quiet(f)
            row_free[q] = tok
            yield 0
            dst = mod(l)[:, 4 * c:4 * c + 4, :]
            bias = s1(f"b_ada{l}")[:, 4 * c:4 * c + 4].rearrange("p (j o) -> p j o", o=1).broadcast_to([128, 4, 2])
            part = banks[b2][:, :].rearrange("p (j g s) -> p j g s", j=4, g=4)
            sums = MODT[:, 192:200].rearrange("p (j s) -> p j s", s=2)
            dve.wait(t_sm)
            t = dve.do(lambda e: e.tensor_reduce(sums, part[:, :, :, 0:2].rearrange("p j g s -> p j s g"), AX.X, ALU.add), tok)
            free[b2] = t
            return dve.do(lambda e: e.tensor_tensor(dst, sums, bias, ALU.add), t)

        def coef(l, i):
            o = W1 + 1280 + 64 * l + 16 * i
            return SM1[:, o:o + 16].rearrange("p (k s) -> p k s", s=2)

        def gain(l, i, part, g, plus, tok):
            gv = s1(f"{g}{l}").rearrange("p (k o) -> p k o", o=1).broadcast_to([128, 8, 2])
            m = mod(l)[:, 8 * part:8 * part + 8, :]
            return dve.do(lambda e: e.scalar_tensor_tensor(coef(l, i), m, plus, gv, ALU.add, ALU.mult), tok)

        def rstd(bank, T, slot, tok, eps, s=0):
            r = STAT[:, 768 * s + 256 * slot:768 * s + 256 * slot + T]
            me = HOLD[:, 256 * s:256 * s + T]
            tm = HOLD[:, 512 + 256 * s:512 + 256 * s + T]
            ps = banks[bank][:, 0:T]
            a = dve.do(lambda e: e.tensor_scalar(me, ps, eps, None, ALU.add), tok)
            free[bank] = a
            b = act.do(lambda e: e.activation(r, me, ACT.Sqrt), a)
            yield 1
            c = dve.do(lambda e: e.reciprocal(r, r), b)
            d = dve.do(lambda e: e.tensor_tensor(tm, r, r, ALU.mult), c)
            d = dve.do(lambda e: e.scalar_tensor_tensor(tm, tm, -0.5, me, ALU.mult, ALU.mult), d)
            d = dve.do(lambda e: e.scalar_tensor_tensor(r, tm, 1.5, r, ALU.add, ALU.mult), d)
            return r, d

        def meansq(src, dst, ks, T, w, toks, dst_free=None):
            b = take()
            ts = []
            for i, k in enumerate(ks):
                ts.append(act.do(lambda e, k=k: e.activation(dst[:, k, 0:T], src[:, k, 0:T], ACT.Square),
                                 toks[i], dst_free))
            for i, k in enumerate(ks):
                if i % 4 == 0:
                    yield 2
                tok = mm(banks[b][:, 0:T], [(w, dst[:, k, 0:T])], ts[i], fr(b), t_const,
                         start=i == 0, stop=i == len(ks) - 1)
            return b, tok

        class Mean:

            def __init__(self, src, dst, n, w):
                self.src, self.dst, self.n, self.w, self.i, self.due, self.b = src, dst, n, w, 0, None, None

            def add(self, k, tok):
                t = act.do(lambda e: e.activation(self.dst[:, k, :], self.src[:, k, :], ACT.Square), tok)
                self.flush()
                self.due = (k, t)

            def flush(self):
                if self.due is None:
                    return
                if self.b is None:
                    self.b = take()
                k, t = self.due
                self.tok = mm(banks[self.b][:, 0:256], [(self.w, self.dst[:, k, :])], t, fr(self.b), t_const,
                              start=self.i == 0, stop=self.i == self.n - 1)
                self.i += 1
                self.due = None

            def close(self):
                self.flush()
                return self.b, self.tok

        def finish(g):
            while True:
                try:
                    next(g)
                except StopIteration as e:
                    return e.value

        def own(t, s):
            return t[:, :, 256 * s:256 * s + 256]

        def prenorm(l, s, toks, ca, part_sh, tok_c, hn_free, eps=1e-6):
            X, N = own(XS, s), own(HN, s)
            b, tk = yield from meansq(X, N, range(8), 256, ones, toks, hn_free)
            r, tr = yield from rstd(b, 256, 0, tk, eps, s)
            m = mod(l)
            outt = []
            for k in range(8):
                a = dve.do(lambda e, k=k: e.scalar_tensor_tensor(
                    N[:, k, :], X[:, k, :], coef(l, ca)[:, k, s:s + 1], r, ALU.mult, ALU.mult), tr, tk, tok_c)
                outt.append(act.do(lambda e, k=k: e.activation(
                    N[:, k, :], N[:, k, :], ACT.Identity, bias=m[:, 8 * part_sh + k, s:s + 1]), a, tok_c))
            return outt

        def post(l, s, Y, mean, cg, tok_c):
            X = own(XS, s)
            b, tk = mean.close()
            r, tr = yield from rstd(b, 256, 0, tk, 1e-6, s)
            outt = []
            for k in range(8):
                a = dve.do(lambda e, k=k: e.scalar_tensor_tensor(
                    Y[:, k, :], Y[:, k, :], coef(l, cg)[:, k, s:s + 1], r, ALU.mult, ALU.mult), tr, tok_c)
                outt.append(dve.do(lambda e, k=k: e.tensor_tensor(X[:, k, :], X[:, k, :], Y[:, k, :], ALU.add), a))
            return outt, tk

        FFH = view(BIG, 0, 32, 256)
        Q = view(BIG, 8192, 4, 256)
        KZ = view(BIG, 9216, 2, 512)
        V = view(BIG, 10240, 4, 128)
        PT = view(BIG, 10752, 2, 2, 512)
        YM = view(BIG, 10752, 8, 256)
        U = view(BIG, 12800, 2, 256)
        GV = view(BIG, 13312, 2, 256)
        FT = view(BIG, 13824, 2, 256)
        GF = view(BIG, 14336, 2, 2, 256)
        P = view(BIG, 12800, 2, 2, 512)
        TMPA = view(BIG, 15360, 256)
        KR = view(BIG, 15616, 256)
        TMPB = view(BIG, 15872, 512)

        def linear(w, cols, src, T, toks, tk, emit, last_rel):
            ks = list(toks) if isinstance(toks, dict) else list(range(8))
            toks = list(toks.values()) if isinstance(toks, dict) else toks
            tiled = isinstance(toks, list) and len(toks) == 8
            for n, c in enumerate(cols):
                b = take()
                tok = mm(banks[b][:, 0:T], [(w[:, k, c:c + 128], src[:, k, 0:T]) for k in ks],
                         tk, fr(b), None if tiled else toks, last=Last(tk) if last_rel and n == len(cols) - 1 else None,
                         each=toks if tiled else ())
                free[b] = emit(n, banks[b][:, 0:T], tok)

        def linears(*a):
            w, cols, src, T, toks, tk, emit, last_rel = a
            for n, c in enumerate(cols):
                linear(w, [c], src, T, toks, tk, lambda _, ps, tok, n=n: emit(n, ps, tok), last_rel and n == len(cols) - 1)
                yield 3.5

        def copy_to(dst, ps, tok, *w):
            return act.do(lambda e: e.activation(dst, ps, ACT.Copy), tok, *w)

        def wchunk(name, c, k=8):
            s, tk = load_chunk(A[name][c])
            return ring(s).rearrange("p (k n) -> p k n", k=k), tk

        ada_t = {}
        mixed = {"ym": None, "p": [None, None], "pt": [None, None], "q": None, "k": None}
        kv = {}
        xt = {0: [t_in] * 8, 1: [t_in] * 8}
        t = dve.do(lambda e: e.memset(KZ[64:128, 0, :], 0.0))
        t_kz = dve.do(lambda e: e.memset(KZ[0:64, 1, :], 0.0))

        def keys_values(l, s, w, tk, hn, rel_last):
            N = own(HN, s)
            ks = slice(256 * s, 256 * s + 256)

            def e_k(n, ps, tok):
                if s == 0:
                    return copy_to(KR, ps, tok, mixed["k"])
                copy_to(KZ[0:64, 0, ks], ps[0:64, :], tok, mixed["kv"], t_kz)
                return copy_to(KZ[64:128, 1, ks], ps[64:128, :], tok)
            mixed.setdefault("kv", None)
            linear(w, [0], N, 256, hn, tk, e_k, False)
            tkk = (act.sem, act.n)
            b = take()
            for tt in range(2):
                tok = mm(banks[b][:, tt * 128:tt * 128 + 128],
                         [(N[:, k, tt * 128:tt * 128 + 128], w[:, k, 128:256]) for k in range(8)], fr(b),
                         last=Last(tk) if rel_last and tt else None)
            tv = copy_to(V[:, 2 * s:2 * s + 2, :].rearrange("p a b -> p (a b)"), banks[b][:, 0:256], tok, mixed["kv"])
            free[b] = tv
            yield 7
            if s == 0:
                b = take()
                tok = mm(banks[b][:, 0:256], [(s1("rot"), KR)], tkk, fr(b))
                t = dve.do(lambda e: e.tensor_tensor(TMPA, banks[b][:, 0:256], s1("ropes"), ALU.mult), tok)
                free[b] = t
                t2 = dve.do(lambda e: e.tensor_tensor(KR, KR, s1("ropec"), ALU.mult), tok, t)
                for hf in range(2):
                    pr = slice(64 * hf, 64 * hf + 64)
                    tkk = dve.do(lambda e, pr=pr, hf=hf: e.tensor_tensor(KZ[pr, hf, ks], KR[pr, :], TMPA[pr, :], ALU.add),
                                 t2, mixed["kv"], t_kz)
                mixed["k"] = tkk
                yield 2
            kv[l, s] = (tkk, tv)

        done = set()

        def until(*what):
            while what not in done:
                yield 1

        def mix(l, s):
            while (l, 3) not in ada_t:
                yield 1
            N, C = own(HN, s), own(CAT, s)
            tg_ = gain(l, 0, 1, "g_pre_mix", 1.0, ada_t[l, 3]) if (l, 0) not in gains else gains[l, 0]
            gains[l, 0] = tg_
            hn = yield from prenorm(l, s, xt[s], 0, 0, tg_, None)
            yield 12
            if (l, s) == (0, 0):
                yield from until("attention", 0, 1)
            w, tk = wchunk(f"w_in{l}", 0)
            tq = []

            def e_q(n, ps, tok):
                t = copy_to(Q[:, n, :], ps, tok, mixed["q"])
                tq.append(t)
                return t
            yield from linears(w, [0, 128, 256, 384], N, 256, hn, tk, e_q, True)
            w, tk = wchunk(f"w_in{l}", 1)
            yield from keys_values(l, s, w, tk, hn, False)
            tu = []

            def e_u(n, ps, tok):
                t = act.do(lambda e: e.activation(U[:, n, :], ps, ACT.Gelu_apprx_tanh), tok, mixed["p"])
                tu.append(t)
                return t
            yield from linears(w, [256, 384], N, 256, hn, tk, e_u, True)
            w, tk = wchunk(f"w_in{l}", 2)
            tgv = []
            for tt in range(2):
                b = take()
                tok = mm(banks[b][:, 0:256],
                         [(N[:, k, tt * 128:tt * 128 + 128], w[:, k, 0:256]) for k in range(8)], tk, fr(b))
                t = act.do(lambda e, tt=tt, b=b: e.activation(GV[:, tt, :], banks[b][:, 0:256],
                                                             ACT.Gelu_apprx_tanh), tok, mixed["p"])
                free[b] = t
                tgv.append(t)
                yield 3.5
            tf = []

            def e_f(n, ps, tok):
                t = copy_to(FT[:, n, :], ps, tok, mixed["p"])
                tf.append(t)
                return t
            yield from linears(w, [256, 384], N, 256, hn, tk, e_f, True)
            if s == 0:
                for n in range(4):
                    b = take()
                    tok = mm(banks[b][:, 0:256], [(s1("rot"), Q[:, n, :])], tq[n], fr(b))
                    t = dve.do(lambda e, b=b: e.tensor_tensor(TMPA, banks[b][:, 0:256], s1("ropes"), ALU.mult), tok)
                    free[b] = t
                    t2 = dve.do(lambda e, n=n: e.tensor_tensor(Q[:, n, :], Q[:, n, :], s1("ropec"), ALU.mult), tok)
                    tq[n] = dve.do(lambda e, n=n: e.tensor_tensor(Q[:, n, :], Q[:, n, :], TMPA, ALU.add), t, t2)
                    yield 1.2
            gvf = GV.rearrange("p a (h d) -> p (a h) d", d=64)
            tA = TMPB.rearrange("p (a d) -> p a d", d=64)
            t = dve.do(lambda e: e.tensor_tensor(tA, gvf, gvf, ALU.mult), *tgv)
            t = dve.do(lambda e: e.tensor_reduce(SV[:, 0:8], tA, AX.X, ALU.add), t)
            t = dve.do(lambda e: e.tensor_scalar(SV[:, 16:24], SV[:, 0:8], 1.0 / 64, 1e-6, ALU.mult, ALU.add), t)
            t = act.do(lambda e: e.activation(SV[:, 32:40], SV[:, 16:24], ACT.Sqrt), t)
            t = dve.do(lambda e: e.reciprocal(SV[:, 48:56], SV[:, 32:40]), t)
            rb = SV[:, 48:56].rearrange("p (a o) -> p a o", o=1).broadcast_to([128, 8, 64])
            t = dve.do(lambda e: e.tensor_tensor(gvf, gvf, rb, ALU.mult), t)
            gb = s1(f"g_sgu{l}").rearrange("p (o c) -> p o c", o=1).broadcast_to([128, 2, 256])
            t_vh = dve.do(lambda e: e.tensor_tensor(GV, GV, gb, ALU.mult), t)
            wsT = s1(f"w_sgu{l}", 4, 128)
            bsg = s1(f"b_sgu{l}", 2, 128)
            yield 3
            ct = [None] * 8
            bdm = s1("bd")
            tg = {}
            for tt in range(2):
                b = take()
                for j in range(2):
                    tok = mm(banks[b][:, 256 * j:256 * j + 256], [(FT[:, j, tt * 128:tt * 128 + 128], bdm)], tf[j], fr(b))
                t = act.do(lambda e, tt=tt, b=b: e.activation(GF[:, tt].rearrange("p a b -> p (a b)"), banks[b][:, :], ACT.Copy), tok, mixed["p"])
                free[b] = t
                tg[tt] = t
            yield 2
            dc, ds = s1("dftc", 2, 256), s1("dfts", 2, 256)
            for j in range(2):
                b = take()
                pairs = []
                for ht in range(2):
                    pairs += [(GF[:, ht, j, 0:128], dc[:, ht, :]), (GF[:, ht, j, 128:256], ds[:, ht, :])]
                tok = mm(banks[b][:, 0:256], pairs, tg[0], tg[1], fr(b))
                t = act.do(lambda e, j=j, b=b: e.activation(C[:, 6 + j, :], banks[b][:, 0:256], ACT.Copy), tok)
                free[b] = t
                ct[6 + j] = t
                yield 2
            t_gf = tok
            for j in range(2):
                b = take()
                for tt in range(2):
                    for hf in range(2):
                        h = 2 * j + hf
                        tok = mm(banks[b][64 * hf:64 * hf + 64, tt * 128:tt * 128 + 128],
                                 [(GV[:, tt, h * 64:h * 64 + 64], wsT[:, h, :])], t_vh, fr(b))
                psv = banks[b][:, 0:256].rearrange("p (a t) -> p a t", t=128)
                bb = bsg[:, j:j + 1, :].broadcast_to([128, 2, 128])
                cv = C[:, 4 + j, :].rearrange("p (a t) -> p a t", t=128)
                t = dve.do(lambda e, psv=psv, bb=bb, cv=cv: e.tensor_tensor(cv, psv, bb, ALU.add), tok)
                free[b] = t
                ct[4 + j] = dve.do(lambda e, j=j: e.tensor_tensor(C[:, 4 + j, :], C[:, 4 + j, :], U[:, j, :], ALU.mult), t, tu[j])
                yield 1.5
            t_ugf = [t_gf, tok, ct[5]]
            if (l, s) == (0, 0):
                yield from until("mix", 0, 1)
            while s == 0 and (l, 1) not in kv:
                yield 1
            sinks = s1(f"sink{l}", 4, 4)
            band = s1("band", 2, 256)
            kvt = [kv[l, 1], kv[l, 0]] if s == 0 else [kv[l, 1]]
            wd = 512 if s == 0 else 256
            nk = wd // 128
            units = [(j, qb) for j in range(4) for qb in range(2)]
            ptr, pr_ = [None, None], [t_ugf, t_ugf]

            def scores(j, qb):
                bb = takes(2)
                for hf in range(2):
                    tok = mm(banks[bb[hf]][:, 0:wd],
                             [(Q[:, j, qb * 128:qb * 128 + 128], KZ[:, hf, 512 - wd:512])],
                             tq[j], kvt[0][0], kvt[-1][0], fr(bb[hf]))
                return bb, tok

            def small(i):
                par = i % 2
                return [x_[:, 2 * par:2 * par + 2] for x_ in (MX, DN, ES, NM, RD)]

            def soft_a(i, j, qb, bb, tok):
                par = i % 2
                mx, dn, es, nm, rd = small(i)
                both = PS[:, 512 * bb[0]:512 * bb[0] + 1024].rearrange("p (h c) -> p h c", h=2)
                if s == 0:
                    o = 128 - 128 * qb
                    mk = band[:, qb:qb + 1, o:o + 128].broadcast_to([128, 2, 128])
                    tok = dve.do(lambda e: e.tensor_tensor(both[:, :, o:o + 128], both[:, :, o:o + 128], mk, ALU.add), tok)
                t = dve.do(lambda e: e.tensor_reduce(mx, both[:, :, 0:wd], AX.X, ALU.max), tok)
                sk = sinks[:, j, 0:4:2]
                t = dve.do(lambda e: e.scalar_tensor_tensor(nm, mx, 0.125, sk, ALU.mult, ALU.max), t)
                tn = dve.do(lambda e: e.tensor_scalar(mx, nm, -1.0, None, ALU.mult), t)
                td = dve.do(lambda e: e.tensor_tensor(nm, sk, mx, ALU.add), tn)
                ex = []
                for hf in range(2):
                    t = act.do(lambda e, hf=hf: e.activation(P[:, par, hf, 0:wd], both[:, hf, 0:wd], ACT.Exp,
                                                            bias=mx[:, hf:hf + 1], scale=0.125,
                                                            accum_out=dn[:, hf:hf + 1]), tn, pr_[par])
                    free[bb[hf]] = t
                    ex.append(t)
                ex.append(act.do(lambda e: e.activation(es, nm, ACT.Exp), td))
                return ex

            def soft_b(i, ex):
                par = i % 2
                mx, dn, es, nm, rd = small(i)
                t = dve.do(lambda e: e.tensor_tensor(rd, dn, es, ALU.add), *ex)
                t = dve.do(lambda e: e.reciprocal(rd, rd), t)
                return [dve.do(lambda e, hf=hf: e.tensor_scalar(P[:, par, hf, 0:wd], P[:, par, hf, 0:wd], rd[:, hf:hf + 1], None, ALU.mult), t)
                        for hf in range(2)]

            def turned(i, pn):
                par = i % 2
                cp = []
                for hf in range(2):
                    b = take()
                    pe.wait(pn[hf], fr(b))
                    for kt in range(nk):
                        f = lambda e, b=b, kt=kt, hf=hf: e.transpose(banks[b][:, kt * 128:kt * 128 + 128],
                                                                    P[:, par, hf, kt * 128:kt * 128 + 128], s1("ident"))
                        tok = pe.do(f) if kt == nk - 1 else pe.quiet(f)
                    t = act.do(lambda e, b=b, hf=hf: e.activation(PT[:, par, hf, 0:wd], banks[b][:, 0:wd], ACT.Copy), tok, ptr[par], mixed["pt"])
                    free[b] = t
                    cp.append(t)
                pr_[par] = tok
                return cp

            def values(i, j, qb, cp):
                par = i % 2
                b = take()
                pe.wait(fr(b), *cp, *[x_[1] for x_ in kvt])
                for kt in range(nk):
                    for hf in range(2):
                        vt = kt if s == 0 else 2 + kt
                        f = lambda e, kt=kt, hf=hf, vt=vt: e.matmul(
                            banks[b][64 * hf:64 * hf + 64, 0:128], V[:, vt, 64 * hf:64 * hf + 64],
                            PT[:, par, hf, kt * 128:kt * 128 + 128], start=kt == 0, stop=kt == nk - 1)
                        tok = pe.do(f) if kt == nk - 1 and hf else pe.quiet(f)
                ptr[par] = tok
                t = act.do(lambda e: e.activation(C[:, j, qb * 128:qb * 128 + 128], banks[b][:, 0:128], ACT.Copy), tok)
                free[b] = t
                ct[j] = t

            n = len(units)
            exs, cps = {}, {}
            sc = {0: scores(*units[0])}
            yield 1.5
            for i in range(n + 2):
                if i + 1 < n:
                    sc[i + 1] = scores(*units[i + 1])
                if i < n:
                    exs[i] = soft_a(i, *units[i], *sc[i])
                if 0 <= i - 1 < n:
                    pn = soft_b(i - 1, exs[i - 1])
                yield 1.5
                if 0 <= i - 1 < n:
                    cps[i - 1] = turned(i - 1, pn)
                if 0 <= i - 2 < n:
                    values(i - 2, *units[i - 2], cps[i - 2])
                yield 4
            mixed["p"] = [pr_[0], pr_[1]]
            mixed["q"] = (pe.sem, pe.n)
            mixed["kv"] = (pe.sem, pe.n)
            done.add(("attention", l, s))
            yield 2
            gm = s1(f"g_mix{l}")
            mt = {}
            for i, (ks, w1_) in enumerate((((6, 7), o256), ((4, 5), o256), ((0, 1, 2, 3), o512))):
                b, tk_ = yield from meansq(C, N, ks, 256, w1_, [ct[k] for k in ks])
                r, tr = yield from rstd(b, 256, i, tk_, 1e-6, s)
                for k in ks:
                    mt[k] = dve.do(lambda e, k=k, r=r: e.scalar_tensor_tensor(
                        C[:, k, :], C[:, k, :], gm[:, k:k + 1], r, ALU.mult, ALU.mult), tr)
                yield 4
            mean = Mean(YM, N, 8, ones)
            for c in range(2):
                w, tk = wchunk(f"w_out{l}", c)

                def e_y(n, ps, tok, c=c):
                    t = copy_to(YM[:, 4 * c + n, :], ps, tok)
                    mean.add(4 * c + n, t)
                    return t
                yield from linears(w, [0, 128, 256, 384], C, 256, mt, tk, e_y, True)
            mixed["cat"] = (rel.sem, rel.n)
            while (l, 11) not in ada_t:
                yield 1
            for i, part, g_, plus in ((1, 2, "g_post_mix", 0.0), (2, 4, "g_pre_ff", 1.0), (3, 5, "g_post_ff", 0.0)):
                if (l, i) not in gains:
                    gains[l, i] = gain(l, i, part, g_, plus, ada_t[l, 11])
            xt[s], _ = yield from post(l, s, YM, mean, 1, gains[l, 3])
            mixed["pt"] = xt[s][-1]
            done.add(("mix", l, s))
            yield 10

        gains = {}
        ffh_free = [None]

        def ff(l, s):
            N, C = own(HN, s), own(CAT, s)
            hn = yield from prenorm(l, s, xt[s], 2, 3, gains[l, 3], None)
            yield 10
            if (l, s) == (0, 0):
                yield from until("ff2", 0, 1)
            h_t = []
            for c in range(8):
                w, tk = wchunk(f"w_ff1_{l}", c)

                def e_h(n, ps, tok, c=c):
                    k = 4 * c + n
                    a = act.do(lambda e: e.activation(FFH[:, k, :], ps, ACT.Relu), tok, ffh_free[0])
                    h_t.append(act.do(lambda e: e.activation(FFH[:, k, :], FFH[:, k, :], ACT.Square), a))
                    return a
                yield from linears(w, [0, 128, 256, 384], N, 256, hn, tk, e_h, True)
            mean = Mean(C, N, 8, ones)
            for c in range(8):
                w, tk = wchunk(f"w_ff2_{l}", c, 32)
                b = take()
                tok = mm(banks[b][:, 0:256], [(w[:, k, :], FFH[:, k, :]) for k in range(32)], tk, fr(b), last=Last(tk), each=h_t)
                t = copy_to(C[:, c, :], banks[b][:, 0:256], tok, (rel.sem, rel.n))
                free[b] = t
                mean.add(c, t)
                if c == 7:
                    ffh_free[0] = (rel.sem, rel.n)
                    done.add(("ff2", l, s))
                yield 13.8
            xt[s], _ = yield from post(l, s, C, mean, 3, gains[l, 3])
            yield 10

        def kv1():
            yield from until("attention", 0, 0)
            while (1, 3) not in ada_t:
                yield 1
            if (1, 0) not in gains:
                gains[1, 0] = gain(1, 0, 1, "g_pre_mix", 1.0, ada_t[1, 3])
            hn = yield from prenorm(1, 1, xt[1], 0, 0, gains[1, 0], None)
            yield 10
            w, tk = wchunk("w_in1", 1)
            yield from keys_values(1, 1, w, tk, hn, True)

        def adas(l, cs, dt=6):
            for c in cs:
                ada_t[l, c] = yield from ada(l, c)
                yield dt

        def chain(*gs):
            for g in gs:
                yield from g

        def together(*gs):
            clocks = [[0.0, i, g] for i, g in enumerate(gs)]
            while clocks:
                clocks.sort(key=lambda c: c[:2])
                try:
                    clocks[0][0] += next(clocks[0][2])
                except StopIteration:
                    clocks.pop(0)

        def after(g, wait):
            yield wait
            yield from g

        ada_t[0, 0] = finish(ada(0, 0))
        sp.quiet(lambda e: e.dma_start(SM1[:, 144:W1], A["sm1"][:, 144:W1]).then_inc(s_sm, 16))
        for q in (pe, act, dve):
            q.wait((s_cc, 16))
        together(adas(0, range(1, 4), 0))
        pe.wait(t_sm)
        act.wait(t_sm)
        together(chain(mix(0, 1), ff(0, 1), until("ff2", 0, 0), kv1()),
                 chain(after(mix(0, 0), 5), ff(0, 0), mix(1, 0), ff(1, 0)),
                 chain(adas(0, range(4, 12), 12), until("mix", 0, 1), adas(1, range(0, 7), 17),
                       until("ff2", 0, 0), adas(1, range(7, 12), 20)))
        x_toks = xt[0]
        t_big_free = [(rel.sem, rel.n), (pe.sem, pe.n), x_toks]

        act.wait(*x_toks)
        act.wait((pe.sem, pe.n), (act.sem, act.n), (dve.sem, dve.n))
        act.quiet(lambda e: e.dma_start(SM1[:, 0:W2], A["sm2"]).then_inc(s_sm2, 16))
        act.quiet(lambda e: e.dma_start(BD[:, :], A["b_down"]).then_inc(s_sm2, 16))
        ID2 = MODT[:, 0:128]
        act.quiet(lambda e: e.dma_start(ID2, A["ident"]).then_inc(s_sm2, 16))
        t_s2 = (s_sm2, 48)
        T = 256
        XAP = view(BIG, 0, 8, 260)
        XA = view(BIG, 2080, 8, 256)
        R = view(BIG, 4128, 8, 256)
        S_ = view(BIG, 6176, 8, 256)
        I_ = view(BIG, 8224, 8, 256)
        Q2 = view(BIG, 10272, 4, 256)
        K2 = view(BIG, 11296, 4, 256)
        V2 = view(BIG, 12320, 2, 1024)
        LG = view(BIG, 14368, 4, 256)
        GLR = view(BIG, 15392, 256)
        ET = HN_[:, 0:2048].rearrange("p (l t) -> p l t", l=8)
        KE = HN_[:, 2048:4096].rearrange("p (l t) -> p l t", l=8)
        QE = CAT_[:, 0:2048].rearrange("p (l t) -> p l t", l=8)
        YB = CAT_[:, 2048:4096].rearrange("p (k t) -> p k t", k=8)
        ACC = view(BIG, 0, 8, 256)
        H = XS[:, :, 0:256]
        SIDE = XS[:, :, 256:512]
        hsrc = x_toks

        def lin2(name, c, emit, T=256, src=XS, toks=None):
            s, tk = load_chunk(A[name][c])
            w = ring(s).rearrange("p (k n) -> p k n", k=8)
            linear(w, [0, 128, 256, 384], src, T, hsrc if toks is None else toks, tk, emit, True)

        tz = dve.do(lambda e: e.memset(XAP[:, :, 0:3], 0.0), t_big_free)
        txa = [None] * 8
        cw, cb = s2("conv_w", 8, 4), s2("conv_b")
        for c in range(2):
            def e_xa(n, ps, tok, c=c):
                k = 4 * c + n
                t = act.do(lambda e: e.activation(XAP[:, k, 3:259], ps, ACT.Copy), tok, t_big_free)
                a = dve.do(lambda e: e.tensor_scalar(XA[:, k, :], XAP[:, k, 0:256], cw[:, k, 0:1], cb[:, k:k + 1],
                                                    ALU.mult, ALU.add), t, tz, t_s2)
                for i in range(1, 4):
                    a = dve.do(lambda e, i=i: e.scalar_tensor_tensor(XA[:, k, :], XAP[:, k, i:i + 256], cw[:, k, i:i + 1],
                                                                    XA[:, k, :], ALU.mult, ALU.add), a)
                txa[k] = a
                return t
            lin2("w_in_2", c, e_xa)
        tq2, tk2, tv2 = [None] * 4, [None] * 4, []
        ya_t, tlg, yb_t, tya, tgo = [], [], [None] * 8, [None] * 8, [None] * 8
        YA = S_

        def lin2g(name, c, emit):
            s, tk = load_chunk(A[name][c])
            w = ring(s).rearrange("p (k n) -> p k n", k=8)
            yield from linears(w, [0, 128, 256, 384], XS, 256, hsrc, tk, emit, True)

        def qkv():

            def e_q2(n, ps, tok):
                tq2[n] = act.do(lambda e: e.activation(Q2[:, n, :], ps, ACT.Copy, scale=128.0 ** -0.5), tok)
                return tq2[n]
            yield from lin2g("w_in_2", 4, e_q2)

            def e_k2(n, ps, tok):
                tk2[n] = act.do(lambda e: e.activation(K2[:, n, :], ps, ACT.Copy), tok)
                return tk2[n]
            yield from lin2g("w_in_2", 5, e_k2)
            for c in range(2):
                s, tk = load_chunk(A["w_in_2"][6 + c])
                w = ring(s).rearrange("p (k n) -> p k n", k=8)
                for tt in range(2):
                    b = take()
                    tok = mm(banks[b][:, :], [(XS[:, k, tt * 128:tt * 128 + 128], w[:, k, :]) for k in range(8)],
                             tk, fr(b), last=Last(tk) if tt == 1 else None)
                    t = copy_to(V2[:, tt, c * 512:c * 512 + 512], banks[b][:, :], tok)
                    free[b] = t
                    tv2.append(t)
                    yield 7

        def lru():
            wr_, wi_ = s2("lru_w_r", 8, 128), s2("lru_w_i", 8, 128)
            br_, bi_ = s2("lru_b_r"), s2("lru_b_i")
            tr_, ti_ = [], []
            for k in range(8):
                b = take()
                tok = mm(banks[b][:, 0:256], [(wr_[:, k, :], XA[:, k, :])], txa[k], fr(b), t_s2)
                t = act.do(lambda e, k=k, b=b: e.activation(R[:, k, :], banks[b][:, 0:256], ACT.Sigmoid, bias=br_[:, k:k + 1]), tok, t_s2)
                free[b] = t
                tr_.append(t)
                b = take()
                tok = mm(banks[b][:, 0:256], [(wi_[:, k, :], XA[:, k, :])], fr(b))
                t = act.do(lambda e, k=k, b=b: e.activation(I_[:, k, :], banks[b][:, 0:256], ACT.Sigmoid, bias=bi_[:, k:k + 1]), tok)
                free[b] = t
                ti_.append(t)
                yield 1
            lam = s2("lam")
            c0, c1, c2, c3, c4 = (SV[:, 64 + 8 * i:72 + 8 * i] for i in range(5))
            t = act.do(lambda e: e.activation(c0, lam, ACT.Abs), t_s2)
            t = act.do(lambda e: e.activation(c0, c0, ACT.Exp, scale=-1.0), t)
            t = dve.do(lambda e: e.tensor_scalar(c1, c0, 2.0, None, ALU.add), t)
            t = dve.do(lambda e: e.reciprocal(c1, c1), t)
            t = dve.do(lambda e: e.tensor_tensor(c1, c1, c0, ALU.mult), t)
            t = dve.do(lambda e: e.tensor_tensor(c2, c1, c1, ALU.mult), t)
            t = dve.do(lambda e: e.tensor_scalar(c3, c2, 1.0 / 17, 1.0 / 15, ALU.mult, ALU.add), t)
            for i in (13, 11, 9, 7, 5, 3, 1):
                t = dve.do(lambda e: e.tensor_tensor(c3, c3, c2, ALU.mult), t)
                t = dve.do(lambda e, i=i: e.tensor_scalar(c3, c3, 1.0 / i, None, ALU.add), t)
            t = dve.do(lambda e: e.scalar_tensor_tensor(c3, c3, 2.0, c1, ALU.mult, ALU.mult), t)
            t = dve.do(lambda e: e.tensor_scalar(c4, lam, -1.0, 0.0, ALU.mult, ALU.max), t)
            t = dve.do(lambda e: e.tensor_tensor(c3, c3, c4, ALU.add), t)
            t = dve.do(lambda e: e.tensor_scalar(c4, c3, 8.0, None, ALU.mult), t)
            t_cl = dve.do(lambda e: e.tensor_scalar(c3, c3, -8.0, None, ALU.mult), t)
            ts_ = []
            for k in range(8):
                ts_.append(act.do(lambda e, k=k: e.activation(S_[:, k, :], R[:, k, :], ACT.Tanh, scale=c4[:, k:k + 1]), t_cl, tr_[k]))
            ta_ = []
            for k in range(8):
                ta_.append(act.do(lambda e, k=k: e.activation(R[:, k, :], R[:, k, :], ACT.Exp, scale=c3[:, k:k + 1]), ts_[k]))
            yield 4
            tsq = []
            for k in range(8):
                t = dve.do(lambda e, k=k: e.tensor_scalar(XAP[:, k, 0:256], S_[:, k, :], 1.0, None, ALU.add), ts_[k], txa[k])
                t = dve.do(lambda e, k=k: e.reciprocal(XAP[:, k, 0:256], XAP[:, k, 0:256]), t)
                t = dve.do(lambda e, k=k: e.scalar_tensor_tensor(S_[:, k, :], S_[:, k, :], 2.0, XAP[:, k, 0:256], ALU.mult, ALU.mult), t)
                tsq.append(act.do(lambda e, k=k: e.activation(S_[:, k, :], S_[:, k, :], ACT.Sqrt), t))
            for k in range(8):
                t = dve.do(lambda e, k=k: e.tensor_tensor(I_[:, k, :], I_[:, k, :], XA[:, k, :], ALU.mult), ti_[k])
                t = dve.do(lambda e, k=k: e.tensor_tensor(I_[:, k, :], I_[:, k, :], S_[:, k, :], ALU.mult), t, tsq[k])
                ya_t.append(dve.do(lambda e, k=k: e.tensor_tensor_scan(S_[:, k, :], R[:, k, :], I_[:, k, :], 0.0, ALU.mult, ALU.add), t, ta_[k]))

        def log_gates():
            wgl = s2("w_glr", 8, 16)
            b = take()
            tok = mm(banks[b][0:16, 0:256], [(wgl[:, k, :], XS[:, k, 0:256]) for k in range(8)], fr(b), t_s2)
            t = copy_to(GLR[0:16, :], banks[b][0:16, 0:256], tok)
            free[b] = t
            wg = s2("w_gate", 4, 128)
            gb_ = s2("gla_b")
            yield 2
            G4 = ET.rearrange("p l t -> p (l t)")[:, 0:1024].rearrange("p (h t) -> p h t", h=4)
            A4 = ET.rearrange("p l t -> p (l t)")[:, 1024:2048].rearrange("p (h t) -> p h t", h=4)
            tab, tz_ = [], []
            tgl = t
            for h in range(4):
                b = take()
                tok = mm(banks[b][:, 0:256], [(wg[0:16, h, :], GLR[0:16, :])], tgl, fr(b))
                tz_.append(dve.do(lambda e, h=h, b=b: e.tensor_scalar(G4[:, h, :], banks[b][:, 0:256], gb_[:, h:h + 1], None, ALU.add), tok))
                free[b] = tz_[-1]
            yield 1
            t = act.do(lambda e: e.activation(A4, G4, ACT.Abs), *tz_)
            t = act.do(lambda e: e.activation(A4, A4, ACT.Exp, scale=-1.0), t)
            t = act.do(lambda e: e.activation(A4, A4, ACT.Ln, bias=1.0), t)
            t = dve.do(lambda e: e.scalar_tensor_tensor(G4, G4, 0.0, A4, ALU.min, ALU.subtract), t)
            t = dve.do(lambda e: e.tensor_scalar(G4, G4, 1.0 / 16, None, ALU.mult), t)
            for h in range(4):
                tlg.append(dve.do(lambda e, h=h: e.tensor_tensor_scan(LG[:, h, :], onet, G4[:, h, :], 0.0, ALU.mult, ALU.add), t))

        GA = SIDE

        def gate(c0_, fn, put):
            for c in range(2):
                def em(n, ps, tok, c=c):
                    return put(4 * c + n, ps, tok)
                yield from lin2g("w_in_2", c0_ + c, em)


        def put_ga(k, ps, tok):
            a = act.do(lambda e: e.activation(GA[:, k, :], ps, ACT.Gelu_apprx_tanh), tok)
            tya[k] = dve.do(lambda e: e.tensor_tensor(YA[:, k, :], YA[:, k, :], GA[:, k, :], ALU.mult), a, ya_t[k])
            return a

        def put_ma(k, ps, tok):
            a = act.do(lambda e: e.activation(XAP[:, k, 0:256], ps, ACT.Sigmoid), tok, ya_t[k])
            tya[k] = dve.do(lambda e: e.tensor_tensor(YA[:, k, :], YA[:, k, :], XAP[:, k, 0:256], ALU.mult), a, tya[k])
            return a
        GB = GA

        def put_go(k, ps, tok):
            tgo[k] = act.do(lambda e: e.activation(GB[:, k, :], ps, ACT.Silu), tok, tya[k])
            return tgo[k]

        def put_mb(k, ps, tok):
            a = act.do(lambda e: e.activation(XAP[:, k, 0:256], ps, ACT.Sigmoid), tok, tya[k])
            tgo[k] = dve.do(lambda e: e.tensor_tensor(GB[:, k, :], GB[:, k, :], XAP[:, k, 0:256], ALU.mult), a, tgo[k])
            return a


        def gla():
            lev = s2("lev", 8, 128)
            gg = s2("gla_g")
            STT = XA.rearrange("p k t -> p (k t)")
            SMK = R.rearrange("p k t -> p (k t)")
            ST = STT[:, 0:384]
            SQO = STT[:, 512:1024].rearrange("p (a t) -> p a t", a=2)
            OC = STT[:, 1024:1536].rearrange("p (a t) -> p a t", a=2)
            t_ke = t_et = None
            t_smr = None
            t_st = None
            def decays(h):
                dts = []
                for l in range(8):
                    Bq = 1 << l
                    nb = 256 // (2 * Bq)
                    bv = LG[:, h, :].rearrange("p (n b) -> p n b", b=2 * Bq)
                    ref = bv[:, :, Bq - 1:Bq].broadcast_to([128, nb, 2 * Bq])
                    dv = ET[:, l, :].rearrange("p (n b) -> p n b", b=2 * Bq)
                    dts.append(dve.do(lambda e, dv=dv, bv=bv, ref=ref: e.tensor_tensor(dv, bv, ref, ALU.subtract), tlg, t_et))
                t = act.do(lambda e: e.activation(ET, ET, ACT.Abs), dts[-1])
                return act.do(lambda e: e.activation(ET, ET, ACT.Exp, scale=-1.0), t)

            t_dec = decays(0)
            yield 6
            for h in range(4):
                t = t_dec
                qb_ = Q2[:, h:h + 1, :].broadcast_to([128, 8, 256])
                kb_ = K2[:, h:h + 1, :].broadcast_to([128, 8, 256])
                tqe = dve.do(lambda e, qb_=qb_: e.tensor_tensor(QE, ET, qb_, ALU.mult), t, tq2[h], t_ke)
                tke = dve.do(lambda e, kb_=kb_: e.tensor_tensor(KE, ET, kb_, ALU.mult), t, tk2[h], t_ke)
                t_et = tke
                yield 8
                for tt in range(2):
                    sl = slice(tt * 128, tt * 128 + 128)
                    if tt:
                        yield 5
                    bs = [take(), take()]
                    toks = []
                    for l in range(8):
                        lh, rh = (KE[:, l, sl], QE[:, l, sl]) if l < 7 else (K2[:, h, sl], Q2[:, h, sl])
                        toks.append(mm(banks[bs[l // 4]][:, (l % 4) * 128:(l % 4) * 128 + 128], [(lh, rh)], tqe, tke, fr(bs[l // 4])))
                    for i in range(2):
                        t = dve.do(lambda e, i=i, bs=bs: e.tensor_tensor(SMK[:, 512 * i:512 * i + 512], banks[bs[i]][:, :],
                                                                 lev[:, 4 * i:4 * i + 4, :].rearrange("p a b -> p (a b)"), ALU.mult), toks[4 * i + 3], t_smr)
                        free[bs[i]] = t
                    t_smr = t = dve.do(lambda e, tt=tt: e.tensor_reduce(ST[:, tt * 128:tt * 128 + 128],
                                                        SMK[:, 0:1024].rearrange("p (l i) -> p i l", l=8), AX.X, ALU.add), t, t_st)
                    if tt == 0:
                        ts0 = t
                yield 5
                b = take()
                tok = mm(banks[b][:, 0:128], [(KE[:, 7, 0:128], QE[:, 7, 128:256])], fr(b))
                t_ke = tok
                ts2 = dve.do(lambda e, b=b: e.tensor_copy(ST[:, 256:384], banks[b][:, 0:128]), tok)
                free[b] = ts2
                if h < 3:
                    t_dec = decays(h + 1)
                yield 3
                b = take()
                for vt in range(2):
                    cs = slice(h * 256 + vt * 128, h * 256 + vt * 128 + 128)
                    mm(banks[b][:, vt * 256:vt * 256 + 128], [(V2[:, 0, cs], ST[:, 0:128])], ts2, t_smr, fr(b), tv2)
                    tok = mm(banks[b][:, vt * 256 + 128:vt * 256 + 256],
                             [(V2[:, 0, cs], ST[:, 256:384]), (V2[:, 1, cs], ST[:, 128:256])])
                t_st = tok
                ov = banks[b][:, :].rearrange("p (a t) -> p a t", a=2)
                tc = act.do(lambda e, ov=ov: e.activation(OC, ov, ACT.Copy), tok, yb_t[2 * h - 1] if h else None)
                free[b] = tc
                bq, tk_ = yield from meansq(OC, SQO, range(2), 256, o256, [tc, tc])
                r, tr = yield from rstd(bq, 256, 0, tk_, 1e-5)
                for vt in range(2):
                    k = 2 * h + vt
                    t = dve.do(lambda e, vt=vt, k=k, r=r: e.scalar_tensor_tensor(YB[:, k, :], OC[:, vt, :], gg[:, vt:vt + 1], r, ALU.mult, ALU.mult), tr)
                    yb_t[k] = t

        together(chain(log_gates(), qkv()), lru())
        together(chain(gate(2, None, put_ga), gate(10, None, put_ma), gate(8, None, put_go), gate(12, None, put_mb)), gla())
        for k in range(8):
            yb_t[k] = dve.do(lambda e, k=k: e.tensor_tensor(YB[:, k, :], YB[:, k, :], GB[:, k, :], ALU.mult), yb_t[k], tgo[k])
        pT = s2("p", 2, 256)
        wp = s2("w_ple", 2, 1024)
        PW = own(HN, 1)
        for k in range(8):
            b = take()
            tok = mm(banks[b][:, 0:256], [(wp[:, i, k * 128:k * 128 + 128], pT[:, i, :]) for i in range(2)], fr(b))
            free[b] = act.do(lambda e, k=k, b=b: e.activation(PW[:, k, :], banks[b][:, 0:256], ACT.Copy), tok, (pe.sem, pe.n), (dve.sem, dve.n))
        ym_t = []
        for k in range(8):
            ym_t.append(dve.do(lambda e, k=k: e.tensor_tensor(YB[:, k, :], YB[:, k, :], YA[:, k, :], ALU.add), yb_t[k], tya[k]))

        AL = 2.0 ** 0.25
        H1 = HN[:, :, 0:256]
        H1f = HN

        def layernorm(Z, zt, dst, g_, b_, sq, extra):
            b = take()
            for k in range(8):
                tok = mm(banks[b][:, 0:256], [(ones, Z[:, k, 0:256])], zt[k], fr(b), start=k == 0, stop=k == 7)
            t = dve.do(lambda e, b=b: e.tensor_copy(HOLD[:, 0:256], banks[b][:, 0:256]), tok)
            free[b] = t
            zc = []
            for k in range(8):
                zc.append(dve.do(lambda e, k=k: e.tensor_tensor(Z[:, k, 0:256], Z[:, k, 0:256], HOLD[:, 0:256], ALU.subtract), t))
            b, tk_ = yield from meansq(Z, sq, range(8), 256, ones, zc, extra)
            r, tr = yield from rstd(b, 256, 0, tk_, 1e-5)
            o = []
            for k in range(8):
                a = dve.do(lambda e, k=k: e.scalar_tensor_tensor(Z[:, k, 0:256], Z[:, k, 0:256], s2(g_)[:, k:k + 1], r, ALU.mult, ALU.mult), tr)
                o.append(act.do(lambda e, k=k: e.activation(dst[:, k, 0:256], Z[:, k, 0:256], ACT.Identity, bias=s2(b_)[:, k:k + 1]), a, extra))
            return o

        ztk = []
        for c in range(2):
            def e_z(n, ps, tok, c=c):
                k = 4 * c + n
                t = dve.do(lambda e: e.scalar_tensor_tensor(XS[:, k, 0:256], XS[:, k, 0:256], AL, ps, ALU.mult, ALU.add), tok)
                ztk.append(t)
                return t
            lin2("w_out_2", c, e_z, src=YB, toks=ym_t)
        h1 = finish(layernorm(XS, ztk, HN, "ln1_g", "ln1_b", SIDE, None))

        b = take()
        wro = s2("w_router", 8, 32)
        for tt in range(2):
            tok = mm(banks[b][:, tt * 32:tt * 32 + 32], [(HN[:, k, tt * 128:tt * 128 + 128], wro[:, k, :]) for k in range(8)], h1, fr(b))
        LGT = SV[:, 0:64].rearrange("p (a e) -> p a e", a=2)
        MSK = SV[:, 128:192].rearrange("p (a e) -> p a e", a=2)
        TM = SV[:, 192:256].rearrange("p (a e) -> p a e", a=2)
        GTE = SV[:, 256:320].rearrange("p (a e) -> p a e", a=2)
        EQ = SV[:, 320:384].rearrange("p (a e) -> p a e", a=2)
        M8 = SV[:, 384:400].rearrange("p (a e) -> p a e", a=2)
        c4b = SV[:, 400:408].rearrange("p (a e) -> p a e", a=2)
        brt = s2("b_router").rearrange("p (o e) -> p o e", o=1).broadcast_to([128, 2, 32])
        psl = banks[b][:, 0:64].rearrange("p (a e) -> p a e", a=2)
        t0 = dve.do(lambda e: e.tensor_tensor(LGT, psl, brt, ALU.add), tok)
        free[b] = t0
        GT = SV
        gtk = []
        for tt in range(2):
            t = dve.do(lambda e, tt=tt: e.max(M8[:, tt, :], LGT[:, tt, :]), t0)
            v4, v1 = M8[:, tt, 3:4], M8[:, tt, 0:1]
            ta = dve.do(lambda e, tt=tt, v4=v4: e.tensor_scalar(MSK[:, tt, :], LGT[:, tt, :], v4, None, ALU.is_gt), t)
            tb = dve.do(lambda e, tt=tt, v4=v4: e.tensor_scalar(EQ[:, tt, :], LGT[:, tt, :], v4, None, ALU.is_equal), t)
            tn = dve.do(lambda e, tt=tt: e.tensor_reduce(c4b[:, tt, 0:1], MSK[:, tt, :], AX.X, ALU.add), ta)
            tn = dve.do(lambda e, tt=tt: e.tensor_scalar(c4b[:, tt, 1:2], c4b[:, tt, 0:1], -1.0, 4.0, ALU.mult, ALU.add), tn)
            tc = dve.do(lambda e, tt=tt: e.tensor_tensor_scan(TM[:, tt, :], onet[:, 0:32], EQ[:, tt, :], 0.0, ALU.mult, ALU.add), tb)
            t = dve.do(lambda e, tt=tt: e.scalar_tensor_tensor(EQ[:, tt, :], TM[:, tt, :], c4b[:, tt, 1:2], EQ[:, tt, :], ALU.is_le, ALU.mult), tc, tn)
            t = dve.do(lambda e, tt=tt: e.tensor_tensor(MSK[:, tt, :], MSK[:, tt, :], EQ[:, tt, :], ALU.add), t)
            tn = dve.do(lambda e, tt=tt, v1=v1: e.tensor_scalar(c4b[:, tt, 2:3], v1, -1.0, None, ALU.mult), t)
            te = act.do(lambda e, tt=tt: e.activation(TM[:, tt, :], LGT[:, tt, :], ACT.Exp, bias=c4b[:, tt, 2:3]), tn)
            t = dve.do(lambda e, tt=tt: e.tensor_tensor(GTE[:, tt, :], TM[:, tt, :], MSK[:, tt, :], ALU.mult), te)
            t = dve.do(lambda e, tt=tt: e.tensor_reduce(c4b[:, tt, 3:4], GTE[:, tt, :], AX.X, ALU.add), t)
            t = dve.do(lambda e, tt=tt: e.reciprocal(c4b[:, tt, 3:4], c4b[:, tt, 3:4]), t)
            gtk.append(dve.do(lambda e, tt=tt: e.tensor_scalar(GTE[:, tt, :], GTE[:, tt, :], c4b[:, tt, 3:4], None, ALU.mult), t))
        b = take()
        for tt in range(2):
            pe.wait(gtk[tt], fr(b))
            tok = pe.do(lambda e, tt=tt, b=b: e.transpose(banks[b][0:32, tt * 128:tt * 128 + 128], GTE[:, tt, :], ID2[:, :]))
        GTT = STAT[0:32, 1024:1280]
        t_gt = copy_to(GTT, banks[b][0:32, 0:256], tok)
        free[b] = t_gt

        acc_b = [0, 1, 2, 3]
        pe.wait(*[fr(i) for i in range(4)])
        pool[:] = [4, 5, 6, 7]
        turn[0] = 0
        ACTT = CAT_[:, 0:2048].rearrange("p (k t) -> p k t", k=8)
        GBC = CAT_[:, 2048:2560].rearrange("p (a t) -> p a t", a=2)
        GH = CAT_[:, 2560:3072].rearrange("p (a t) -> p a t", a=2)
        SG = CAT_[:, 3072:3584].rearrange("p (a t) -> p a t", a=2)
        UH = CAT_[:, 3584:4096].rearrange("p (a t) -> p a t", a=2)
        bup = s2("b_up", 32, 16)
        t = dve.do(lambda e: e.memset(view(BIG, 12288, 2048), 0.0), (act.sem, act.n), (pe.sem, pe.n), (rel.sem, rel.n))
        sp.wait((act.sem, act.n), (dve.sem, dve.n), (pe.sem, pe.n), (rel.sem, rel.n))
        sp.quiet(lambda e: e.dma_start(BIG[0:32, 12288:14336], A["b_up_rows"]).then_inc(s_sm3, 16))
        sp.quiet(lambda e: e.dma_start(HOLD[:, 256:512], A["iota"]).then_inc(s_sm3, 16))
        sp.quiet(lambda e: e.dma_start(HOLD[:, 768:896], A["tri"]).then_inc(s_sm3, 16))
        t_bupr = [t, (s_sm3, 48)]
        IOTA, IOTA2, TRI, ONE1 = HOLD[:, 256:384], HOLD[:, 384:512], HOLD[:, 768:896], onet[:, 0:128]
        for q in (pe, dve):
            q.wait(t_bupr)
        t_bigdone = [(act.sem, act.n), (dve.sem, dve.n), (pe.sem, pe.n), (rel.sem, rel.n)]
        def accap(d):
            return banks[acc_b[d // 2]][:, (d % 2) * 256:(d % 2) * 256 + 256]

        for d in range(8):
            mm(accap(d), [(BD[0:32, d * 128:d * 128 + 128], GTT)], t_gt, t_s2, start=d % 2 == 0, stop=False, check=False)
        rel0 = rel.n
        load = []
        for ex in range(NEXP):
            srcs = [A["w_up"][ex, c] for c in range(4)] + [A["w_down"][ex, c] for c in range(2)]
            load.append([load_chunk(src, True, t_bigdone, rel0 + 6 * ex + i + 1) for i, src in enumerate(srcs)])

        def dense():
            gbc_free = None
            a_read = None
            par = 0
            gh_free = [None, None]
            for ex in range(NEXP):
                b = take()
                selw = ID2[0:32, ex:ex + 1].broadcast_to([32, 128])
                tok = mm(banks[b][:, 0:256], [(selw, GTT)], fr(b), t_s2)
                tgb = copy_to(GBC[:, ex % 2, :], banks[b][:, 0:256], tok, gbc_free)
                free[b] = tgb
                at = []
                for c in range(4):
                    s, tk = load[ex][c]
                    w = ring(s).rearrange("p (k n) -> p k n", k=8)
                    for j in range(2):
                        f = 2 * c + j
                        bg = take()
                        tg_ = mm(banks[bg][:, 0:256], [(w[:, k, j * 256:j * 256 + 128], HN[:, k, 0:256]) for k in range(8)], tk, fr(bg))
                        bu = take()
                        tu_ = mm(banks[bu][:, 0:256], [(w[:, k, j * 256 + 128:j * 256 + 256], HN[:, k, 0:256]) for k in range(8)],
                                 fr(bu), last=rel if j == 1 else None)
                        q = par = par ^ 1
                        t1 = dve.do(lambda e, bg=bg, q=q, ex=ex, f=f: e.tensor_scalar(GH[:, q, :], banks[bg][:, 0:256], bup[:, ex, f:f + 1], 7.0, ALU.add, ALU.min), tg_)
                        free[bg] = t1
                        t2 = act.do(lambda e, q=q: e.activation(SG[:, q, :], GH[:, q, :], ACT.Sigmoid, scale=1.702), t1, gh_free[q])
                        t3 = dve.do(lambda e, bu=bu, q=q, ex=ex, f=f: e.tensor_scalar(UH[:, q, :], banks[bu][:, 0:256], bup[:, ex, 8 + f:9 + f], 7.0, ALU.add, ALU.min), tu_)
                        free[bu] = t3
                        t3 = dve.do(lambda e, q=q: e.tensor_scalar(UH[:, q, :], UH[:, q, :], -7.0, 1.0, ALU.max, ALU.add), t3)
                        t3 = dve.do(lambda e, q=q: e.tensor_tensor(UH[:, q, :], UH[:, q, :], GH[:, q, :], ALU.mult), t3)
                        t4 = dve.do(lambda e, q=q, ex=ex: e.tensor_tensor(SG[:, q, :], SG[:, q, :], GBC[:, ex % 2, :], ALU.mult), t2, tgb)
                        t5 = dve.do(lambda e, q=q, f=f: e.tensor_tensor(ACTT[:, f, :], UH[:, q, :], SG[:, q, :], ALU.mult), t3, t4, a_read)
                        gh_free[q] = t5
                        at.append(t5)
                gbc_free = at[-1]
                for c in range(2):
                    s, tk = load[ex][4 + c]
                    w = ring(s).rearrange("p (k n) -> p k n", k=8)
                    for j in range(4):
                        d = 4 * c + j
                        mm(accap(d), [(w[:, k, j * 128:j * 128 + 128], ACTT[:, k, :]) for k in range(8)], tk, at,
                           start=False, stop=ex == NEXP - 1, check=False, last=rel if j == 3 else None)
                a_read = (rel.sem, rel.n)

        HTM = XS_[:, 0:2048].rearrange("p (a d) -> p a d", a=2)
        XG = [XS_[:, 2048 + 1024 * i:3072 + 1024 * i].rearrange("p (k s) -> p k s", k=8) for i in range(2)]
        AV = CAT_[:, 0:1024]
        AVT = CAT_[:, 1024:2048]
        YV = CAT_[:, 2048:3072]
        SEL = CAT_[:, 3072:3328].rearrange("p (a s) -> p a s", a=2)
        SELG = CAT_[:, 3328:3584].rearrange("p (a s) -> p a s", a=2)
        SCZ = CAT_[:, 3584:4096].rearrange("p (h t) -> p h t", h=2)
        SCF = view(BIG, 15872, 256)
        G1_, S1_, U1_ = (view(BIG, 14336 + 512 * i, 2, 256) for i in range(3))
        BUPR = view(BIG, 12288, 2048)
        LENS = NEXP

        def select(ex, free_s):
            t = free_s
            for tt in range(2):
                t = dve.do(lambda e, tt=tt: e.tensor_scalar(SEL[:, tt, :], IOTA, POS[:, tt, ex:ex + 1], MSK[:, tt, ex:ex + 1],
                                                           ALU.is_equal, ALU.mult), t)
            return t

        def gather(ex, ts, x_free):
            X = XG[ex % 2]
            out_ = []
            for half in range(2):
                b = take()
                for kk in range(4):
                    k = 4 * half + kk
                    tok = mm(banks[b][:, kk * 128:kk * 128 + 128],
                             [(HTM[:, tt, k * 128:k * 128 + 128], SEL[:, tt, :]) for tt in range(2)], ts, fr(b), t_htm)
                t = act.do(lambda e, X=X, half=half, b=b: e.activation(
                    X[:, 4 * half:4 * half + 4, :].rearrange("p k s -> p (k s)"), banks[b][:, :], ACT.Copy), tok, x_free)
                free[b] = t
                out_.append(t)
            return out_, tok

        def expert(ex, wide, st):
            xg_t, sel_read, scat_read = st["xg"], st["sel_read"], st["scat"]
            X = XG[ex % 2]
            C = 128 if wide else 64
            t = sel_read
            iot = IOTA if wide else IOTA2
            for tt in range(2):
                t = dve.do(lambda e, tt=tt: e.tensor_scalar(SELG[:, tt, :], iot, POS[:, tt, ex:ex + 1], GTE[:, tt, ex:ex + 1],
                                                           ALU.is_equal, ALU.mult), t)
            t_selg = t
            ts_next = select(ex + 1, sel_read) if ex + 1 < NEXP else None
            av = []
            for c in range(4):
                s, tk = load[ex][c]
                w = ring(s).rearrange("p (k n) -> p k n", k=8)
                b = take()
                pe.wait(tk, fr(b), xg_t, t_bupr)
                onehot = ID2[:, ex:ex + 1].broadcast_to([128, C])
                for k in range(9):
                    for h in range(1 if wide else 2):
                        lh = X[:, k, 0:C] if k < 8 else onehot
                        if wide:
                            o_ = banks[b][:, :]
                            rh = w[:, k, :] if k < 8 else BUPR[:, c * 512:c * 512 + 512]
                        else:
                            o_ = banks[b][64 * h:64 * h + 64, 0:256]
                            rh = w[:, k, h * 256:h * 256 + 256] if k < 8 else BUPR[:, c * 512 + h * 256:c * 512 + h * 256 + 256]
                        f = lambda e, o_=o_, lh=lh, rh=rh, k=k: e.matmul(o_, lh, rh, start=k == 0, stop=k == 8)
                        if k == 8 and h == (0 if wide else 1):
                            rel.n += 1
                            pe.quiet(lambda e, f=f: f(e).then_inc(rel.sem, 1))
                        else:
                            pe.quiet(f)
                tok = (rel.sem, rel.n)
                H_ = 2 if wide else 1
                ps = banks[b][:, 0:256 * H_].rearrange("p (h g n) -> p h g n", h=H_, g=2)
                q = c % 2
                gh, sg, uh = (x_[:, q, 0:128 * H_].rearrange("p (h n) -> p h n", h=H_) for x_ in (G1_, S1_, U1_))
                AVc = AV.rearrange("p (c n) -> p c n", c=4)[:, c, 0:128 * H_].rearrange("p (h n) -> p h n", h=H_)
                t1 = dve.do(lambda e, gh=gh, ps=ps: e.tensor_scalar(gh, ps[:, :, 0, :], 7.0, None, ALU.min), tok)
                t2 = act.do(lambda e, gh=gh, sg=sg: e.activation(sg, gh, ACT.Sigmoid, scale=1.702), t1)
                t3 = dve.do(lambda e, uh=uh, ps=ps: e.tensor_scalar(uh, ps[:, :, 1, :], 7.0, -7.0, ALU.min, ALU.max), tok)
                free[b] = t3
                t3 = dve.do(lambda e, uh=uh, gh=gh: e.scalar_tensor_tensor(uh, uh, 1.0, gh, ALU.add, ALU.mult), t3)
                av.append(dve.do(lambda e, uh=uh, sg=sg, AVc=AVc: e.tensor_tensor(AVc, uh, sg, ALU.mult), t3, t2, st["avt"]))
            b = take()
            pe.wait(t_selg, fr(b))
            for tt in range(2):
                f = lambda e, tt=tt, b=b: e.transpose(banks[b][:, tt * 128:tt * 128 + 128], SELG[:, tt, :], ID2)
                tok = pe.do(f) if tt else pe.quiet(f)
            for h in range(2):
                pr = slice(64 * h, 64 * h + 64)
                dst = SCF[pr, :] if wide else SCZ[pr, h, :]
                t_sc = dve.do(lambda e, b=b, pr=pr, dst=dst: e.tensor_copy(dst, banks[b][pr, 0:256]), tok, scat_read)
            free[b] = t_sc
            if ex + 1 < NEXP:
                st["xg"], _ = gather(ex + 1, ts_next, st["x_read"])
            st["sel_read"] = (pe.sem, pe.n)
            st["x_read"] = (rel.sem, rel.n)
            at = []
            for half in range(2):
                b = take()
                pe.wait(av[2 * half + 1], fr(b))
                W_ = 512 if wide else 256
                for i in range(W_ // 128):
                    c, hh = (2 * half + i // 2, i % 2) if wide else (2 * half + i, 0)
                    src = AV[:, c * 256 + hh * 128:c * 256 + hh * 128 + 128]
                    f = lambda e, b=b, i=i, src=src: e.transpose(banks[b][:, i * 128:i * 128 + 128], src, ID2)
                    tok = pe.do(f) if i == W_ // 128 - 1 else pe.quiet(f)
                dst = AVT[:, half * W_:half * W_ + W_]
                t = dve.do(lambda e, b=b, dst=dst: e.tensor_copy(dst, banks[b][:, 0:W_]), tok, st["down"])
                free[b] = t
                at.append(t)
            st["avt"] = tok
            T_ = AVT[:, 0:8 * C].rearrange("p (k s) -> p k s", k=8)
            yt = []
            for c in range(2):
                s, tk = load[ex][4 + c]
                w = ring(s).rearrange("p (k n) -> p k n", k=8)
                b = take()
                pe.wait(tk, fr(b), at)
                for k in range(8):
                    for h in range(1 if wide else 2):
                        if wide:
                            o_, rh = banks[b][:, :], w[:, k, :]
                        else:
                            o_, rh = banks[b][64 * h:64 * h + 64, 0:256], w[:, k, h * 256:h * 256 + 256]
                        f = lambda e, o_=o_, lh=T_[:, k, :], rh=rh, k=k: e.matmul(o_, lh, rh, start=k == 0, stop=k == 7)
                        if k == 7 and h == (0 if wide else 1):
                            rel.n += 1
                            pe.quiet(lambda e, f=f: f(e).then_inc(rel.sem, 1))
                        else:
                            pe.quiet(f)
                W_ = 512 if wide else 256
                t = act.do(lambda e, b=b, c=c: e.activation(YV[:, c * W_:c * W_ + W_], banks[b][:, 0:W_], ACT.Copy),
                           (rel.sem, rel.n), scat_read)
                free[b] = t
                yt.append(t)
            st["down"] = (rel.sem, rel.n)
            for d in range(8):
                c, j = d // 4, d % 4
                if wide:
                    lh, rh = YV[:, d * 128:d * 128 + 128], SCF
                else:
                    lh, rh = YV[:, c * 256 + (j % 2) * 128:c * 256 + (j % 2) * 128 + 128], SCZ[:, j // 2, :]
                tok = mm(accap(d), [(lh, rh)], t_sc, yt[c], start=False, stop=ex == NEXP - 1, check=False)
            st["scat"] = tok

        queues = (pe, act, dve)

        def snap():
            return [(q, q.n, dict(q.seen)) for q in queues], rel.n, list(free), turn[0]

        def restore(sn):
            for q, n, seen in sn[0]:
                q.n, q.seen, q.items = n, dict(seen), []
            rel.n, turn[0] = sn[1], sn[3]
            free[:] = sn[2]

        def fork(reg, zero, other, same):
            before = [q.items for q in queues]
            sn = snap()
            restore(sn)
            zero()
            one, end1 = [q.items for q in queues], snap()
            restore(sn)
            other()
            two, end2 = [q.items for q in queues], snap()
            if same:
                assert [x[1] for x in end1[0]] == [x[1] for x in end2[0]] and end1[1:] == end2[1:]
            for q, b_, i1, i2, e1, e2 in zip(queues, before, one, two, end1[0], end2[0]):
                q.seen = {k: min(v, e2[2].get(k, 0)) for k, v in e1[2].items()}
                q.items = b_ + [(reg, i1, i2)]

        bq_ = take()
        tok = mm(banks[bq_][:, 0:32], [(TRI, MSK[:, 0, :])], gtk, fr(bq_), t_s2)
        tok = mm(banks[bq_][:, 32:64], [(ONE1, MSK[:, 0, :]), (TRI, MSK[:, 1, :])], start=True)
        tok = mm(banks[bq_][:, 64:96], [(ONE1, MSK[:, 0, :]), (ONE1, MSK[:, 1, :])], start=True)
        POS = SV[:, 0:64].rearrange("p (a e) -> p a e", a=2)
        t = dve.do(lambda e: e.tensor_copy(SV[:, 0:64], banks[bq_][:, 0:64]), tok)
        CNT = SV[0:1, 408:440 - 2]
        t = dve.do(lambda e: e.tensor_reduce(SV[0:1, 410:411], banks[bq_][0:1, 64:96], AX.X, ALU.max), t)
        t = dve.do(lambda e: e.tensor_scalar(FLAG[0:1, 32:33], SV[0:1, 410:411], 128.0, None, ALU.is_gt), t)
        t_flag = dve.do(lambda e: e.tensor_scalar(FLAG[0:1, 0:32], banks[bq_][0:1, 64:96], 64.0, None, ALU.is_gt), t)
        free[bq_] = t_flag
        tks = []
        for tt in range(2):
            for half in range(2):
                b = take()
                pe.wait(h1, fr(b))
                for i in range(4):
                    k = 4 * half + i
                    f = lambda e, b=b, i=i, k=k, tt=tt: e.transpose(banks[b][:, i * 128:i * 128 + 128], HN[:, k, tt * 128:tt * 128 + 128], ID2)
                    tok = pe.do(f) if i == 3 else pe.quiet(f)
                t = act.do(lambda e, b=b, half=half, tt=tt: e.activation(HTM[:, tt, 512 * half:512 * half + 512], banks[b][:, :], ACT.Copy), tok)
                free[b] = t
                tks.append(t)
        t_htm = tks
        for q in queues:
            q.wait(t_flag, (pe.sem, pe.n), (act.sem, act.n), (dve.sem, dve.n))

            def ld(e, q=q):
                e.load(q.regs, FLAG[0:1, 0:32])
                return e.load(q.over, FLAG[0:1, 32:33])
            q.quiet(ld)

        def sparse():
            for h in range(2):
                t = dve.do(lambda e, h=h: e.memset(SCZ[64 - 64 * h:128 - 64 * h, h, :], 0.0))
            st = {"xg": None, "sel_read": None, "scat": None, "avt": None, "down": None, "x_read": None}
            ts = select(0, None)
            st["xg"], st["sel_read"] = gather(0, ts, None)
            pe.wait(t)
            for ex in range(NEXP):
                ends = []
                st0 = dict(st)

                def go(wide):
                    s_ = dict(st0)
                    expert(ex, wide, s_)
                    ends.append(s_)
                fork(ex, lambda: go(False), lambda: go(True), True)
                assert ends[0] == ends[1]
                st = ends[0]

        base = {q: (q.sem, q.n) for q in queues}
        after = {q: sem(f"s_{q.name}_z") for q in queues}

        def path(body, tag):
            for q in queues:
                q.sem, q.n = sems[tag][q], 0
            body()
            for q in queues:
                q.wait((q.sem, q.n))
                q.quiet(lambda e: e.sem_inc(s_join, 1))

        sems = {tag: {q: sem(f"s_{q.name}_{tag}") for q in queues} for tag in ("f", "g")}
        s_join = sem("s_join")
        for i in range(8):
            free[i] = None
        fork(None, lambda: path(sparse, "f"), lambda: path(dense, "g"), False)
        rel.n = rel0 + 6 * NEXP
        for q in queues:
            q.sem, q.n = after[q], 0
            q.wait((s_join, 3), (rel.sem, rel.n))
        for i in range(8):
            free[i] = None
        t_acc = (rel.sem, rel.n)

        Z2 = XS
        zt = []
        for k in range(8):
            zt.append(dve.do(lambda e, k=k: e.scalar_tensor_tensor(XS[:, k, 0:256], HN[:, k, 0:256], AL, accap(k), ALU.mult, ALU.add), t_acc))
        for i in range(4):
            free[i] = zt[-1]
        pool[:] = list(range(8))
        h2 = finish(layernorm(XS, zt, HN, "ln2_g", "ln2_b", SIDE, zt[-1]))
        ZO = CAT_[:, 0:2048].rearrange("p (k t) -> p k t", k=8)
        OUTB = XS[:, :, 0:256]
        fin = []
        gates_w = [load_chunk(A["w_ple_gate"][c], True) for c in range(2)]
        for c in range(2):
            s, tk = gates_w[c]
            w = ring(s).rearrange("p (k n) -> p k n", k=8)

            def e_p(n, ps, tok, c=c):
                k = 4 * c + n
                a = act.do(lambda e: e.activation(ZO[:, k, :], ps, ACT.Sigmoid, bias=s2("b_ple")[:, k:k + 1]), tok, t_acc)
                t = dve.do(lambda e: e.tensor_tensor(ZO[:, k, :], ZO[:, k, :], PW[:, k, :], ALU.mult), a)
                fin.append(dve.do(lambda e: e.tensor_tensor(ZO[:, k, :], ZO[:, k, :], HN[:, k, 0:256], ALU.add), t))
                return a
            linear(w, [0, 128, 256, 384], HN, 256, h2, tk, e_p, True)
            sp.wait(fin[-1])
            sp.quiet(lambda e, c=c: e.dma_start(out[:, 4 * c:4 * c + 4, :], ZO[:, 4 * c:4 * c + 4, :]).then_inc(s_out, 16))
        sp.wait((s_out, 32))

        block = ctx.enter_context(nc.Block())

        @block.sync
        def _(e):
            sp.emit(e, sp.items)

        @block.scalar
        def _(e):
            act.run(e)

        @block.vector
        def _(e):
            dve.run(e)

        @block.tensor
        def _(e):
            pe.run(e)


def constants():
    c = {}
    c["ident"] = np.eye(128)
    pos = np.arange(256)
    row, col = (pos // 64).astype(np.float32), (pos % 64).astype(np.float32)
    inv = (np.float32(10000.0) ** (-np.arange(16, dtype=np.float32) / np.float32(16))).astype(np.float32)
    ar, ac = row[:, None] * inv[None], col[:, None] * inv[None]
    ang = np.concatenate([ar, ar, ac, ac], 1).astype(np.float64)
    c["ropec"] = np.tile(np.cos(ang).T, (2, 1))
    c["ropes"] = np.tile(np.sin(ang).T, (2, 1))
    rot = np.zeros((128, 128))
    for b in (0, 64):
        for i in range(16):
            rot[b + 16 + i, b + i] = -1
            rot[b + i, b + 16 + i] = 1
            rot[b + 48 + i, b + 32 + i] = -1
            rot[b + 32 + i, b + 48 + i] = 1
    c["rot"] = rot
    k = np.arange(64)
    a64 = 2 * np.pi * ((k[:, None] * k[None]) % 64) / 64
    z = np.zeros((64, 64))
    cb, sb_ = np.cos(a64) / 128, np.sin(a64) / 128
    c["bd"] = np.concatenate([np.block([[cb, z], [z, cb]]), np.block([[sb_, z], [z, sb_]])], 1)
    t = np.arange(256)
    a = 2 * np.pi * ((t[:, None] * t[None]) % 256) / 256
    c["dftc"] = np.cos(a).reshape(2, 128, 256).transpose(1, 0, 2)
    c["dfts"] = -np.sin(a).reshape(2, 128, 256).transpose(1, 0, 2)
    q = np.arange(256).reshape(2, 128)
    c["band"] = np.where(np.abs(q[:, :, None] - t[None, None]) <= 128, 0.0, -8e30).transpose(1, 0, 2)
    lev = np.zeros((128, 8, 128))
    for j in range(128):
        for i in range(j, 128):
            lev[j, 7 if i == j else int(i ^ j).bit_length() - 1, i] = 1
    c["lev"] = lev
    return c


def pack(table, width, vals):
    sm = np.zeros((128, width), np.float32)
    for n, (o, w) in table.items():
        v = np.asarray(vals[n])
        v = v.reshape(v.shape[0], -1)
        assert v.shape[1] == w, (n, v.shape, w)
        sm[:v.shape[0], o:o + w] = v
    return sm


def col(v):
    return v.reshape(-1, 128).T


def tiles8(w):
    n = w.shape[1] // 512
    return np.ascontiguousarray(w.reshape(8, 128, n, 512).transpose(2, 1, 0, 3)).reshape(n, 128, 4096)


def layout(inp):
    f = {k: np.asarray(v) for k, v in inp.items()}
    con = constants()
    (T1, W1), (T2, W2) = smalls()
    perm = np.concatenate([np.concatenate([np.arange(64 * j, 64 * j + 64), np.arange(64 * (j + 4), 64 * (j + 4) + 64)]) for j in range(4)])
    rows = np.concatenate([perm, np.arange(512, 1024)])
    v = dict(con)
    v["cc"] = np.stack([col(f["c"][0]), col(f["c_ctx"])], -1)
    A = {}
    for l in range(2):
        v[f"b_ada{l}"] = col(f["b_ada"][l])
        for n in ("g_pre_mix", "g_post_mix", "g_pre_ff", "g_post_ff"):
            v[f"{n}{l}"] = col(f[n][l])
        v[f"g_mix{l}"] = col(f["g_mix"][l][rows])
        sk = f["sink"][l].reshape(2, 4).T
        v[f"sink{l}"] = np.broadcast_to(np.repeat(sk, 2, axis=1).reshape(1, 16), (128, 16))
        v[f"b_sgu{l}"] = np.repeat(f["b_sgu"][l].reshape(2, 2, 128).transpose(1, 0, 2), 64, axis=0)
        v[f"g_sgu{l}"] = np.broadcast_to(f["g_sgu"][l].reshape(1, 256), (128, 256))
        v[f"w_sgu{l}"] = f["w_sgu"][l].transpose(2, 0, 1)
        A[f"w_ada{l}"] = tiles8(f["w_ada"][l])
        wi = f["w_in"][l]
        A[f"w_in{l}"] = tiles8(np.concatenate([wi[:, perm], wi[:, 512:]], 1))
        A[f"w_out{l}"] = tiles8(f["w_out"][l][rows])
        A[f"w_ff1_{l}"] = tiles8(f["w_ff1"][l])
        A[f"w_ff2_{l}"] = np.ascontiguousarray(f["w_ff2"][l].reshape(32, 128, 8, 128).transpose(2, 1, 0, 3)).reshape(8, 128, 4096)
    A["sm1"] = pack(T1, W1, v)
    xs = np.concatenate([f["x"][0], f["ctx"][0]], 0)
    A["xs"] = np.ascontiguousarray(xs.T.reshape(8, 128, 512).transpose(1, 0, 2)).reshape(128, 4096)
    A["ident"] = con["ident"].astype(np.float32)
    w2 = f["w_in_2"][0]
    A["w_in_2"] = tiles8(np.concatenate([w2[:, :5120], w2[:, 5136:]], 1))
    u = {"lev": con["lev"]}
    u["conv_w"] = f["conv_w_2"][0].reshape(4, 8, 128).transpose(2, 1, 0)
    for n, s in (("conv_b", "conv_b_2"), ("lru_b_r", "lru_b_r_2"), ("lru_b_i", "lru_b_i_2"), ("lam", "lru_lambda_2"),
                 ("gla_b", "gla_b_gate_2"), ("gla_g", "gla_norm_g_2"), ("ln1_g", "ln1_g_2"), ("ln1_b", "ln1_b_2"),
                 ("ln2_g", "ln2_g_2"), ("ln2_b", "ln2_b_2"), ("b_ple", "b_ple_gate_2")):
        u[n] = col(f[s][0])
    u["b_router"] = np.broadcast_to(f["b_router_2"][0][None], (128, 32))
    u["b_up"] = f["b_up_2"][0].reshape(32, 16, 128).transpose(2, 0, 1)
    u["w_router"] = f["w_router_2"][0].reshape(8, 128, 32).transpose(1, 0, 2)
    u["w_glr"] = w2[:, 5120:5136].reshape(8, 128, 16).transpose(1, 0, 2)
    u["w_gate"] = f["gla_w_gate_2"][0]
    u["lru_w_r"] = f["lru_w_r_2"][0].transpose(1, 0, 2)
    u["lru_w_i"] = f["lru_w_i_2"][0].transpose(1, 0, 2)
    u["p"] = f["p_2"][0, 0].T.reshape(2, 128, 256).transpose(1, 0, 2)
    u["w_ple"] = f["w_ple_2"][0].reshape(2, 128, 1024).transpose(1, 0, 2)
    A["sm2"] = pack(T2, W2, u)
    A["b_down"] = f["b_down_2"][0]
    A["b_up_rows"] = f["b_up_2"][0].reshape(32, 2, 4, 2, 128).transpose(0, 2, 3, 1, 4).reshape(32, 2048)
    i = np.arange(128)
    A["iota"] = np.broadcast_to(np.concatenate([i, i % 64])[None], (128, 256)).astype(np.float32)
    A["tri"] = (i[:, None] < i[None]).astype(np.float32)
    A["w_out_2"] = tiles8(f["w_out_2"][0])
    A["w_ple_gate"] = tiles8(f["w_ple_gate_2"][0])
    up = f["w_up_2"][0].reshape(32, 8, 128, 2, 4, 2, 128).transpose(0, 4, 2, 1, 5, 3, 6)
    A["w_up"] = np.ascontiguousarray(up).reshape(32, 4, 128, 4096)
    dn = f["w_down_2"][0].reshape(32, 8, 128, 2, 512).transpose(0, 3, 2, 1, 4)
    A["w_down"] = np.ascontiguousarray(dn).reshape(32, 2, 128, 4096)
    return A


def kernel(**inputs):
    import concourse.bacc as bacc
    from concourse.bass_utils import run_bass_kernel_spmd as run

    arrays = {k: np.ascontiguousarray(a) for k, a in layout(inputs).items()}
    nc = bacc.Bacc("TRN2", target_bir_lowering=False, num_devices=1)
    A = {n: nc.dram_tensor(f"in_{n}", a.shape, mybir.dt.from_np(a.dtype), kind="ExternalInput").ap() for n, a in arrays.items()}
    out = nc.dram_tensor("out_t", (128, 8, 256), F32, kind="ExternalOutput").ap()
    build(nc, A, out)
    r = run(nc, [{f"in_{n}": a for n, a in arrays.items()}], core_ids=[0])
    o = r.results[0]["out_t"]
    return np.ascontiguousarray(o.transpose(2, 1, 0).reshape(1, 256, 1024))
```
